# Optimizing a Trainium2 kernel written in Bass

```python
import jax, jax.numpy as jnp
from jax import lax
import numpy as np

D_MODEL = 1024
BATCH = 1
SEQ = 512
DEPTH = 2

N_MIXERS = 2
N_LAYERS_A = (DEPTH + 1) // 2
N_LAYERS_B = DEPTH // 2
MLA_HEADS = 8
QK_NOPE = 128
QK_ROPE = 64
V_DIM = 128
Q_LORA = 384
KV_LORA = 256
ROPE_THETA = 10000.0
SWA_HEADS = 16
SWA_KV_HEADS = 4
SWA_HEAD_DIM = 64
WINDOW = 128
D_FF = 4 * D_MODEL
BLOCK_Q = 128
EPS = 1e-6


def rmsnorm(x, g):
    xf = x.astype(jnp.float32)
    y = xf * lax.rsqrt(jnp.mean(xf * xf, axis=-1, keepdims=True) + EPS)
    return (y * g.astype(jnp.float32)).astype(x.dtype)

def modulate(x, g, shift, scale):
    return rmsnorm(x, g) * (1.0 + scale[:, None, :]) + shift[:, None, :]

def rope(x, positions):
    half = QK_ROPE // 2
    inv_freq = ROPE_THETA ** (-jnp.arange(half, dtype=jnp.float32) / half)
    ang = positions.astype(jnp.float32)[..., None] * inv_freq
    shape = ang.shape[:2] + (1,) * (x.ndim - 3) + (half,)
    cos = jnp.cos(ang).reshape(shape)
    sin = jnp.sin(ang).reshape(shape)
    xf = x.astype(jnp.float32)
    x1, x2 = xf[..., :half], xf[..., half:]
    out = jnp.concatenate([x1 * cos - x2 * sin, x1 * sin + x2 * cos], axis=-1)
    return out.astype(x.dtype)

def alibi_slopes(n_heads):
    return jnp.asarray(2.0 ** (-8.0 * np.arange(1, n_heads + 1) / n_heads), dtype=jnp.float32)

def mla(h, positions, w_dq, g_q, w_uq, w_dkv, g_kv, w_ukv, w_o):
    B, S, _ = h.shape
    H = MLA_HEADS
    cq = rmsnorm(h @ w_dq, g_q)
    q = (cq @ w_uq).reshape(B, S, H, QK_NOPE + QK_ROPE)
    q_nope = q[..., :QK_NOPE]
    q_rope = rope(q[..., QK_NOPE:], positions)
    ckv_kr = h @ w_dkv
    ckv = rmsnorm(ckv_kr[..., :KV_LORA], g_kv)
    k_rope = rope(ckv_kr[..., KV_LORA:], positions)
    kv = (ckv @ w_ukv).reshape(B, S, H, QK_NOPE + V_DIM)
    k_nope, v = kv[..., :QK_NOPE], kv[..., QK_NOPE:]
    scale = (QK_NOPE + QK_ROPE) ** -0.5
    n_blk = S // BLOCK_Q
    qn_blk = q_nope.reshape(B, n_blk, BLOCK_Q, H, QK_NOPE).transpose(1, 0, 2, 3, 4)
    qr_blk = q_rope.reshape(B, n_blk, BLOCK_Q, H, QK_ROPE).transpose(1, 0, 2, 3, 4)
    key_idx = jnp.arange(S)

    def one_block(args):
        i, qn, qr = args
        s = (jnp.einsum('bqhd,bkhd->bhqk', qn, k_nope)
             + jnp.einsum('bqhr,bkr->bhqk', qr, k_rope)).astype(jnp.float32) * scale
        q_idx = i * BLOCK_Q + jnp.arange(BLOCK_Q)
        causal = key_idx[None, :] <= q_idx[:, None]
        s = jnp.where(causal[None, None], s, -jnp.inf)
        p = jax.nn.softmax(s, axis=-1).astype(v.dtype)
        return jnp.einsum('bhqk,bkhd->bqhd', p, v)

    o = lax.map(one_block, (jnp.arange(n_blk), qn_blk, qr_blk))
    o = o.transpose(1, 0, 2, 3, 4).reshape(B, S, H * V_DIM)
    return o @ w_o

def swa(h, w_qkv, b_qkv, sinks, w_o, b_o):
    B, S, _ = h.shape
    Hq, Hk, Dh, W = SWA_HEADS, SWA_KV_HEADS, SWA_HEAD_DIM, WINDOW
    G = Hq // Hk
    qkv = h @ w_qkv + b_qkv
    q = qkv[..., :Hq * Dh]
    k = qkv[..., Hq * Dh:(Hq + Hk) * Dh].reshape(B, S, Hk, Dh)
    v = qkv[..., (Hq + Hk) * Dh:].reshape(B, S, Hk, Dh)
    n_blk = S // W
    qb = q.reshape(B, n_blk, W, Hk, G, Dh)

    def band(t):
        tb = t.reshape(B, n_blk, W, Hk, Dh)
        prev = jnp.pad(tb[:, :-1], ((0, 0), (1, 0), (0, 0), (0, 0), (0, 0)))
        return jnp.concatenate([prev, tb], axis=2)

    kb, vb = band(k), band(v)
    s = jnp.einsum('bnqkgd,bnjkd->bnkgqj', qb, kb).astype(jnp.float32) * (Dh ** -0.5)
    dist = W + jnp.arange(W)[:, None] - jnp.arange(2 * W)[None, :]
    in_window = (dist >= 0) & (dist < W)
    real_key = (jnp.arange(n_blk)[:, None] > 0) | (jnp.arange(2 * W)[None, :] >= W)
    mask = in_window[None] & real_key[:, None, :]
    slopes = alibi_slopes(Hq).reshape(Hk, G)
    s = s - slopes[:, :, None, None] * dist.astype(jnp.float32)
    s = jnp.where(mask[None, :, None, None], s, -jnp.inf)
    sink = sinks.astype(jnp.float32).reshape(Hk, G)[:, :, None]
    m = jnp.maximum(s.max(axis=-1), sink)
    p = jnp.exp(s - m[..., None])
    denom = p.sum(axis=-1) + jnp.exp(sink - m)
    p = (p / denom[..., None]).astype(vb.dtype)
    o = jnp.einsum('bnkgqj,bnjkd->bnqkgd', p, vb).reshape(B, S, Hq * Dh)
    return o @ w_o + b_o

def first_inputs(seed: int = 0) -> dict:
    key = jax.random.key(seed)
    ks = jax.random.split(key, 24)
    f32 = jnp.float32

    def w(k, shape, fan_in, gain=1.0):
        return jax.random.normal(k, shape, f32) * (gain * fan_in ** -0.5)

    def g(k, shape):
        return 1.0 + 0.05 * jax.random.normal(k, shape, f32)

    A, Bn = N_LAYERS_A, N_LAYERS_B
    x = jax.random.normal(ks[0], (BATCH, SEQ, D_MODEL), f32)
    c = jax.random.normal(ks[1], (BATCH, D_MODEL), f32)
    positions = (jnp.arange(SEQ, dtype=jnp.int32)[None, :]
                 + jax.random.randint(ks[2], (BATCH, 1), 0, 1024, dtype=jnp.int32))
    return {
        'x': x,
        'c': c,
        'positions': positions,
        'w_ada': w(ks[3], (DEPTH, D_MODEL, 6 * D_MODEL), D_MODEL, 0.5),
        'b_ada': 0.02 * jax.random.normal(ks[4], (DEPTH, 6 * D_MODEL), f32),
        'g_mix': g(ks[5], (DEPTH, D_MODEL)),
        'g_mlp': g(ks[6], (DEPTH, D_MODEL)),
        'mla_w_dq': w(ks[7], (A, D_MODEL, Q_LORA), D_MODEL),
        'mla_g_q': g(ks[8], (A, Q_LORA)),
        'mla_w_uq': w(ks[9], (A, Q_LORA, MLA_HEADS * (QK_NOPE + QK_ROPE)), Q_LORA),
        'mla_w_dkv': w(ks[10], (A, D_MODEL, KV_LORA + QK_ROPE), D_MODEL),
        'mla_g_kv': g(ks[11], (A, KV_LORA)),
        'mla_w_ukv': w(ks[12], (A, KV_LORA, MLA_HEADS * (QK_NOPE + V_DIM)), KV_LORA),
        'mla_w_o': w(ks[13], (A, MLA_HEADS * V_DIM, D_MODEL), MLA_HEADS * V_DIM),
        'swa_w_qkv': w(ks[14], (Bn, D_MODEL, (SWA_HEADS + 2 * SWA_KV_HEADS) * SWA_HEAD_DIM), D_MODEL),
        'swa_b_qkv': 0.02 * jax.random.normal(ks[15], (Bn, (SWA_HEADS + 2 * SWA_KV_HEADS) * SWA_HEAD_DIM), f32),
        'swa_sinks': 0.5 * jax.random.normal(ks[16], (Bn, SWA_HEADS), f32),
        'swa_w_o': w(ks[17], (Bn, SWA_HEADS * SWA_HEAD_DIM, D_MODEL), SWA_HEADS * SWA_HEAD_DIM),
        'swa_b_o': 0.02 * jax.random.normal(ks[18], (Bn, D_MODEL), f32),
        'w_ff1': w(ks[19], (DEPTH, D_MODEL, D_FF), D_MODEL),
        'w_ff2': w(ks[20], (DEPTH, D_FF, D_MODEL), D_FF),
        'g_final': g(ks[21], (D_MODEL,)),
    }

def first_block(x, c, positions, w_ada, b_ada, g_mix, g_mlp,
              mla_w_dq, mla_g_q, mla_w_uq, mla_w_dkv, mla_g_kv, mla_w_ukv, mla_w_o,
              swa_w_qkv, swa_b_qkv, swa_sinks, swa_w_o, swa_b_o,
              w_ff1, w_ff2, g_final):
    cond = jax.nn.silu(c)
    for i in range(DEPTH):
        mod = cond @ w_ada[i] + b_ada[i]
        sh1, sc1, gt1, sh2, sc2, gt2 = jnp.split(mod, 6, axis=-1)
        h = modulate(x, g_mix[i], sh1, sc1)
        j = i // N_MIXERS
        if i % N_MIXERS == 0:
            y = mla(h, positions, mla_w_dq[j], mla_g_q[j], mla_w_uq[j], mla_w_dkv[j],
                    mla_g_kv[j], mla_w_ukv[j], mla_w_o[j])
        else:
            y = swa(h, swa_w_qkv[j], swa_b_qkv[j], swa_sinks[j], swa_w_o[j], swa_b_o[j])
        x = x + gt1[:, None, :] * y
        h = modulate(x, g_mlp[i], sh2, sc2)
        y = jnp.square(jax.nn.relu(h @ w_ff1[i])) @ w_ff2[i]
        x = x + gt2[:, None, :] * y
    return rmsnorm(x, g_final)


DEPTH_2 = 1

HEAD_DIM = 64
HEADS_PER_GROUP = 4
DILATED_GROUPS = ((128, 1), (512, 4), (2048, 16))
N_GROUPS = len(DILATED_GROUPS)
N_ATTN_HEADS = N_GROUPS * HEADS_PER_GROUP
ATTN_WIDTH = N_ATTN_HEADS * HEAD_DIM
ATTN_OUT_WIDTH = HEADS_PER_GROUP * HEAD_DIM
ROT_DIM = HEAD_DIM // 4
ROPE_THETA_2 = 500000.0
BLOCK = 128
POOL_WINDOWS = (2, 4, 8, 16)
POOL_GROUP_WIDTH = 128
POOL_WIDTH = len(POOL_WINDOWS) * POOL_GROUP_WIDTH
N_BRANCHES = 2
IN_WIDTH = 3 * ATTN_WIDTH + POOL_WIDTH + N_BRANCHES * D_MODEL
D_FF_2 = 2816
RMS_EPS = 1e-6


def rms_norm(x, g):
    xf = x.astype(jnp.float32)
    y = xf * lax.rsqrt(jnp.mean(xf * xf, axis=-1, keepdims=True) + RMS_EPS)
    return (y * g.astype(jnp.float32)).astype(x.dtype)

def swiglu(x, w1, w3, w2):
    return (jax.nn.silu(x @ w1) * (x @ w3)) @ w2

def rope_tables(seq):
    pos = jnp.arange(seq, dtype=jnp.float32)
    inv = ROPE_THETA_2 ** (-jnp.arange(0, ROT_DIM, 2, dtype=jnp.float32) / ROT_DIM)
    ang = pos[:, None] * inv[None, :]
    return jnp.cos(ang), jnp.sin(ang)

def apply_partial_rope(x, cos, sin):
    xf = x.astype(jnp.float32)
    half = ROT_DIM // 2
    x1, x2 = xf[..., :half], xf[..., half:ROT_DIM]
    c, s = cos[None, :, None, :], sin[None, :, None, :]
    out = jnp.concatenate([x1 * c - x2 * s, x2 * c + x1 * s, xf[..., ROT_DIM:]], axis=-1)
    return out.astype(x.dtype)

def dilated_window_attention(q, k, v, window, dilation):
    B, S, H, Dh = q.shape
    r = dilation
    L = S // r
    n_back = window // r
    nb = -(-L // BLOCK)
    Lp = nb * BLOCK

    def to_blocks(t):
        t = t.reshape(B, L, r, H, Dh).transpose(0, 2, 1, 3, 4)
        t = jnp.pad(t, ((0, 0), (0, 0), (0, Lp - L), (0, 0), (0, 0)))
        return t.reshape(B, r, nb, BLOCK, H, Dh)

    def band(t):
        prev = jnp.pad(t[:, :, :-1], ((0, 0), (0, 0), (1, 0), (0, 0), (0, 0), (0, 0)))
        return jnp.concatenate([prev, t], axis=3)

    qb = to_blocks(q)
    kk = band(to_blocks(k))
    vv = band(to_blocks(v))
    s = jnp.einsum('brnqhd,brnkhd->brnhqk', qb, kk).astype(jnp.float32) * (Dh ** -0.5)
    qi = jnp.arange(BLOCK)[:, None]
    kj = jnp.arange(2 * BLOCK)[None, :]
    dist = qi + BLOCK - kj
    key_pos = (jnp.arange(nb)[:, None, None] - 1) * BLOCK + kj[None]
    allowed = (dist >= 0)[None] & (dist <= n_back)[None] & (key_pos >= 0)
    s = jnp.where(allowed[None, None, :, None], s, -jnp.inf)
    m = jnp.max(s, axis=-1, keepdims=True)
    p = jnp.exp(s - m)
    l = jnp.sum(p, axis=-1, keepdims=True)
    o = jnp.einsum('brnhqk,brnkhd->brnqhd', p, vv.astype(jnp.float32)) / jnp.swapaxes(l, 3, 4)
    lse = (m + jnp.log(l))[..., 0]
    o = o.reshape(B, r, Lp, H, Dh)[:, :, :L].transpose(0, 2, 1, 3, 4).reshape(B, S, H, Dh)
    lse = lse.transpose(0, 1, 2, 4, 3).reshape(B, r, Lp, H)[:, :, :L].transpose(0, 2, 1, 3).reshape(B, S, H)
    return o, lse

def dilated_mixture_attention(q, k, v):
    B, S = q.shape[:2]
    cos, sin = rope_tables(S)
    q = apply_partial_rope(q, cos, sin)
    k = apply_partial_rope(k, cos, sin)
    outs, lses = [], []
    for g, (window, dilation) in enumerate(DILATED_GROUPS):
        hs = slice(g * HEADS_PER_GROUP, (g + 1) * HEADS_PER_GROUP)
        o, lse = dilated_window_attention(q[:, :, hs], k[:, :, hs], v[:, :, hs], window, dilation)
        outs.append(o)
        lses.append(lse)
    alpha = jax.nn.softmax(jnp.stack(lses, axis=0), axis=0)
    o = jnp.sum(alpha[..., None] * jnp.stack(outs, axis=0), axis=0)
    return o.reshape(B, S, ATTN_OUT_WIDTH).astype(v.dtype)

def multiscale_pool(p, w_pool, pool_scale):
    B, S, C = p.shape
    pf = p.astype(jnp.float32)
    cs0 = jnp.concatenate([jnp.zeros((B, 1, C), jnp.float32), jnp.cumsum(pf, axis=1)], axis=1)
    outs = []
    for gi, win in enumerate(POOL_WINDOWS):
        cs = slice(gi * POOL_GROUP_WIDTH, (gi + 1) * POOL_GROUP_WIDTH)
        c = cs0[..., cs]
        lagged = jnp.pad(c[:, :S - win + 1], ((0, 0), (win - 1, 0), (0, 0)))
        cnt = jnp.minimum(jnp.arange(1, S + 1), win).astype(jnp.float32)[None, :, None]
        outs.append((c[:, 1:] - lagged) / cnt - pf[..., cs])
    d = jnp.stack(outs, axis=2).astype(p.dtype)
    y = jnp.einsum('bsgc,gcd->bsgd', d, w_pool).reshape(B, S, C)
    return y * pool_scale

def second_inputs(seed: int = 0) -> dict:
    key = jax.random.key(seed)
    ks = jax.random.split(key, 20)
    f32 = jnp.float32

    def nrm(k, shape, fan_in):
        return jax.random.normal(k, shape, f32) * (fan_in ** -0.5)

    def gain(k, shape):
        return 1.0 + 0.02 * jax.random.normal(k, shape, f32)

    L = DEPTH_2
    return {
        "x": jax.random.normal(ks[0], (BATCH, SEQ, D_MODEL), f32),
        "ffn1_norm": gain(ks[1], (L, D_MODEL)),
        "ffn1_w1": nrm(ks[2], (L, D_MODEL, D_FF_2), D_MODEL),
        "ffn1_w3": nrm(ks[3], (L, D_MODEL, D_FF_2), D_MODEL),
        "ffn1_w2": nrm(ks[4], (L, D_FF_2, D_MODEL), D_FF_2),
        "mix_norm": gain(ks[5], (L, D_MODEL)),
        "w_in": nrm(ks[6], (L, D_MODEL, IN_WIDTH), D_MODEL),
        "w_branch_attn": nrm(ks[7], (L, ATTN_OUT_WIDTH, D_MODEL), ATTN_OUT_WIDTH),
        "w_branch_pool": nrm(ks[8], (L, POOL_WIDTH, D_MODEL), POOL_WIDTH),
        "pool_w": nrm(ks[9], (L, len(POOL_WINDOWS), POOL_GROUP_WIDTH, POOL_GROUP_WIDTH), POOL_GROUP_WIDTH),
        "pool_scale": gain(ks[10], (L, POOL_WIDTH)),
        "w_out": nrm(ks[11], (L, D_MODEL, D_MODEL), D_MODEL),
        "ffn2_norm": gain(ks[12], (L, D_MODEL)),
        "ffn2_w1": nrm(ks[13], (L, D_MODEL, D_FF_2), D_MODEL),
        "ffn2_w3": nrm(ks[14], (L, D_MODEL, D_FF_2), D_MODEL),
        "ffn2_w2": nrm(ks[15], (L, D_FF_2, D_MODEL), D_FF_2),
        "final_norm": gain(ks[16], (D_MODEL,)),
    }

def second_block(x, ffn1_norm, ffn1_w1, ffn1_w3, ffn1_w2, mix_norm, w_in, w_branch_attn, w_branch_pool,
              pool_w, pool_scale, w_out, ffn2_norm, ffn2_w1, ffn2_w3, ffn2_w2, final_norm):
    B, S, D = x.shape
    h = x
    for l in range(DEPTH_2):
        h = h + 0.5 * swiglu(rms_norm(h, ffn1_norm[l]), ffn1_w1[l], ffn1_w3[l], ffn1_w2[l])
        u = rms_norm(h, mix_norm[l])
        proj = u @ w_in[l]
        o = 0
        q = proj[..., o:o + ATTN_WIDTH].reshape(B, S, N_ATTN_HEADS, HEAD_DIM); o += ATTN_WIDTH
        k = proj[..., o:o + ATTN_WIDTH].reshape(B, S, N_ATTN_HEADS, HEAD_DIM); o += ATTN_WIDTH
        v = proj[..., o:o + ATTN_WIDTH].reshape(B, S, N_ATTN_HEADS, HEAD_DIM); o += ATTN_WIDTH
        pz = proj[..., o:o + POOL_WIDTH]; o += POOL_WIDTH
        gates = jax.nn.sigmoid(proj[..., o:o + N_BRANCHES * D_MODEL].reshape(B, S, N_BRANCHES, D_MODEL))
        y_attn = dilated_mixture_attention(q, k, v) @ w_branch_attn[l]
        y_pool = multiscale_pool(pz, pool_w[l], pool_scale[l]) @ w_branch_pool[l]
        merged = gates[:, :, 0] * y_attn + gates[:, :, 1] * y_pool
        h = h + merged @ w_out[l]
        h = h + 0.5 * swiglu(rms_norm(h, ffn2_norm[l]), ffn2_w1[l], ffn2_w3[l], ffn2_w2[l])
    return rms_norm(h, final_norm)


def setup_inputs(seed=0):
    out = dict(first_inputs(seed))
    for name, value in second_inputs(seed + 1).items():
        if name != "x":
            out[name + "_2"] = value
    return out


def reference(
    x, c, positions, w_ada, b_ada, g_mix, g_mlp, mla_w_dq, mla_g_q, mla_w_uq, mla_w_dkv,
    mla_g_kv, mla_w_ukv, mla_w_o, swa_w_qkv, swa_b_qkv, swa_sinks, swa_w_o, swa_b_o, w_ff1,
    w_ff2, g_final, ffn1_norm_2, ffn1_w1_2, ffn1_w3_2, ffn1_w2_2, mix_norm_2, w_in_2,
    w_branch_attn_2, w_branch_pool_2, pool_w_2, pool_scale_2, w_out_2, ffn2_norm_2, ffn2_w1_2,
    ffn2_w3_2, ffn2_w2_2, final_norm_2,
):
    x = first_block(
        x, c, positions, w_ada, b_ada, g_mix, g_mlp, mla_w_dq, mla_g_q, mla_w_uq, mla_w_dkv,
        mla_g_kv, mla_w_ukv, mla_w_o, swa_w_qkv, swa_b_qkv, swa_sinks, swa_w_o, swa_b_o, w_ff1,
        w_ff2, g_final,
    )
    return second_block(
        x, ffn1_norm_2, ffn1_w1_2, ffn1_w3_2, ffn1_w2_2, mix_norm_2, w_in_2, w_branch_attn_2,
        w_branch_pool_2, pool_w_2, pool_scale_2, w_out_2, ffn2_norm_2, ffn2_w1_2, ffn2_w3_2,
        ffn2_w2_2, final_norm_2,
    )


_drawn_inputs = setup_inputs


def setup_inputs(seed=0):
    import zlib

    import numpy as np

    out = dict(_drawn_inputs(seed))
    spreads = {}
    factors = {'g_mix': 5.706,
     'mla_g_q': 8.0,
     'mla_g_kv': 8.0,
     'swa_b_qkv': 8.0,
     'swa_sinks': 15.22,
     'swa_b_o': 8.0,
     'ffn1_norm_2': 6.457,
     'mix_norm_2': 6.213,
     'pool_scale_2': 18.306,
     'ffn2_norm_2': 25.495,
     'final_norm_2': 7.423}
    for name, (base, spread) in spreads.items():
        noise = np.random.default_rng([zlib.crc32(name.encode()), seed]).standard_normal(out[name].shape)
        drawn = base * np.exp(spread * noise) if base else spread * noise
        out[name] = __import__('jax').numpy.asarray(drawn.astype(out[name].dtype))
    for name, factor in factors.items():
        out[name] = (out[name] * factor).astype(out[name].dtype)
    return out
```

```python
import concourse.bass as bass
from concourse import mybir
from contextlib import ExitStack

S = 512
D = 1024
F32 = mybir.dt.float32
F32R = mybir.dt.float32r
I32 = mybir.dt.int32
ALU = mybir.AluOpType
ACT = mybir.ActivationFunctionType
AX = mybir.AxisListType
EPS = 1e-6
KB = 1024
NRAW = 3
NW = 3
NTMP = 6


def flat(w):
    if w is None:
        return []
    if isinstance(w, tuple) and w and isinstance(w[0], str):
        return [w]
    return [t for x in w for t in flat(x)]


class Queues:

    def __init__(self):
        self.q = {e: [] for e in ("sp", "act", "dve", "pool", "pe")}
        self.n = {}

    def _add(self, eng, sem, by, fn, waits):
        tok = None
        if sem is not None:
            self.n[sem] = self.n.get(sem, 0) + by
            tok = (sem, self.n[sem])
        self.q[eng].append((flat(waits), fn, sem, by))
        return tok

    def act(self, fn, *waits):
        return self._add("act", "act", 1, fn, waits)

    def dve(self, fn, *waits):
        return self._add("dve", "dve", 1, fn, waits)

    def pe(self, fn, *waits, sig=False):
        return self._add("pe", "pe" if sig else None, 1, fn, waits)

    def dma(self, sem, out, in_, *waits):
        return self._add("sp", sem, 16, lambda e: e.dma_start(out, in_), waits)

    def play(self, eng, engine, sems):
        seen = {}
        for waits, fn, sem, by in self.q[eng]:
            for s, v in waits:
                if seen.get(s, 0) < v:
                    engine.wait_ge(sems[s], v)
                    seen[s] = v
            ins = fn(engine)
            if sem is not None:
                ins.then_inc(sems[sem], by)


class Ring:

    def __init__(self, n):
        self.n, self.at, self.rel = n, 0, [None] * n

    def take(self):
        i = self.at % self.n
        self.at += 1
        return i


def bass_two_blocks(nc, A, out):
    Q = Queues()
    act, dve, pe, dma = Q.act, Q.dve, Q.pe, Q.dma

    ctx = ExitStack()
    with ctx:
        base = -(-nc.sbuf_base // 64) * 64
        at = [base]

        def place(nbytes):
            o = at[0]
            at[0] += nbytes
            return o

        names = [0]

        def sb(shape, dt, offset):
            names[0] += 1
            return nc.alloc_sbuf_tensor_at(f"t{names[0]}", shape, dt, offset=offset)

        o_raw = place(NRAW * 8 * KB)
        o_hi = place(NW * 8 * KB)
        o_lo = place(NW * 8 * KB)
        o_x = place(16 * KB)
        o_h = place(32 * KB)
        AR = place(64 * KB)
        o_tmp = place(NTMP * 2 * KB)
        o_r = place(2 * KB)
        o_ssq = place(2 * KB)
        o_acc = place(4 * KB)
        o_c = place(3 * 512)
        o_v = place(107 * 4 + 96 * 4 + 20)
        o_mod = place(2 * 48 * 4)
        o_gs = place(4 * 8 * 4)
        o_st = place(4 * 64 * 4)
        assert at[0] <= nc.sbuf_usable_end, at[0]

        RAW = [sb([128, 2048], F32, o_raw + i * 8 * KB) for i in range(NRAW)]
        WHI = [sb([128, 2048], F32R, o_hi + i * 8 * KB) for i in range(NW)]
        WLO = [sb([128, 2048], F32R, o_lo + i * 8 * KB) for i in range(NW)]
        X = sb([128, 8, S], F32, o_x)
        HHI = sb([128, 8, S], F32R, o_h)
        HLO = sb([128, 8, S], F32R, o_h + 16 * KB)
        TMP = [sb([128, S], F32, o_tmp + i * 2 * KB) for i in range(NTMP)]
        RT = sb([128, S], F32, o_r)
        SSQ = sb([128, S], F32, o_ssq)
        ACC = sb([128, D], F32, o_acc)
        CONST = sb([128, 3, 128], F32, o_c)
        ident, ones, rot = CONST[:, 0, :], CONST[:, 1, :], CONST[:, 2, :]
        VEC = sb([128, 107 + 96 + 5], F32, o_v)
        MOD = sb([128, 2, 48], F32, o_mod)
        GS = sb([128, 4, 8], F32, o_gs)
        ST = sb([128, 256], F32, o_st)

        PS = ctx.enter_context(nc.psum_tensor("PS", [128, 8, 512], F32))

        tmps = Ring(NTMP)
        banks = Ring(8)

        V1 = sb([107, 128], F32, AR + 16 * KB)
        V2 = sb([96, 128], F32, AR + 17 * KB)
        XIN = sb([128, 4, D], F32, AR)
        COS = sb([128, S], F32, AR + 60 * KB)
        SIN = sb([128, S], F32, AR + 62 * KB)
        POS = sb([128, S], I32, AR + 20 * KB)
        PA = sb([128, S], F32, AR + 22 * KB)
        PB = sb([128, S], F32, AR + 24 * KB)
        PC = sb([128, S], F32, AR + 26 * KB)
        PD = sb([128, S], F32, AR + 28 * KB)

        rows = {}
        r = 0
        t_vec = None
        for name, ap, k in (
            ("c", A["c"].rearrange("b (j p) -> (b j) p", p=128), 8),
            ("g_mix", A["g_mix"].rearrange("l (j p) -> (l j) p", p=128), 16),
            ("g_mlp", A["g_mlp"].rearrange("l (j p) -> (l j) p", p=128), 16),
            ("g_q", A["mla_g_q"].rearrange("l (j p) -> (l j) p", p=128), 3),
            ("g_kv", A["mla_g_kv"].rearrange("l (j p) -> (l j) p", p=128), 2),
            ("g_final", A["g_final"].rearrange("(j p) -> j p", p=128), 8),
            ("ffn1_norm", A["ffn1_norm_2"].rearrange("l (j p) -> (l j) p", p=128), 8),
            ("mix_norm", A["mix_norm_2"].rearrange("l (j p) -> (l j) p", p=128), 8),
            ("ffn2_norm", A["ffn2_norm_2"].rearrange("l (j p) -> (l j) p", p=128), 8),
            ("final_norm", A["final_norm_2"].rearrange("(j p) -> j p", p=128), 8),
            ("pool_scale", A["pool_scale_2"].rearrange("l (j p) -> (l j) p", p=128), 4),
            ("bq0", A["swa_b_qkv"][:, 0:512].rearrange("l (e j d) -> (l j) e d", e=2, d=64), 4),
            ("bq1", A["swa_b_qkv"][:, 512:1024].rearrange("l (e j d) -> (l j) e d", e=2, d=64), 4),
            ("bk", A["swa_b_qkv"][:, 1024:1280].rearrange("l (j p) -> (l j) p", p=128), 2),
            ("b_o", A["swa_b_o"].rearrange("l (j p) -> (l j) p", p=128), 8),
        ):
            rows[name] = r
            dst = V1[r:r + k, :]
            if name in ("bq0", "bq1"):
                dst = dst.rearrange("j (e d) -> j e d", e=2)
            t_vec = dma("vec", dst, ap)
            r += k
        assert r == 107
        t_vec = dma("vec", V2[:, :], A["b_ada"].rearrange("l (j p) -> (l j) p", p=128))
        t_vec = dma("vec", CONST[:, :, :], A["k_const"])
        t_vec = dma("vec", VEC[:, 203:204], A["k_invf"])
        t_vec = dma("vec", POS[:, :], A["positions"].to_broadcast([128, S]))
        t_x = dma("x", XIN[:, :, :], A["x"].rearrange("b (t p) d -> p (b t) d", p=128))

        def col(name, j=0, k=1):
            return VEC[:, rows[name] + j:rows[name] + j + k]

        def bada(l, v):
            return VEC[:, 107 + l * 48 + v * 8:107 + l * 48 + v * 8 + 8]

        invf = VEC[:, 203:204]

        b = banks.take()
        t = pe(lambda e, b=b: e.transpose(PS[:, b, 0:107], V1[:, :], ident[0:107, 0:107]), t_vec)
        t = pe(lambda e, b=b: e.transpose(PS[:, b, 128:224], V2[:, :], ident[0:96, 0:96]), sig=True)
        t_v1 = dve(lambda e, b=b: e.tensor_copy(VEC[:, 0:107], PS[:, b, 0:107]), t)
        t_cols = dve(lambda e, b=b: e.tensor_copy(VEC[:, 107:203], PS[:, b, 128:224]), t)
        banks.rel[b] = t_cols

        SC = sb([128, 8], F32, AR + 18 * KB)
        CC = sb([128, 8], F32, AR + 19 * KB)
        SILU = sb([128, 8], F32, o_st)
        t = act(lambda e: e.activation(SC[:, :], col("c", 0, 8), ACT.Exp, scale=-1.0), t_v1)
        t = dve(lambda e: e.tensor_scalar(CC[:, :], SC[:, :], 1.0, None, ALU.add), t)
        t = dve(lambda e: e.reciprocal(SC[:, :], CC[:, :]), t)
        SILUC = VEC[:, rows["c"]:rows["c"] + 8]
        t_silu = dve(lambda e: e.tensor_tensor(SILUC, SILUC, SC[:, :], ALU.mult), t)

        raw_ring = Ring(NRAW)
        w_ring = Ring(NW)
        plan = []
        state = {"loaded": 0, "split": 0, "used": 0}
        late = []
        mod_tok = {}
        mod_used = {}
        acc_rel = [None]

        def weight(name, ap, kt, ncol, parts=None):
            plan.append(dict(kind="w", name=name, ap=ap, kt=kt, nc=ncol, parts=parts))

        def ada(l, v):
            w = A["w_ada"][l].rearrange("(k p) n -> p k n", p=128)
            for u in range(4):
                plan.append(dict(kind="a", l=l, v=v, u=u, kt=2, nc=D,
                                 ap=w[:, 2 * u:2 * u + 2, v * D:(v + 1) * D]))

        def load():
            it = plan[state["loaded"]]
            state["loaded"] += 1
            i = raw_ring.take()
            it["raw"] = i
            n = it["kt"] * it["nc"]
            it["rawv"] = RAW[i][:, 0:n].rearrange("p (k n) -> p k n", k=it["kt"])
            it["landed"] = dma(f"raw{i}", it["rawv"], it["ap"], raw_ring.rel[i])

        def finish_mod(l, v, t_acc):
            b = banks.take()
            for j in range(8):
                t = pe(lambda e, j=j: e.matmul(PS[:, b, j:j + 1], ACC[:, j * 128:(j + 1) * 128], ones[:, 0:1],
                                               start=True, stop=True),
                       banks.rel[b] if j == 0 else None, t_acc, sig=(j == 7))
            acc_rel[0] = t
            dst = MOD[:, l, v * 8:v * 8 + 8]
            t = dve(lambda e: e.tensor_tensor(dst, PS[:, b, 0:8], bada(l, v), ALU.add), t, t_cols)
            banks.rel[b] = t
            if v in (1, 4):
                which = 2 * l + (v == 4)
                g = col("g_mix" if v == 1 else "g_mlp", 8 * l, 8)
                t = dve(lambda e: e.scalar_tensor_tensor(GS[:, which, :], dst, 1.0, g, ALU.add, ALU.mult), t)
            mod_tok[(l, v)] = t

        def split():
            it = plan[state["split"]]
            state["split"] += 1
            raw = it["rawv"]
            if it["kind"] == "a":
                t = it.get("prev")
                for kk in range(2):
                    k = 2 * it["u"] + kk
                    c = SILUC[:, k:k + 1]
                    if k == 0:
                        while late:
                            late.pop(0)()
                        t = dve(lambda e, kk=kk, c=c: e.tensor_scalar(ACC[:, :], raw[:, kk, :], c, None, ALU.mult),
                                it["landed"], acc_rel[0], t_silu)
                    else:
                        t = dve(lambda e, kk=kk, c=c: e.scalar_tensor_tensor(ACC[:, :], raw[:, kk, :], c, ACC[:, :],
                                                                             ALU.mult, ALU.add),
                                it["landed"], state["acc"])
                    state["acc"] = t
                raw_ring.rel[it["raw"]] = t
                if it["u"] == 3:
                    late.append(lambda l=it["l"], v=it["v"], t=t: finish_mod(l, v, t))
            else:
                i = w_ring.take()
                it["slot"] = i
                width = it.get("wide", it["nc"])
                parts = it["parts"] or [(lambda w: w, lambda w: w)]
                wd = it["wd"] = it["kt"] * width
                hi = WHI[i][:, 0:wd].rearrange("p (k n) -> p k n", k=it["kt"])
                lo = WLO[i][:, 0:wd].rearrange("p (k n) -> p k n", k=it["kt"])
                it["hi"], it["lo"] = hi, lo
                th, tl = [], []
                for dst, src in parts:
                    th.append(act(lambda e, d=dst(hi), s=src(raw): e.activation(d, s, ACT.Copy),
                                  it["landed"], w_ring.rel[i]))
                for (dst, src), t in zip(parts, th):
                    tl.append(dve(lambda e, d=dst(lo), h=dst(hi), s=src(raw):
                                  e.tensor_tensor(d, s, h.bitcast(F32), ALU.subtract), it["landed"], t))
                it["ready"] = [th[-1], tl[-1]]
                raw_ring.rel[it["raw"]] = [th[-1], tl[-1]]
                w_ring.rel[i] = "held"
            if state["loaded"] < len(plan):
                load()

        def use(name):
            k = state["used"]
            while plan[k]["kind"] != "w":
                k += 1
            it = plan[k]
            assert it["name"] == name, (it["name"], name)
            state["used"] = k + 1
            while state["split"] < len(plan):
                nxt = plan[state["split"]]
                if nxt["kind"] == "w" and w_ring.rel[w_ring.at % NW] == "held":
                    break
                if nxt["kind"] == "a" and state["split"] > k + 4:
                    break
                split()
            assert "ready" in it
            return it

        def done(it, t):
            w_ring.rel[it["slot"]] = t
            while late:
                late.pop(0)()

        wt = lambda ap: ap.rearrange("(k p) n -> p k n", p=128)
        w_dq, w_dkv = wt(A["mla_w_dq"][0]), wt(A["mla_w_dkv"][0])
        w_uq, w_ukv, w_mo = wt(A["mla_w_uq"][0]), wt(A["mla_w_ukv"][0]), wt(A["mla_w_o"][0])
        w_qkv, w_so = wt(A["swa_w_qkv"][0]), wt(A["swa_w_o"][0])
        w_in, w_out = wt(A["w_in_2"][0]), wt(A["w_out_2"][0])
        w_ba, w_bp = wt(A["w_branch_attn_2"][0]), wt(A["w_branch_pool_2"][0])
        w_pool = A["pool_w_2"][0].rearrange("g c d -> c g d")

        ada(0, 1)
        ada(0, 0)
        for a in range(2):
            weight("dq", w_dq[:, 4 * a:4 * a + 4, :], 4, 384)
        dkv_parts = [(lambda w: w[:, :, 0:320], lambda w: w), (lambda w: w[:, :, 320:384], lambda w: w[:, :, 256:320])]
        for a in range(2):
            weight("dkv", w_dkv[:, 4 * a:4 * a + 4, :], 4, 320)
            plan[-1]["wide"] = 384
            plan[-1]["parts"] = dkv_parts
        ada(0, 2)

        def uq_nope(w):
            return w[:, :, 0:256].rearrange("p k (h c) -> p k h c", h=2)

        def uq_rope(w):
            return w[:, :, 256:384].rearrange("p k (h c) -> p k h c", h=2)

        uq_parts = [(uq_nope, lambda w: w.rearrange("p k (h c) -> p k h c", h=2)[:, :, :, 0:128]),
                    (uq_rope, lambda w: w.rearrange("p k (h c) -> p k h c", h=2)[:, :, :, 128:192])]
        for a in range(4):
            weight("uq", w_uq[:, :, 384 * a:384 * a + 384], 3, 384, uq_parts)
        ada(0, 4)
        for a in range(2):
            weight("ukv", w_ukv[:, :, 1024 * a:1024 * a + 1024], 2, 1024)

        def square(name, w, cols=2, per=512, ks=(4, 4), k0=0):
            for n in range(cols):
                k = k0
                for kt in ks:
                    weight(name, w[:, k:k + kt, n * per:(n + 1) * per], kt, per)
                    k += kt

        ada(0, 3)
        square("mo", w_mo)
        pend = [(0, 5), (1, 1), (1, 0), (1, 2), (1, 4), (1, 3), (1, 5)]

        def ff_plan(l, extra):
            w1, w2 = wt(A["w_ff1"][l]), wt(A["w_ff2"][l])

            def up(q):
                square(f"up{l}", w1[:, :, 1024 * q:1024 * q + 1024])

            def down(q):
                square(f"down{l}", w2, k0=8 * q)

            up(0)
            for q in range(4):
                if extra:
                    ada(*extra.pop(0))
                if q < 3:
                    up(q + 1)
                if extra:
                    ada(*extra.pop(0))
                down(q)

        ff_plan(0, pend)
        assert not pend

        def pairs(h):
            return (lambda w: w.rearrange("p k (j e d) -> p k j e d", e=2, d=64)[:, :, :, h, :],
                    lambda w: w[:, :, 256 * h:256 * h + 256].rearrange("p k (j d) -> p k j d", d=64))

        for n in range(3):
            for a in range(2):
                weight("qkv", w_qkv[:, 4 * a:4 * a + 4, 512 * n:512 * n + 512], 4, 512,
                       [pairs(0), pairs(1)] if n < 2 else None)
        square("so", w_so)
        ff_plan(1, [])

        def glu_plan(w1, w3, w2):
            w1, w3, w2 = wt(w1), wt(w3), wt(w2)

            def up(blk):
                for g in ((0, 4), (4, 8), (8, 11))[blk:blk + 1]:
                    for c in range(*g):
                        weight("w1", w1[:, :, 256 * c:256 * c + 256], 8, 256)
                        weight("w3", w3[:, :, 256 * c:256 * c + 256], 8, 256)

            def down(blk):
                square("w2", w2, ks=((4, 4), (4, 4), (3, 3))[blk], k0=8 * blk)

            up(0)
            for blk in range(3):
                if blk < 2:
                    up(blk + 1)
                down(blk)

        glu_plan(A["ffn1_w1_2"][0], A["ffn1_w3_2"][0], A["ffn1_w2_2"][0])
        square("qk", w_in, cols=3)
        square("v", w_in[:, :, 1536:2048], cols=1)
        weight("v2", w_in[:, :, 2048:2304], 8, 256)
        square("pz", w_in[:, :, 2304:2816], cols=1)
        weight("pw", w_pool, 4, 128)
        for n in range(2):
            square("ga", w_in[:, :, 2816 + 512 * n:3328 + 512 * n], cols=1)
            weight("ba", w_ba[:, :, 512 * n:512 * n + 512], 2, 512)
            square("gp", w_in[:, :, 3840 + 512 * n:4352 + 512 * n], cols=1)
            weight("bp", w_bp[:, :, 512 * n:512 * n + 512], 4, 512)
        square("out", w_out)
        glu_plan(A["ffn2_w1_2"][0], A["ffn2_w3_2"][0], A["ffn2_w2_2"][0])

        for _ in range(NRAW):
            load()

        def mm3(o, wh, wl, xh, xl, first, last, waits, sig):
            pe(lambda e: e.matmul(o, wh, xh, start=first, stop=False), waits)
            pe(lambda e: e.matmul(o, wh, xl, start=False, stop=False))
            return pe(lambda e: e.matmul(o, wl, xh, start=False, stop=last), sig=sig)

        def linear(name, nunits, outs, xs, evac, swap=False):
            bk = [banks.take() for _ in outs]
            k0 = 0
            for u in range(nunits):
                it = use(name)
                last_unit = u == nunits - 1
                for n, (c, w) in enumerate(outs):
                    for k in range(it["kt"]):
                        xh, xl, tx = xs(k0 + k, n)
                        wh, wl = it["hi"][:, k, c:c + w], it["lo"][:, k, c:c + w]
                        end = k == it["kt"] - 1
                        waits = [it["ready"], tx, banks.rel[bk[n]] if u == 0 and k == 0 else None]
                        sig = end and (last_unit or n == len(outs) - 1)
                        first, last = u == 0 and k == 0, last_unit and end
                        if swap:
                            t = mm3(PS[:, bk[n], 0:w], xh, xl, wh, wl, first, last, waits, sig)
                        else:
                            t = mm3(PS[:, bk[n], :], wh, wl, xh, xl, first, last, waits, sig)
                    if last_unit:
                        outs[n] = (c, w, t)
                k0 += it["kt"]
                done(it, t)
            for n, (c, w, t) in enumerate(outs):
                banks.rel[bk[n]] = evac(n, bk[n], t)

        x_tok = [None] * 8
        ssq_rel = [None]
        r_rel = [None]
        h_rel = [None]
        h_tok = [None] * 8

        def take_tmp():
            for _ in range(NTMP):
                i = tmps.take()
                if tmps.rel[i] != "held":
                    break
            rel, tmps.rel[i] = tmps.rel[i], "held"
            assert rel != "held"
            return i, TMP[i], rel

        def sumsq(j, src, t):
            if j == 0:
                sumsq.t = act(lambda e: e.activation(SSQ[:, :], src, ACT.Square), t, ssq_rel[0])
            else:
                i, tm, rel = take_tmp()
                ts = act(lambda e: e.activation(tm[:, :], src, ACT.Square), t, rel)
                sumsq.t = dve(lambda e: e.tensor_tensor(SSQ[:, :], SSQ[:, :], tm[:, :], ALU.add), ts, sumsq.t)
                tmps.rel[i] = sumsq.t

        def rstd(n):
            b = banks.take()
            t = pe(lambda e: e.matmul(PS[:, b, :], ones, SSQ[:, :], start=True, stop=True),
                   sumsq.t, banks.rel[b], sig=True)
            ssq_rel[0] = t
            i, tm, rel = take_tmp()
            t = dve(lambda e: e.tensor_scalar(tm[:, :], PS[:, b, :], 1.0 / n, EPS, ALU.mult, ALU.add), t, rel)
            banks.rel[b] = t
            j, tm2, rel = take_tmp()
            t = act(lambda e: e.activation(tm2[:, :], tm[:, :], ACT.Sqrt), t, rel)
            tmps.rel[i] = t
            t = dve(lambda e: e.reciprocal(RT[:, :], tm2[:, :]), t, r_rel[0])
            tmps.rel[j] = t
            return t

        def normed(n, src, src_tok, gain, shift, hi, lo, t_r, after):
            toks = [None] * n
            held = {}
            for j in range(n + 1):
                if j < n:
                    i, tm, rel = take_tmp()
                    t = dve(lambda e, j=j, tm=tm: e.scalar_tensor_tensor(tm[:, :], src(j), gain(j), RT[:, :],
                                                                         ALU.mult, ALU.mult), rel, t_r, src_tok[j])
                    if shift is None:
                        th = act(lambda e, j=j, tm=tm: e.activation(hi(j), tm[:, :], ACT.Copy), t, after)
                    else:
                        th = act(lambda e, j=j, tm=tm: e.activation(hi(j), tm[:, :], ACT.Identity, bias=shift(j)), t,
                                 after)
                    held[j] = (i, tm, t, th)
                    r_rel[0] = t
                if j >= 1:
                    p = j - 1
                    i, tm, t, th = held.pop(p)
                    if shift is None:
                        tl = dve(lambda e, p=p, tm=tm: e.tensor_tensor(lo(p), tm[:, :], hi(p).bitcast(F32),
                                                                       ALU.subtract), t, th, after)
                    else:
                        tl = dve(lambda e, p=p, tm=tm: e.scalar_tensor_tensor(lo(p), tm[:, :], shift(p),
                                                                              hi(p).bitcast(F32), ALU.add,
                                                                              ALU.subtract), t, th, after)
                    tmps.rel[i] = [th, tl]
                    toks[p] = [th, tl]
            return toks

        def modulation(l, v):
            while not ((l, v) in mod_tok and (l, v + 1) in mod_tok):
                if late:
                    late.pop(0)()
                else:
                    split()

        def norm_x(gain, shift):
            t_r = rstd(D)
            h_tok[:] = normed(8, lambda j: X[:, j, :], x_tok, gain, shift,
                              lambda j: HHI[:, j, :], lambda j: HLO[:, j, :], t_r, h_rel[0])

        def hx(k, n):
            return HHI[:, k, :], HLO[:, k, :], h_tok[k]

        def hx_tok(k, n):
            return HHI[:, k, n * 128:(n + 1) * 128], HLO[:, k, n * 128:(n + 1) * 128], h_tok[k]

        def two_parts(hi, lo, src, t, *after):
            th = act(lambda e: e.activation(hi, src, ACT.Copy), t, after)
            tl = dve(lambda e: e.tensor_tensor(lo, src, hi.bitcast(F32), ALU.subtract), t, th, after)
            return [th, tl]

        def add_x(j, b, scale, t, t_scale, stats=True):
            t = dve(lambda e: e.scalar_tensor_tensor(X[:, j, :], PS[:, b, :], scale, X[:, j, :], ALU.mult, ALU.add),
                    t, x_tok[j], t_scale)
            x_tok[j] = [t]
            if stats:
                sumsq(j, X[:, j, :], t)
            return t

        four = [(0, 128), (128, 128), (256, 128), (384, 128)]

        def rotated(dst, b, t, cosv, sinv, rotm, t_tab, after):
            i, tm, rel = take_tmp()
            ta = act(lambda e: e.activation(tm[:, :], PS[:, b, :], ACT.Copy), t, rel)
            b2 = banks.take()
            tp = pe(lambda e: e.matmul(PS[:, b2, :], rotm, tm[:, :], start=True, stop=True), ta, banks.rel[b2], t_tab,
                    sig=True)
            i2, tm2, rel2 = take_tmp()
            t1 = dve(lambda e: e.tensor_tensor(dst, tm[:, :], cosv, ALU.mult), ta, t_tab, after)
            t2 = dve(lambda e: e.tensor_tensor(tm2[:, :], PS[:, b2, :], sinv, ALU.mult), tp, rel2, t_tab)
            banks.rel[b2] = t2
            t3 = dve(lambda e: e.tensor_tensor(dst, dst, tm2[:, :], ALU.add), t1, t2)
            tmps.rel[i] = [tp, t1]
            tmps.rel[i2] = t3
            return ta, t3

        for j in range(8):
            b = banks.take()
            for t4 in range(4):
                t = pe(lambda e, j=j, b=b, t4=t4: e.transpose(PS[:, b, t4 * 128:(t4 + 1) * 128],
                                                              XIN[:, t4, j * 128:(j + 1) * 128], ident),
                       t_x, t_vec, banks.rel[b] if t4 == 0 else None, sig=(t4 == 3))
            t = act(lambda e, j=j, b=b: e.activation(X[:, j, :], PS[:, b, :], ACT.Copy), t)
            banks.rel[b] = t
            x_tok[j] = [t]
            sumsq(j, X[:, j, :], t)

        TWO_PI = 6.283185307179586
        C1, C2 = 6.28125, 0.0019350051879882812
        C3 = TWO_PI - C1 - C2
        MAGIC = 12582912.0
        t = dve(lambda e: e.tensor_copy(PA[:, :], POS[:, :]), t_vec)
        t_ang = dve(lambda e: e.tensor_scalar(PB[:, :], PA[:, :], invf, None, ALU.mult), t)
        t_tab = []
        for dst, quarter in ((SIN, 0.0), (COS, 0.25)):
            t = dve(lambda e, quarter=quarter: e.tensor_scalar(PC[:, :], PB[:, :], 1.0 / TWO_PI, quarter, ALU.mult,
                                                               ALU.add), t_ang, t_tab)
            t = dve(lambda e: e.tensor_scalar(PD[:, :], PC[:, :], MAGIC, None, ALU.add), t)
            t = dve(lambda e: e.tensor_scalar(PC[:, :], PD[:, :], MAGIC, None, ALU.subtract), t)
            t = dve(lambda e: e.scalar_tensor_tensor(PD[:, :], PC[:, :], -C1, PB[:, :], ALU.mult, ALU.add), t)
            t = dve(lambda e: e.scalar_tensor_tensor(PA[:, :], PC[:, :], -C2, PD[:, :], ALU.mult, ALU.add), t)
            t = dve(lambda e: e.scalar_tensor_tensor(PD[:, :], PC[:, :], -C3, PA[:, :], ALU.mult, ALU.add), t)
            t = dve(lambda e, quarter=quarter: e.tensor_scalar(PA[:, :], PD[:, :], quarter * TWO_PI, 3.1415925,
                                                               ALU.add, ALU.min), t)
            t = dve(lambda e: e.tensor_scalar(PD[:, :], PA[:, :], -3.1415925, None, ALU.max), t)
            t_tab = [act(lambda e, dst=dst: e.activation(dst[:, :], PD[:, :], ACT.Sin), t)]
        CMASK = sb([128, 128], F32, AR + 32 * KB)
        t_mask = dma("mask0", CMASK[:, :], A["k_causal"])

        modulation(0, 0)
        norm_x(lambda j: GS[:, 0, j:j + 1], lambda j: MOD[:, 0, j:j + 1])
        CQH = sb([128, 3, S], F32R, AR + 33 * KB)
        CQL = sb([128, 3, S], F32R, AR + 39 * KB)
        CKH = sb([128, 2, S], F32R, AR + 45 * KB)
        CKL = sb([128, 2, S], F32R, AR + 49 * KB)
        KR = sb([128, S], F32, AR + 53 * KB)
        QN = sb([128, 8, S], F32, AR)
        QR = sb([128, 4, S], F32, AR + 16 * KB)
        PBUF = [sb([128, 1280], F32, AR + 24 * KB), sb([128, 1280], F32, AR + 55 * KB)]
        KN = sb([128, 8, S], F32, o_h)
        VV = sb([128, 8, 4, 128], F32, o_h + 16 * KB)

        def low_rank(name, outs, n, gain, hi, lo, width, extra=None):
            held = []

            def evac(m, b, t):
                if m >= n:
                    return extra(b, t)
                i, tm, rel = take_tmp()
                t = act(lambda e: e.activation(tm[:, :], PS[:, b, :], ACT.Copy), t, rel)
                held.append((i, tm, t))
                sumsq(m, tm[:, :], t)
                return t

            linear(name, 2, outs, hx, evac)
            t_r = rstd(width)
            toks = []
            for j, (i, tm, t) in enumerate(held):
                t1 = dve(lambda e, j=j, tm=tm: e.scalar_tensor_tensor(tm[:, :], tm[:, :], gain(j), RT[:, :], ALU.mult,
                                                                      ALU.mult), t, t_r, sumsq.t)
                r_rel[0] = t1
                tt = two_parts(hi[:, j, :], lo[:, j, :], tm[:, :], t1)
                tmps.rel[i] = tt
                toks.append(tt)
            return toks

        cq_tok = low_rank("dq", [(0, 128), (128, 128), (256, 128)], 3, lambda j: col("g_q", j), CQH, CQL, 384)
        kr = {}

        def kr_evac(b, t):
            ta, kr["t"] = rotated(KR[:, :], b, t, COS[:, :], SIN[:, :], rot, t_tab, None)
            return ta

        ck_tok = low_rank("dkv", [(0, 128), (128, 128), (256, 128)], 2, lambda j: col("g_kv", j), CKH, CKL, 256,
                          kr_evac)
        h_free = Q.n["pe"]

        qn_tok, qr_tok = {}, {}
        for p in range(4):
            def evac(n, b, t, p=p):
                if n < 2:
                    h = 2 * p + n
                    t = act(lambda e: e.activation(QN[:, h, :], PS[:, b, :], ACT.Copy), t)
                    qn_tok[h] = t
                    return t
                ta, qr_tok[p] = rotated(QR[:, p, :], b, t, COS[:, :], SIN[:, :], rot, t_tab, None)
                return ta
            linear("uq", 1, [(0, 128), (128, 128), (256, 128)],
                   lambda k, n: (CQH[:, k, :], CQL[:, k, :], cq_tok[k]), evac)
        kn_tok, vv_tok = {}, {}
        for hb in range(2):
            it = use("ukv")
            for hh in range(4):
                h = 4 * hb + hh
                b = banks.take()
                for k in range(2):
                    t = mm3(PS[:, b, :], it["hi"][:, k, 256 * hh:256 * hh + 128],
                            it["lo"][:, k, 256 * hh:256 * hh + 128], CKH[:, k, :], CKL[:, k, :], k == 0, k == 1,
                            [it["ready"], ck_tok[k], banks.rel[b] if k == 0 else None], k == 1)
                t = act(lambda e, h=h, b=b: e.activation(KN[:, h, :], PS[:, b, :], ACT.Copy), t)
                banks.rel[b] = t
                kn_tok[h] = t
            vh = it["hi"].rearrange("p k (h c) -> p k h c", c=256)
            vl = it["lo"].rearrange("p k (h c) -> p k h c", c=256)
            for t4 in range(4):
                b = banks.take()
                ts = slice(t4 * 128, t4 * 128 + 128)
                o = PS[:, b, :].rearrange("p (h c) -> p h c", c=128)
                for k in range(2):
                    t = mm3(o, CKH[:, k, ts], CKL[:, k, ts], vh[:, k, :, 128:256], vl[:, k, :, 128:256],
                            k == 0, k == 1, [banks.rel[b] if k == 0 else None], k == 1)
                tv = dve(lambda e, hb=hb, t4=t4, o=o: e.tensor_copy(VV[:, 4 * hb:4 * hb + 4, t4, :], o), t)
                banks.rel[b] = tv
                vv_tok[(hb, t4)] = tv
            done(it, t)

        MSCALE = 192.0 ** -0.5
        SPOS = {0: (1, 0), 1: (2, 0), 2: (1, 128), 3: (0, 0)}
        POFF = [0, 128, 384, 768]
        free = {b: banks.rel[b] for b in range(8)}
        p_rel = [None, None]
        soft = {}
        o_tok = [None] * 8

        def m_scores(h):
            off = 64 * (h % 2)
            toks = {}
            for i in (0, 2, 1, 3):
                bk, c = SPOS[i]
                w = 128 * (i + 1)
                o = PS[:, bk, c:c + w]
                qs = slice(i * 128, i * 128 + 128)
                pe(lambda e, o=o, qs=qs, w=w: e.matmul(o, QN[:, h, qs], KN[:, h, 0:w], start=True, stop=False),
                   free[bk], qn_tok[h], kn_tok[h])
                toks[i] = pe(lambda e, o=o, qs=qs, w=w: e.matmul(o, QR[off:off + 64, h // 2, qs], KR[off:off + 64, 0:w],
                                                                 start=False, stop=True),
                             qr_tok[h // 2], kr["t"], sig=True)
            st = ST[:, 16 * h:16 * h + 16]
            tm = {}
            for i in (0, 2, 1, 3):
                bk, c = SPOS[i]
                d = PS[:, bk, c + 128 * i:c + 128 * i + 128]
                tm[i] = dve(lambda e, d=d: e.tensor_tensor(d, d, CMASK[:, :], ALU.add), toks[0 if i == 2 else i],
                            toks[2] if i == 0 else toks[i], t_mask)
            tx = []
            for i in (0, 2, 1, 3):
                bk, c = SPOS[i]
                s = PS[:, bk, c:c + 128 * (i + 1)]
                tx.append(dve(lambda e, s=s, i=i: e.tensor_reduce(st[:, i:i + 1], s, AX.X, ALU.max), tm[i]))
            tn = dve(lambda e: e.tensor_scalar(st[:, 4:8], st[:, 0:4], -MSCALE, None, ALU.mult), tx)
            P = PBUF[h % 2]
            te = {}
            for i in (0, 2, 1, 3):
                bk, c = SPOS[i]
                w = 128 * (i + 1)
                te[i] = act(lambda e, i=i, bk=bk, c=c, w=w: e.activation(
                    P[:, POFF[i]:POFF[i] + w], PS[:, bk, c:c + w], ACT.Exp, bias=st[:, 4 + i:5 + i], scale=MSCALE,
                    accum_out=st[:, 8 + i:9 + i]), tn, p_rel[h % 2])
            free[0], free[1], free[2] = te[3], [te[0], te[2]], te[1]
            tr = dve(lambda e: e.reciprocal(st[:, 12:16], st[:, 8:12]), list(te.values()))
            tp = {}
            for i in (0, 2, 1, 3):
                w = 128 * (i + 1)
                Pi = P[:, POFF[i]:POFF[i] + w]
                tp[i] = dve(lambda e, Pi=Pi, i=i: e.tensor_scalar(Pi, Pi, st[:, 12 + i:13 + i], None, ALU.mult), tr)
            soft[h] = tp

        def m_values(h):
            P = PBUF[h % 2]
            tp = soft[h]
            where = {0: (3, 0), 1: (4, 0), 2: (5, 0), 3: (4, 384)}
            tl = {}
            for j in (0, 1, 3, 2):
                bk, c = where[j]
                for i in range(j, 4):
                    t = pe(lambda e, bk=bk, c=c, i=i, j=j: e.transpose(
                        PS[:, bk, c + (i - j) * 128:c + (i - j) * 128 + 128],
                        P[:, POFF[i] + j * 128:POFF[i] + j * 128 + 128], ident), free[bk], tp[i], sig=(i == 3))
                tl[j] = t
            p_rel[h % 2] = t
            pt = {}
            for bk, n, tok, on in ((3, 512, tl[0], act), (4, 512, tl[3], dve), (5, 256, tl[2], act)):
                i, tm, rel = take_tmp()
                if on is act:
                    t = act(lambda e, bk=bk, n=n, tm=tm: e.activation(tm[:, 0:n], PS[:, bk, 0:n], ACT.Copy), tok, rel)
                else:
                    t = dve(lambda e, bk=bk, n=n, tm=tm: e.tensor_copy(tm[:, 0:n], PS[:, bk, 0:n]), tok, rel)
                free[bk] = t
                pt[bk] = (i, tm, t)
            ob = 6 + h % 2
            for j in range(4):
                bk, c = where[j]
                w = 512 - 128 * j
                i, tm, t = pt[bk]
                tpv = pe(lambda e, j=j, c=c, w=w, tm=tm: e.matmul(PS[:, ob, 128 * j:512], VV[:, h, j, :], tm[:, c:c + w],
                                                                  start=(j == 0), stop=(j == 3),
                                                                  skip_group_check=True),
                         t, free[ob], vv_tok[(h // 4, j)], sig=(j == 3))
            for i, tm, t in pt.values():
                tmps.rel[i] = tpv
            o_tok[h] = two_parts(HHI[:, h, :], HLO[:, h, :], PS[:, ob, :], tpv)
            free[ob] = o_tok[h]

        m_scores(0)
        for h in range(8):
            if h < 7:
                m_scores(h + 1)
            m_values(h)
        for b in range(8):
            banks.rel[b] = free[b]

        def ox(k, n):
            return HHI[:, k, :], HLO[:, k, :], o_tok[k]

        for n2 in range(2):
            linear("mo", 2, list(four), ox,
                   lambda n, b, t: add_x(4 * n2 + n, b, MOD[:, 0, 16 + 4 * n2 + n:17 + 4 * n2 + n], t, mod_tok[(0, 2)]))
        h_rel[0] = ("pe", Q.n["pe"])

        HID = [[sb([128, 8, S], F32R, AR + (2 * i + k) * 16 * KB) for k in range(2)] for i in range(2)]
        hid_tok = [[None] * 8, [None] * 8]
        hid_rel = [None, None]

        def ff(l, t_arena):
            hid_rel[:] = [t_arena, t_arena]

            def up(q):
                hi, lo = HID[q % 2]
                for n2 in range(2):
                    def evac(n, b, t, n2=n2):
                        j = 4 * n2 + n
                        i, tm, rel = take_tmp()
                        ta = act(lambda e: e.activation(tm[:, :], PS[:, b, :], ACT.Relu), t, rel)
                        i2, tm2, rel2 = take_tmp()
                        td = dve(lambda e: e.tensor_tensor(tm2[:, :], tm[:, :], tm[:, :], ALU.mult), ta, rel2)
                        tmps.rel[i] = td
                        tt = two_parts(hi[:, j, :], lo[:, j, :], tm2[:, :], td, hid_rel[q % 2])
                        tmps.rel[i2] = tt
                        hid_tok[q % 2][j] = tt
                        return ta
                    linear(f"up{l}", 2, list(four), hx, evac)

            def down(q):
                hi, lo = HID[q % 2]
                for n2 in range(2):
                    linear(f"down{l}", 2, list(four), lambda k, n: (hi[:, k, :], lo[:, k, :], hid_tok[q % 2][k]),
                           lambda n, b, t: add_x(4 * n2 + n, b, MOD[:, l, 40 + 4 * n2 + n:41 + 4 * n2 + n], t,
                                                 mod_tok[(l, 5)], q == 3))
                hid_rel[q % 2] = ("pe", Q.n["pe"])

            up(0)
            for q in range(4):
                if q < 3:
                    up(q + 1)
                if q == 2:
                    h_rel[0] = ("pe", Q.n["pe"])
                down(q)

        def mod_norm(l, part):
            v = 3 * part
            modulation(l, v)
            norm_x(lambda j: GS[:, 2 * l + part, j:j + 1], lambda j: MOD[:, l, 8 * v + j:8 * v + j + 1])

        def now(eng):
            return (eng, Q.n[eng])

        mod_norm(0, 1)
        ff(0, now("pe"))

        t_arena = [now("pe"), now("act"), now("dve")]
        mod_norm(1, 0)
        SQ = sb([128, 8, S], F32, AR)
        SK = sb([128, 2, S], F32, AR + 16 * KB)
        SV = sb([128, 4, 256], F32, AR + 20 * KB)
        DIST = sb([128, 1024], F32, AR + 24 * KB)
        SB2 = [sb([128, 4, 256], F32, AR + 28 * KB), sb([128, 4, 256], F32, AR + 32 * KB)]
        PT2 = [sb([128, 1024], F32, AR + 36 * KB), sb([128, 1024], F32, AR + 40 * KB)]
        BV = sb([128, 256], F32, AR + 44 * KB)
        SINK = sb([128, 16], F32, AR + 45 * KB)
        t_swa = dma("swa", DIST[:, :], A["k_dist"], t_arena)
        t_swa = dma("swa", BV[:, :], A["swa_b_qkv"][:, 1280:1536].to_broadcast([128, 256]))
        t_swa = dma("swa", SINK[:, :], A["swa_sinks"].to_broadcast([128, 16]))

        sq_tok, sk_tok, sv_tok = {}, {}, {}
        for n2 in range(2):
            def evac(n, b, t, n2=n2):
                j = 4 * n2 + n
                sq_tok[j] = act(lambda e: e.activation(SQ[:, j, :], PS[:, b, :], ACT.Identity, bias=col("bq0", j)), t,
                                t_arena)
                return sq_tok[j]
            linear("qkv", 2, list(four), hx, evac)
        ia, ib = use("qkv"), use("qkv")
        for n in range(2):
            b = banks.take()
            for k in range(8):
                it = (ia, ib)[k // 4]
                cs = slice(128 * n, 128 * n + 128)
                t = mm3(PS[:, b, :], it["hi"][:, k % 4, cs], it["lo"][:, k % 4, cs], HHI[:, k, :], HLO[:, k, :],
                        k == 0, k == 7, [it["ready"], h_tok[k], banks.rel[b] if k == 0 else None], k == 7)
            sk_tok[n] = act(lambda e, n=n, b=b: e.activation(SK[:, n, :], PS[:, b, :], ACT.Identity, bias=col("bk", n)),
                            t, t_arena)
            banks.rel[b] = sk_tok[n]
        for t4 in range(4):
            b = banks.take()
            ts = slice(128 * t4, 128 * t4 + 128)
            for k in range(8):
                it = (ia, ib)[k // 4]
                t = mm3(PS[:, b, 0:256], HHI[:, k, ts], HLO[:, k, ts], it["hi"][:, k % 4, 256:512],
                        it["lo"][:, k % 4, 256:512], k == 0, k == 7, [banks.rel[b] if k == 0 else None], k == 7)
            sv_tok[t4] = dve(lambda e, t4=t4, b=b: e.tensor_tensor(SV[:, t4, :], PS[:, b, 0:256], BV[:, :], ALU.add), t,
                             t_swa, t_arena)
            banks.rel[b] = sv_tok[t4]
        done(ia, t)
        done(ib, t)
        t_h = t

        free = {b: banks.rel[b] for b in range(8)}
        sb_rel = [None, None]
        pt_rel = [None, None]
        soft2 = {}

        def s_scores(h):
            half, hh = h // 8, h % 8
            tile, off = 4 * half + hh % 4, 64 * (hh // 4)
            kt = h // 8
            bk = 2 * (h % 2)
            toks = []
            for n in range(4):
                ks = slice(128 * max(n - 1, 0), 128 * max(n - 1, 0) + 256)
                o = PS[:, bk + n // 2, 256 * (n % 2):256 * (n % 2) + 256]
                qs = slice(128 * n, 128 * n + 128)
                t = pe(lambda e, o=o, qs=qs, ks=ks: e.matmul(o, SQ[off:off + 64, tile, qs], SK[off:off + 64, kt, ks],
                                                             start=True, stop=True),
                       free[bk], free[bk + 1], sq_tok[tile], sk_tok[kt], sig=(n == 3))
            slope = 2.0 ** (-8.0 * (h + 1) / 16)
            B = SB2[h % 2]
            st = ST[:, 16 * (h % 16):16 * (h % 16) + 16]
            t = dve(lambda e: e.scalar_tensor_tensor(B.rearrange("p n k -> p (n k)"), DIST[:, :], -8.0 * slope,
                                                     PS[:, bk:bk + 2, :].rearrange("p n k -> p (n k)"), ALU.mult,
                                                     ALU.add), t, t_swa, sb_rel[h % 2])
            free[bk] = free[bk + 1] = t
            t = dve(lambda e: e.tensor_reduce(st[:, 0:4], B[:, :, :], AX.X, ALU.max), t)
            t = dve(lambda e: e.tensor_scalar(st[:, 4:8], st[:, 0:4], 0.125, SINK[:, h:h + 1], ALU.mult, ALU.max), t)
            t = dve(lambda e: e.tensor_scalar(st[:, 0:4], st[:, 4:8], -1.0, None, ALU.mult), t)
            te = []
            for n in range(4):
                te.append(act(lambda e, n=n: e.activation(B[:, n, :], B[:, n, :], ACT.Exp, bias=st[:, n:n + 1],
                                                          scale=0.125, accum_out=st[:, 8 + n:9 + n]), t))
            te.append(act(lambda e: e.activation(st[:, 12:16], st[:, 0:4], ACT.Exp, bias=SINK[:, h:h + 1]), t))
            t = dve(lambda e: e.tensor_tensor(st[:, 4:8], st[:, 8:12], st[:, 12:16], ALU.add), te)
            t = dve(lambda e: e.reciprocal(st[:, 0:4], st[:, 4:8]), t)
            soft2[h] = dve(lambda e: e.tensor_tensor(B[:, :, :], B[:, :, :],
                                                     st[:, 0:4].unsqueeze(2).to_broadcast([128, 4, 256]), ALU.mult), t)

        def s_values(h):
            B, P = SB2[h % 2], PT2[h % 2]
            g = h // 4
            for m in range(1, 8):
                n, w = m // 2, m % 2
                src = B[:, n, 128 * w:128 * w + 128] if n else B[:, 0, 0:128]
                t = pe(lambda e, m=m, src=src: e.transpose(PS[:, 4 + m // 4, 128 * (m % 4):128 * (m % 4) + 128], src,
                                                           ident), free[4], free[5], soft2[h], sig=(m == 7))
            sb_rel[h % 2] = t
            ps = PS[:, 4:6, :].rearrange("p n k -> p (n k)")
            t = act(lambda e: e.activation(P[:, 128:1024], ps[:, 128:1024], ACT.Copy), t, pt_rel[h % 2])
            free[4] = free[5] = t
            ob, off = 6 + (h // 2) % 2, 64 * (h % 2)
            for n in range(4):
                o = PS[off:off + 64, ob, 128 * n:128 * n + 128]
                if n:
                    pe(lambda e, o=o, n=n: e.matmul(o, SV[:, n - 1, 64 * g:64 * g + 64], P[:, 256 * n:256 * n + 128],
                                                    start=True, stop=False),
                       t, free[ob], sv_tok[n])
                tv = pe(lambda e, o=o, n=n: e.matmul(o, SV[:, n, 64 * g:64 * g + 64], P[:, 256 * n + 128:256 * n + 256],
                                                     start=(n == 0), stop=True), t, free[ob], sv_tok[n], sig=(n == 3))
            pt_rel[h % 2] = tv
            if h % 2:
                o_tok[h // 2] = two_parts(HHI[:, h // 2, :], HLO[:, h // 2, :], PS[:, ob, :], tv, t_h)
                free[ob] = o_tok[h // 2]

        s_scores(0)
        for h in range(16):
            if h < 15:
                s_scores(h + 1)
            s_values(h)
        for b in range(8):
            banks.rel[b] = free[b]

        GB = sb([128, 8], F32, AR + 46 * KB)
        t_gb = dve(lambda e: e.tensor_tensor(GB[:, :], MOD[:, 1, 16:24], col("b_o", 0, 8), ALU.mult), mod_tok[(1, 2)],
                   t_cols, t_arena)
        for n2 in range(2):
            def evac(n, b, t, n2=n2):
                j = 4 * n2 + n
                i, tm, rel = take_tmp()
                t = dve(lambda e: e.tensor_scalar(tm[:, :], PS[:, b, :], MOD[:, 1, 16 + j:17 + j], GB[:, j:j + 1],
                                                  ALU.mult, ALU.add), t, rel, t_gb)
                t2 = dve(lambda e: e.tensor_tensor(X[:, j, :], X[:, j, :], tm[:, :], ALU.add), t, x_tok[j])
                tmps.rel[i] = t2
                x_tok[j] = [t2]
                sumsq(j, X[:, j, :], t2)
                return t
            linear("so", 2, list(four), ox, evac)
        h_rel[0] = now("pe")
        mod_norm(1, 1)
        ff(1, [now("pe"), now("dve")])

        def norm_in_place(gain):
            t_r = rstd(D)
            for j in range(8):
                t = dve(lambda e, j=j: e.scalar_tensor_tensor(X[:, j, :], X[:, j, :], gain(j), RT[:, :], ALU.mult,
                                                              ALU.mult), t_r, x_tok[j], sumsq.t)
                r_rel[0] = t
                x_tok[j] = [t]
            for j in range(8):
                sumsq(j, X[:, j, :], x_tok[j])

        norm_in_place(lambda j: col("g_final", j))

        def glu(gain):
            norm_x(gain, None)
            t_arena = [now("pe"), now("dve")]
            hid_rel[:] = [t_arena, t_arena]

            def up(blk):
                hi, lo = HID[blk % 2]
                for c in range((4, 4, 3)[blk]):
                    bk = [banks.take() for _ in range(4)]
                    tk = []
                    for w, name in enumerate(("w1", "w3")):
                        it = use(name)
                        for n in range(2):
                            b = bk[2 * w + n]
                            for k in range(8):
                                cs = slice(128 * n, 128 * n + 128)
                                t = mm3(PS[:, b, :], it["hi"][:, k, cs], it["lo"][:, k, cs], HHI[:, k, :],
                                        HLO[:, k, :], k == 0, k == 7,
                                        [it["ready"], h_tok[k], banks.rel[b] if k == 0 else None], k == 7)
                            tk.append(t)
                        done(it, t)
                    for n in range(2):
                        j = 2 * c + n
                        b1, b3 = bk[n], bk[2 + n]
                        i, tm, rel = take_tmp()
                        ta = act(lambda e, tm=tm, b1=b1: e.activation(tm[:, :], PS[:, b1, :], ACT.Silu), tk[n], rel)
                        banks.rel[b1] = ta
                        td = dve(lambda e, tm=tm, b3=b3: e.tensor_tensor(tm[:, :], tm[:, :], PS[:, b3, :], ALU.mult),
                                 ta, tk[2 + n])
                        banks.rel[b3] = td
                        tt = two_parts(hi[:, j, :], lo[:, j, :], tm[:, :], td, hid_rel[blk % 2])
                        tmps.rel[i] = tt
                        hid_tok[blk % 2][j] = tt

            def down(blk):
                hi, lo = HID[blk % 2]
                for n2 in range(2):
                    linear("w2", 2, list(four), lambda k, n: (hi[:, k, :], lo[:, k, :], hid_tok[blk % 2][k]),
                           lambda n, b, t: add_x(4 * n2 + n, b, 0.5, t, None, blk == 2))
                hid_rel[blk % 2] = now("pe")

            up(0)
            for blk in range(3):
                if blk < 2:
                    up(blk + 1)
                if blk == 1:
                    h_rel[0] = now("pe")
                down(blk)

        glu(lambda j: col("ffn1_norm", j))

        norm_x(lambda j: col("mix_norm", j), None)
        t_arena = [now("pe"), now("dve"), now("act")]
        DQ = sb([128, 12, S], F32, AR)
        DV = sb([128, 4, 768], F32, AR + 24 * KB)
        DM = sb([128, 10, 128], F32, AR + 36 * KB)
        SB3 = [sb([128, 1280], F32, AR + 41 * KB), sb([128, 1280], F32, AR + 46 * KB)]
        PT3 = [sb([128, 1280], F32, AR + 51 * KB), sb([128, 1280], F32, AR + 56 * KB)]
        DCOS = sb([128, S], F32, AR + 51 * KB)
        DSIN = sb([128, S], F32, AR + 53 * KB)
        DROT = sb([128, 128], F32, AR + 55 * KB)
        OHI = sb([128, 2, S], F32R, AR)
        OLO = sb([128, 2, S], F32R, AR + 4 * KB)
        t_dm = dma("dil", DM[:, :, :], A["k_dil"], t_arena)
        t_dm = dma("dil", DCOS[:, :], A["k_dcos"])
        t_dm = dma("dil", DSIN[:, :], A["k_dsin"])
        t_dm = dma("dil", DROT[:, :], A["k_drot"])
        dq_tok = {}
        for n3 in range(3):
            def evac(n, b, t, n3=n3):
                j = 4 * n3 + n
                ta, dq_tok[j] = rotated(DQ[:, j, :], b, t, DCOS[:, :], DSIN[:, :], DROT[:, :], t_dm, t_arena)
                return ta
            linear("qk", 2, list(four), hx, evac)
        dv_tok = {}

        def v_evac(c, w):
            def evac(n, b, t):
                tv = act(lambda e: e.activation(DV[:, n, c:c + w], PS[:, b, 0:w], ACT.Copy), t, t_arena)
                dv_tok.setdefault(n, []).append(tv)
                return tv
            return evac

        linear("v", 2, [(0, 512)] * 4, hx_tok, v_evac(0, 512), swap=True)
        linear("v2", 1, [(0, 256)] * 4, hx_tok, v_evac(512, 256), swap=True)

        free = {b: banks.rel[b] for b in range(8)}
        sb3_rel = [None, None]
        pt3_rel = [dq_tok[11], dq_tok[11]]
        soft3 = {}
        SALL = PS[:, 0:3, :].rearrange("p n k -> p (n k)")
        TALL = PS[:, 3:6, :].rearrange("p n k -> p (n k)")

        def blocks(i):
            out = [(0, kb) for kb in ((i - 1, i) if i else (0,))]
            return out + [(1, kb) for kb in range(i + 1)] + [(2, kb) for kb in range(i + 1)]

        def d_scores(s):
            j, i = s // 4, s % 4
            off = 64 * (j % 2)
            bl = blocks(i)
            runs = []
            for c, (g, kb) in enumerate(bl):
                if runs and runs[-1][1] == g and c % 4:
                    runs[-1][3] += 1
                else:
                    runs.append([c, g, kb, 1])
            for m, (c, g, kb, n) in enumerate(runs):
                qt = (4 * g + j) // 2
                t = pe(lambda e, c=c, kb=kb, n=n, qt=qt: e.matmul(
                    SALL[:, 128 * c:128 * (c + n)], DQ[off:off + 64, qt, 128 * i:128 * i + 128],
                    DQ[off:off + 64, 6 + qt, 128 * kb:128 * (kb + n)], start=True, stop=True),
                    free[0], free[1], free[2], dq_tok[qt], dq_tok[6 + qt], sig=(m == len(runs) - 1))
            B = SB3[s % 2]
            st = ST[:, 4 * s:4 * s + 4]
            g0 = 2 if i else 1
            tm = []
            for c, n, m0 in ((0, g0, 2 - g0), (g0, i + 1, 5 - i), (g0 + i + 1, i + 1, 9 - i)):
                tm.append(dve(lambda e, c=c, n=n, m0=m0: e.tensor_tensor(
                    B[:, 128 * c:128 * (c + n)], SALL[:, 128 * c:128 * (c + n)],
                    DM[:, m0:m0 + n, :].rearrange("p n k -> p (n k)"), ALU.add), t, t_dm, sb3_rel[s % 2]))
            free[0] = free[1] = free[2] = tm[-1]
            w = 128 * len(bl)
            t = dve(lambda e: e.tensor_reduce(st[:, 0:1], B[:, 0:w], AX.X, ALU.max), tm)
            t = dve(lambda e: e.tensor_scalar(st[:, 1:2], st[:, 0:1], -0.125, None, ALU.mult), t)
            t = act(lambda e: e.activation(B[:, 0:w], B[:, 0:w], ACT.Exp, bias=st[:, 1:2], scale=0.125,
                                           accum_out=st[:, 2:3]), t)
            t = dve(lambda e: e.reciprocal(st[:, 3:4], st[:, 2:3]), t)
            soft3[s] = dve(lambda e: e.tensor_scalar(B[:, 0:w], B[:, 0:w], st[:, 3:4], None, ALU.mult), t)

        do_tok = [None, None]

        def d_values(s):
            j, i = s // 4, s % 4
            off = 64 * (j % 2)
            bl = blocks(i)
            B, P = SB3[s % 2], PT3[s % 2]
            n = len(bl)
            for c in range(n):
                t = pe(lambda e, c=c: e.transpose(TALL[:, 128 * c:128 * c + 128], B[:, 128 * c:128 * c + 128], ident),
                       free[3], soft3[s], sig=(c == n - 1))
            sb3_rel[s % 2] = t
            t = act(lambda e: e.activation(P[:, 0:128 * n], TALL[:, 0:128 * n], ACT.Copy), t, pt3_rel[s % 2])
            free[3] = t
            ob = 6 + j // 2
            o = PS[off:off + 64, ob, 128 * i:128 * i + 128]
            for c, (g, kb) in enumerate(bl):
                vc = 64 * (4 * g + j)
                tv = pe(lambda e, c=c, kb=kb, vc=vc: e.matmul(o, DV[:, kb, vc:vc + 64], P[:, 128 * c:128 * c + 128],
                                                              start=(c == 0), stop=(c == n - 1)),
                        t, free[ob] if i == 0 else None, dv_tok[kb], sig=(c == n - 1))
            pt3_rel[s % 2] = tv
            if i == 3 and j % 2:
                m = j // 2
                do_tok[m] = two_parts(OHI[:, m, :], OLO[:, m, :], PS[:, ob, :], tv)
                free[ob] = do_tok[m]

        d_scores(0)
        for s in range(16):
            if s < 15:
                d_scores(s + 1)
            d_values(s)
        free[4] = free[5] = free[3]
        for b in range(8):
            banks.rel[b] = free[b]

        t_arena = [now("pe"), now("dve"), now("act")]
        PZ = sb([128, 2, 16 + S], F32, AR + 40 * KB)
        CNT = sb([128, 4, S], F32, AR + 46 * KB)
        DH = sb([128, 4, S], F32R, AR + 8 * KB)
        DL = sb([128, 4, S], F32R, AR + 16 * KB)
        YH = sb([128, 4, S], F32R, AR + 24 * KB)
        YL = sb([128, 4, S], F32R, AR + 32 * KB)
        t_cnt = dma("cnt", CNT[:, :, :], A["k_cnt"].to_broadcast([128, 4, S]), t_arena)
        t_z = dve(lambda e: e.memset(PZ[:, :, 0:16], 0.0), t_arena)
        d_tok = {}
        pz_rel = [None, None]

        def pz_evac(n, b, t):
            i, tm, rel = take_tmp()
            p0 = act(lambda e: e.activation(tm[:, :], PS[:, b, :], ACT.Copy), t, rel)
            cur = act(lambda e: e.activation(PZ[:, 0, 16:16 + S], PS[:, b, :], ACT.Copy), t, pz_rel, t_arena)
            for step in range(n + 1):
                w = 1 << step
                src, dst = step % 2, 1 - step % 2
                cur = dve(lambda e, w=w, src=src, dst=dst: e.tensor_tensor(
                    PZ[:, dst, 16:16 + S], PZ[:, src, 16:16 + S], PZ[:, src, 16 - w:16 - w + S], ALU.add), cur, t_z,
                    pz_rel)
            fin = (n + 1) % 2
            i2, tm2, rel2 = take_tmp()
            t1 = dve(lambda e: e.tensor_tensor(tm2[:, :], PZ[:, fin, 16:16 + S], CNT[:, n, :], ALU.mult), cur, t_cnt,
                     rel2)
            pz_rel[0] = t1
            t2 = dve(lambda e: e.tensor_tensor(tm2[:, :], tm2[:, :], tm[:, :], ALU.subtract), t1, p0)
            tmps.rel[i] = t2
            d_tok[n] = two_parts(DH[:, n, :], DL[:, n, :], tm2[:, :], t2, t_arena)
            tmps.rel[i2] = d_tok[n]
            return [p0, cur]

        linear("pz", 2, list(four), hx, pz_evac)
        it = use("pw")
        y_tok = {}
        for g in range(4):
            b = banks.take()
            t = mm3(PS[:, b, :], it["hi"][:, g, :], it["lo"][:, g, :], DH[:, g, :], DL[:, g, :], True, True,
                    [it["ready"], d_tok[g], banks.rel[b]], True)
            i, tm, rel = take_tmp()
            t1 = dve(lambda e, g=g, b=b, tm=tm: e.tensor_scalar(tm[:, :], PS[:, b, :], col("pool_scale", g), None,
                                                                ALU.mult), t, rel)
            banks.rel[b] = t1
            y_tok[g] = two_parts(YH[:, g, :], YL[:, g, :], tm[:, :], t1, t_arena)
            tmps.rel[i] = y_tok[g]
        done(it, t)
        t_pool = [now("pe"), now("dve"), now("act")]

        MO = [8, 10, 12, 14, 16, 18, 20, 22, 40, 42, 44, 46, 48, 50, 52, 54]
        MH = [sb([128, S], F32R, AR + MO[j] * KB) for j in range(8)]
        ML = [sb([128, S], F32R, AR + MO[8 + j] * KB) for j in range(8)]
        GA = [sb([128, S], F32, AR + (56 + 2 * n) * KB) for n in range(4)]
        ga_rel = [None] * 4
        m_tok = {}
        for n2 in range(2):
            g_tok, a_tok = {}, {}

            def ga_evac(n, b, t):
                g_tok[n] = act(lambda e: e.activation(GA[n][:, :], PS[:, b, :], ACT.Sigmoid), t, t_pool, ga_rel[n])
                return g_tok[n]

            def ba_evac(n, b, t):
                a_tok[n] = dve(lambda e: e.tensor_tensor(GA[n][:, :], GA[n][:, :], PS[:, b, :], ALU.mult), t, g_tok[n])
                return a_tok[n]

            linear("ga", 2, list(four), hx, ga_evac)
            linear("ba", 1, list(four), lambda k, n: (OHI[:, k, :], OLO[:, k, :], do_tok[k]), ba_evac)
            gp = {}

            def gp_evac(n, b, t):
                i, tm, rel = take_tmp()
                ta = act(lambda e: e.activation(tm[:, :], PS[:, b, :], ACT.Sigmoid), t, rel)
                gp[n] = (i, tm, ta)
                return ta

            def bp_evac(n, b, t, n2=n2):
                j = 4 * n2 + n
                i, tm, ta = gp[n]
                t1 = dve(lambda e: e.tensor_tensor(tm[:, :], tm[:, :], PS[:, b, :], ALU.mult), t, ta)
                t2 = dve(lambda e: e.tensor_tensor(tm[:, :], tm[:, :], GA[n][:, :], ALU.add), t1, a_tok[n])
                ga_rel[n] = t2
                m_tok[j] = two_parts(MH[j][:, :], ML[j][:, :], tm[:, :], t2, t_pool)
                tmps.rel[i] = m_tok[j]
                return t1

            linear("gp", 2, list(four), hx, gp_evac)
            linear("bp", 1, list(four), lambda k, n: (YH[:, k, :], YL[:, k, :], y_tok[k]), bp_evac)
        h_rel[0] = now("pe")
        for n2 in range(2):
            linear("out", 2, list(four), lambda k, n: (MH[k][:, :], ML[k][:, :], m_tok[k]),
                   lambda n, b, t: add_x(4 * n2 + n, b, 1.0, t, None))

        glu(lambda j: col("ffn2_norm", j))

        t_arena = [now("pe"), now("dve"), now("act")]
        OUT = sb([128, 4, D], F32, AR)
        t_r = rstd(D)
        t_o = []
        for j in range(8):
            i, tm, rel = take_tmp()
            t = dve(lambda e, j=j, tm=tm: e.scalar_tensor_tensor(tm[:, :], X[:, j, :], col("final_norm", j), RT[:, :],
                                                                 ALU.mult, ALU.mult), t_r, rel, x_tok[j])
            b = banks.take()
            for t4 in range(4):
                t = pe(lambda e, b=b, t4=t4, tm=tm: e.transpose(PS[:, b, t4 * 128:t4 * 128 + 128],
                                                                tm[:, t4 * 128:t4 * 128 + 128], ident),
                       t, banks.rel[b], sig=(t4 == 3)) or t
            tmps.rel[i] = t
            t = act(lambda e, j=j, b=b: e.activation(OUT[:, :, 128 * j:128 * j + 128],
                                                     PS[:, b, :].rearrange("p (t c) -> p t c", t=4), ACT.Copy), t,
                    t_arena)
            banks.rel[b] = t
            t_o.append(t)
        t_out = dma("out", out.rearrange("b (t p) d -> p (b t) d", p=128), OUT[:, :, :], t_o)
        assert state["split"] == len(plan) and not late

        sems = {s: ctx.enter_context(nc.semaphore(f"s_{s}")) for s in Q.n}
        block = ctx.enter_context(nc.Block())

        @block.sync
        def _(e):
            Q.play("sp", e, sems)
            e.wait_ge(sems[t_out[0]], t_out[1])

        @block.scalar
        def _(e):
            Q.play("act", e, sems)

        @block.vector
        def _(e):
            Q.play("dve", e, sems)

        @block.tensor
        def _(e):
            Q.play("pe", e, sems)


_INS = ['x', 'c', 'positions', 'w_ada', 'b_ada', 'g_mix', 'g_mlp', 'mla_w_dq', 'mla_g_q', 'mla_w_uq', 'mla_w_dkv',
        'mla_g_kv', 'mla_w_ukv', 'mla_w_o', 'swa_w_qkv', 'swa_b_qkv', 'swa_sinks', 'swa_w_o', 'swa_b_o', 'w_ff1',
        'w_ff2', 'g_final', 'ffn1_norm_2', 'ffn1_w1_2', 'ffn1_w3_2', 'ffn1_w2_2', 'mix_norm_2', 'w_in_2',
        'w_branch_attn_2', 'w_branch_pool_2', 'pool_w_2', 'pool_scale_2', 'w_out_2', 'ffn2_norm_2', 'ffn2_w1_2',
        'ffn2_w3_2', 'ffn2_w2_2', 'final_norm_2']


def shape_constants():
    import numpy as np

    f = np.float32
    NEG = f(-2.0e38)
    p = np.arange(128)
    q, k = p[:, None], p[None, :]
    ident = np.eye(128, dtype=f)
    rot = np.zeros((128, 128), f)
    drot = np.zeros((128, 128), f)
    for m in range(128):
        d = m % 64
        rot[m + 32 if d < 32 else m - 32, m] = -1.0 if d < 32 else 1.0
        if d < 8:
            drot[m + 8, m] = -1.0
        elif d < 16:
            drot[m - 8, m] = 1.0
    causal = np.where(k <= q, f(0), NEG).astype(f)
    invf = (f(10000.0) ** (-np.arange(32, dtype=f) / f(32))).astype(f)[p % 32][:, None]
    BIG = f(1.0e37)
    own = np.where(k <= q, q - k, BIG).astype(f)
    prev = np.where(q + 128 - k < 128, q + 128 - k, BIG).astype(f)
    pair = np.concatenate([prev, own], 1)
    first = np.concatenate([own, np.full((128, 128), BIG, f)], 1)
    dist = np.concatenate([first, pair, pair, pair], 1)

    def mask(ok):
        return np.where(ok, f(0), NEG).astype(f)

    m4, m16 = (q - k) % 4 == 0, (q - k) % 16 == 0
    low = k <= q
    dil = np.stack([mask(k >= q), mask(low)] + [mask(m4)] * 3 + [mask(m4 & low)] + [mask(m16)] * 3
                   + [mask(m16 & low)], 1)
    inv = (f(500000.0) ** (-np.arange(0, 16, 2, dtype=f) / f(16))).astype(f)
    ang = (np.arange(512, dtype=f)[None, :] * inv[:, None]).astype(f)
    dcos, dsin = np.ones((128, 512), f), np.zeros((128, 512), f)
    for m in range(128):
        if m % 64 < 16:
            dcos[m] = np.cos(ang[m % 8])
            dsin[m] = np.sin(ang[m % 8])
    cnt = np.stack([f(1) / np.minimum(np.arange(1, 513), w).astype(f) for w in (2, 4, 8, 16)])[None]
    return {"k_const": np.stack([ident, np.ones((128, 128), f), rot], 1), "k_causal": causal, "k_invf": invf,
            "k_dist": dist, "k_dil": dil, "k_dcos": dcos, "k_dsin": dsin, "k_drot": drot, "k_cnt": cnt.astype(f)}


def kernel(**inputs):
    import numpy as _np
    import concourse.bacc as _bacc
    from concourse import mybir as _mybir
    from concourse.bass_utils import run_bass_kernel_spmd as _run

    nc = _bacc.Bacc("TRN2", target_bir_lowering=False, num_devices=1)
    arrays, aps = {}, {}
    given = {name: _np.ascontiguousarray(inputs[name]) for name in _INS}
    for name, a in {**given, **shape_constants()}.items():
        a = _np.ascontiguousarray(a)
        arrays[f"in_{name}_dram"] = a
        aps[name] = nc.dram_tensor(f"in_{name}_dram", a.shape, _mybir.dt.from_np(a.dtype), kind="ExternalInput").ap()
    out = nc.dram_tensor("out_0_dram", (1, 512, 1024), _mybir.dt.from_np(_np.dtype("float32")),
                         kind="ExternalOutput").ap()
    bass_two_blocks(nc, aps, out)
    r = _run(nc, [arrays], core_ids=[0])
    return r.results[0]["out_0_dram"]
```

```python
import concourse.bass as bass
from concourse import mybir
from contextlib import ExitStack

S = 512
D = 1024
F32 = mybir.dt.float32
F32R = mybir.dt.float32r
I32 = mybir.dt.int32
ALU = mybir.AluOpType
ACT = mybir.ActivationFunctionType
AX = mybir.AxisListType
EPS = 1e-6
KB = 1024
NRAW = 3
NW = 3
NTMP = 5
FULL = slice(0, 512)
HALF = (slice(0, 256), slice(256, 512))


def flat(w):
    if w is None:
        return []
    if isinstance(w, tuple) and w and isinstance(w[0], str):
        return [w]
    return [t for x in w for t in flat(x)]


class Queues:

    def __init__(self):
        self.q = {e: [] for e in ("sp", "act", "dve", "pool", "pe")}
        self.n = {}

    def _add(self, eng, sem, by, fn, waits):
        tok = None
        if sem is not None:
            self.n[sem] = self.n.get(sem, 0) + by
            tok = (sem, self.n[sem])
        self.q[eng].append((flat(waits), fn, sem, by))
        return tok

    def act(self, fn, *waits):
        return self._add("act", "act", 1, fn, waits)

    def dve(self, fn, *waits):
        return self._add("dve", "dve", 1, fn, waits)

    def pe(self, fn, *waits, sig=False):
        return self._add("pe", "pe" if sig else None, 1, fn, waits)

    def pool(self, fn, *waits):
        return self._add("pool", "pool", 1, fn, waits)

    def dma(self, sem, out, in_, *waits, eng="sp"):
        return self._add(eng, sem, 16, lambda e: e.dma_start(out, in_), waits)

    def now(self, *engs):
        return [(e, self.n[e]) for e in engs]

    def play(self, eng, engine, sems):
        seen = {}
        for waits, fn, sem, by in self.q[eng]:
            for s, v in waits:
                if seen.get(s, 0) < v:
                    engine.wait_ge(sems[s], v)
                    seen[s] = v
            ins = fn(engine)
            if sem is not None:
                ins.then_inc(sems[sem], by)


class Ring:

    def __init__(self, n):
        self.ids, self.at, self.rel, self.busy = list(range(n)), 0, [None] * n, set()

    def only(self, *ids):
        self.ids, self.at = list(ids), 0

    def next(self):
        return self.ids[self.at % len(self.ids)]

    def take(self):
        for _ in self.ids:
            i = self.next()
            self.at += 1
            if i not in self.busy:
                return i
        assert False, "no slot is free"


def bass_two_blocks(nc, A, out):
    Q = Queues()
    act, dve, pe, pool, dma, now = Q.act, Q.dve, Q.pe, Q.pool, Q.dma, Q.now

    ctx = ExitStack()
    with ctx:
        base = -(-nc.sbuf_base // 64) * 64
        at = [base]

        def place(nbytes):
            o = at[0]
            at[0] += nbytes
            return o

        names = [0]

        def sb(shape, dt, offset):
            names[0] += 1
            return nc.alloc_sbuf_tensor_at(f"t{names[0]}", shape, dt, offset=offset)

        o_raw = place(NRAW * 8 * KB)
        o_hi = place(NW * 8 * KB)
        o_lo = place(NW * 8 * KB)
        o_x = place(16 * KB)
        o_h = place(32 * KB)
        AR = place(66 * KB)
        o_tmp = place(NTMP * 2 * KB)
        o_r = place(2 * KB)
        o_ssq = place(2 * KB)
        o_acc = place(4 * KB)
        o_c = place(4 * 512)
        o_v = place(216 * 4)
        o_mod = place(2 * 48 * 4)
        o_gs = place(4 * 8 * 4)
        o_st = place(72 * 4)
        assert at[0] <= nc.sbuf_usable_end, at[0]

        RAW = [sb([128, 2048], F32, o_raw + i * 8 * KB) for i in range(NRAW)]
        WHI = [sb([128, 2048], F32R, o_hi + i * 8 * KB) for i in range(NW)]
        WLO = [sb([128, 2048], F32R, o_lo + i * 8 * KB) for i in range(NW)]
        X = sb([128, 8, S], F32, o_x)
        HHI = sb([128, 8, S], F32R, o_h)
        HLO = sb([128, 8, S], F32R, o_h + 16 * KB)
        TMP = [sb([128, S], F32, o_tmp + i * 2 * KB) for i in range(NTMP)]
        TMPR = [sb([128, S], F32R, o_tmp + i * 2 * KB) for i in range(NTMP)]
        RT = sb([128, S], F32, o_r)
        SSQ = sb([128, S], F32, o_ssq)
        ACC = sb([128, D], F32, o_acc)
        ACCR = sb([128, D], F32R, o_acc)
        CONST = sb([128, 3, 128], F32, o_c)
        ident, causal, rot = CONST[:, 0, :], CONST[:, 1, :], CONST[:, 2, :]
        ONESR = sb([128, 128], F32R, o_c + 3 * 512)
        ones = ONESR[:, :].bitcast(F32)
        VEC = sb([128, 115 + 96 + 1], F32, o_v)
        MOD = sb([128, 2, 48], F32, o_mod)
        GS = sb([128, 4, 8], F32, o_gs)
        ST = sb([128, 64], F32, o_st)

        PS = ctx.enter_context(nc.psum_tensor("PS", [128, 8, 512], F32))

        tmps = Ring(NTMP)
        banks = Ring(8)

        XIN = sb([128, 4, D], F32, AR)
        V1 = sb([115, 128], F32, AR + 16 * KB)
        V2 = sb([96, 128], F32, AR + 17 * KB)
        V0 = sb([8, 128], F32, AR + 18 * KB)
        SC = sb([128, 8], F32, AR + 19 * KB)
        CC = sb([128, 8], F32, AR + 19 * KB + 64)
        POS = sb([128, S], I32, AR + 20 * KB)
        PA = sb([128, S], F32, AR + 22 * KB)
        PB = sb([128, S], F32, AR + 24 * KB)
        PC = sb([128, S], F32, AR + 26 * KB)
        PD = sb([128, S], F32, AR + 28 * KB)
        COS = sb([128, S], F32, AR + 62 * KB)
        SIN = sb([128, S], F32, AR + 64 * KB)

        t_c = dma("c", V0[:, :], A["c"].rearrange("b (j p) -> (b j) p", p=128))
        t_const = dma("const", CONST[:, :, :], A["k_const"])

        rows = {}
        r = 0
        for name, ap, k in (
            ("c", None, 8),
            ("g_mix", A["g_mix"].rearrange("l (j p) -> (l j) p", p=128), 16),
            ("g_mlp", A["g_mlp"].rearrange("l (j p) -> (l j) p", p=128), 16),
            ("g_q", A["mla_g_q"].rearrange("l (j p) -> (l j) p", p=128), 3),
            ("g_kv", A["mla_g_kv"].rearrange("l (j p) -> (l j) p", p=128), 2),
            ("g_final", A["g_final"].rearrange("(j p) -> j p", p=128), 8),
            ("ffn1_norm", A["ffn1_norm_2"].rearrange("l (j p) -> (l j) p", p=128), 8),
            ("mix_norm", A["mix_norm_2"].rearrange("l (j p) -> (l j) p", p=128), 8),
            ("ffn2_norm", A["ffn2_norm_2"].rearrange("l (j p) -> (l j) p", p=128), 8),
            ("final_norm", A["final_norm_2"].rearrange("(j p) -> j p", p=128), 8),
            ("pool_scale", A["pool_scale_2"].rearrange("l (j p) -> (l j) p", p=128), 4),
            ("bq", A["swa_b_qkv"][:, 0:1024].rearrange("l (h d) -> (l h) d", d=64), 16),
            ("bk", A["swa_b_qkv"][:, 1024:1280].rearrange("l (j p) -> (l j) p", p=128), 2),
            ("b_o", A["swa_b_o"].rearrange("l (j p) -> (l j) p", p=128), 8),
        ):
            rows[name] = r
            if name == "c":
                ap = A["c"].rearrange("b (j p) -> (b j) p", p=128)
            if name == "bq":
                dma("vec", V1[r:r + k, 0:64], ap, eng="pool")
                dma("vec", V1[r:r + k, 64:128], ap, eng="pool")
            else:
                dma("vec", V1[r:r + k, :], ap, eng="pool")
            r += k
        assert r == 115
        dma("vec", V2[:, :], A["b_ada"].rearrange("l (j p) -> (l j) p", p=128), eng="pool")
        dma("vec", VEC[:, 211:212], A["k_invf"], eng="pool")
        t_vec = dma("vec", POS[:, :], A["positions"].to_broadcast([128, S]), eng="pool")

        def col(name, j=0, k=1):
            return VEC[:, rows[name] + j:rows[name] + j + k]

        def bada(l, v):
            return VEC[:, 115 + l * 48 + v * 8:115 + l * 48 + v * 8 + 8]

        invf = VEC[:, 211:212]
        SILUC = sb([128, 8], F32, o_st + 64 * 4)

        b = banks.take()
        t = pe(lambda e, b=b: e.transpose(PS[:, b, 0:8], V0[:, :], ident[0:8, 0:8]), t_c, t_const, sig=True)
        t_e = act(lambda e, b=b: e.activation(SC[:, :], PS[:, b, 0:8], ACT.Exp, scale=-1.0), t)
        t = dve(lambda e: e.tensor_scalar(CC[:, :], SC[:, :], 1.0, None, ALU.add), t_e)
        t = dve(lambda e: e.reciprocal(SC[:, :], CC[:, :]), t)
        t_silu = dve(lambda e, b=b: e.tensor_tensor(SILUC[:, :], PS[:, b, 0:8], SC[:, :], ALU.mult), t)
        banks.rel[b] = [t_e, t_silu]
        t = dve(lambda e: e.memset(TMP[0][:, 0:128], 1.0))
        t_ones = dve(lambda e: e.tensor_copy(ONESR[:, :], TMP[0][:, 0:128]), t)
        tmps.rel[0] = t_ones

        raw_ring = Ring(NRAW)
        w_ring = Ring(NW)
        plan = []
        state = {"loaded": 0, "split": 0, "used": 0, "reach": 4}
        late = []
        t_cols = []
        mod_tok = {}
        mod_used = {}
        acc_rel = [None]

        def weight(name, ap, kt, ncol, parts=None):
            plan.append(dict(kind="w", name=name, ap=ap, kt=kt, nc=ncol, parts=parts))

        def ada(l, v):
            w = A["w_ada"][l].rearrange("(k p) n -> p k n", p=128)
            for u in range(4):
                plan.append(dict(kind="a", l=l, v=v, u=u, kt=2, nc=D,
                                 ap=w[:, 2 * u:2 * u + 2, v * D:(v + 1) * D]))

        def load():
            it = plan[state["loaded"]]
            state["loaded"] += 1
            i = raw_ring.take()
            it["raw"] = i
            n = it["kt"] * it["nc"]
            it["rawv"] = RAW[i][:, 0:n].rearrange("p (k n) -> p k n", k=it["kt"])
            ap, dst = it["ap"], it["rawv"]
            pieces = [(dst, ap)]
            if it.get("split3"):
                pieces = [(dst[:, :, 128 * g:128 * g + 128], ap[:, :, g, :]) for g in range(3)]
            for dst, ap in pieces:
                it["landed"] = dma(f"raw{i}", dst, ap, raw_ring.rel[i])

        def take_tmp():
            for _ in range(NTMP):
                i = tmps.take()
                if tmps.rel[i] != "held":
                    break
            rel, tmps.rel[i] = tmps.rel[i], "held"
            assert rel != "held"
            return i, TMP[i], rel

        def begin_mod(l, v, t_acc):
            held = []
            for hf in range(2):
                cs = slice(512 * hf, 512 * hf + 512)
                i, _, rel = take_tmp()
                th = act(lambda e, i=i, cs=cs: e.activation(TMPR[i][:, :], ACC[:, cs], ACT.Copy), t_acc, rel)
                tl = dve(lambda e, i=i, cs=cs: e.tensor_tensor(ACCR[:, cs], ACC[:, cs], TMPR[i][:, :].bitcast(F32),
                                                               ALU.subtract), th)
                held.append((i, cs, th, tl))
            late.append((state["used"] + 1, lambda: end_mod(l, v, held)))

        def end_mod(l, v, held):
            dst = MOD[:, l, v * 8:v * 8 + 8]
            freed = []
            for hf, (i, cs, th, tl) in enumerate(held):
                b = banks.take()
                pe(lambda e, i=i, b=b: e.matmul(PS[:, b, :], ONESR[:, :], TMPR[i][:, :], start=True, stop=False),
                   th, t_ones, banks.rel[b])
                t = pe(lambda e, b=b, cs=cs: e.matmul(PS[:, b, :], ONESR[:, :], ACCR[:, cs], start=False, stop=True),
                       tl, sig=True)
                tmps.rel[i] = t
                freed.append(t)
                sq = PS[:, b, :].rearrange("p (j c) -> p j c", c=128)
                t = dve(lambda e, sq=sq: e.tensor_tensor(sq, sq, ident.unsqueeze(1).to_broadcast([128, 4, 128]),
                                                         ALU.mult), t)
                t = dve(lambda e, sq=sq, hf=hf: e.tensor_reduce(dst[:, 4 * hf:4 * hf + 4], sq, AX.X, ALU.add), t)
                banks.rel[b] = t
            acc_rel[0] = freed
            t = dve(lambda e: e.tensor_tensor(dst, dst, bada(l, v), ALU.add), t, t_cols)
            if v in (1, 4):
                which = 2 * l + (v == 4)
                g = col("g_mix" if v == 1 else "g_mlp", 8 * l, 8)
                t = dve(lambda e: e.scalar_tensor_tensor(GS[:, which, :], dst, 1.0, g, ALU.add, ALU.mult), t, t_cols)
            mod_tok[(l, v)] = t

        def settle(everything=False):
            while late and (everything or late[0][0] <= state["used"]):
                late.pop(0)[1]()

        def split():
            it = plan[state["split"]]
            state["split"] += 1
            raw = it["rawv"]
            if it["kind"] == "a":
                t = it.get("prev")
                for kk in range(2):
                    k = 2 * it["u"] + kk
                    c = SILUC[:, k:k + 1]
                    if k == 0:
                        settle(True)
                        t = dve(lambda e, kk=kk, c=c: e.tensor_scalar(ACC[:, :], raw[:, kk, :], c, None, ALU.mult),
                                it["landed"], acc_rel[0], t_silu)
                    else:
                        t = dve(lambda e, kk=kk, c=c: e.scalar_tensor_tensor(ACC[:, :], raw[:, kk, :], c, ACC[:, :],
                                                                             ALU.mult, ALU.add),
                                it["landed"], state["acc"])
                    state["acc"] = t
                raw_ring.rel[it["raw"]] = t
                if it["u"] == 3:
                    late.append((state["used"] + 2, lambda l=it["l"], v=it["v"], t=t: begin_mod(l, v, t)))
            else:
                i = w_ring.take()
                it["slot"] = i
                width = it.get("wide", it["nc"])
                parts = it["parts"] or [(lambda w: w, lambda w: w)]
                wd = it["wd"] = it["kt"] * width
                hi = WHI[i][:, 0:wd].rearrange("p (k n) -> p k n", k=it["kt"])
                lo = WLO[i][:, 0:wd].rearrange("p (k n) -> p k n", k=it["kt"])
                it["hi"], it["lo"] = hi, lo
                th, tl = [], []
                for dst, src in parts:
                    th.append(act(lambda e, d=dst(hi), s=src(raw): e.activation(d, s, ACT.Copy),
                                  it["landed"], w_ring.rel[i]))
                for (dst, src), t in zip(parts, th):
                    tl.append(dve(lambda e, d=dst(lo), h=dst(hi), s=src(raw):
                                  e.tensor_tensor(d, s, h.bitcast(F32), ALU.subtract), it["landed"], t))
                it["ready"] = [th[-1], tl[-1]]
                raw_ring.rel[it["raw"]] = [th[-1], tl[-1]]
                w_ring.rel[i] = "held"
            if state["loaded"] < len(plan):
                load()

        def use(name):
            k = state["used"]
            while plan[k]["kind"] != "w":
                k += 1
            it = plan[k]
            assert it["name"] == name, (it["name"], name)
            state["used"] = k + 1
            while state["split"] < len(plan):
                nxt = plan[state["split"]]
                if nxt["kind"] == "w" and w_ring.rel[w_ring.next()] == "held":
                    break
                if nxt["kind"] == "a" and state["split"] > k + state["reach"]:
                    break
                split()
            assert "ready" in it
            return it

        def ahead():
            if state["split"] < len(plan):
                if plan[state["split"]]["kind"] == "a" or w_ring.rel[w_ring.next()] != "held":
                    split()

        def done(it, t):
            w_ring.rel[it["slot"]] = t
            settle()

        wt = lambda ap: ap.rearrange("(k p) n -> p k n", p=128)
        w_dq, w_dkv = wt(A["mla_w_dq"][0]), wt(A["mla_w_dkv"][0])
        w_uq, w_ukv, w_mo = wt(A["mla_w_uq"][0]), wt(A["mla_w_ukv"][0]), wt(A["mla_w_o"][0])
        w_qkv, w_so = wt(A["swa_w_qkv"][0]), wt(A["swa_w_o"][0])
        w_in, w_out = wt(A["w_in_2"][0]), wt(A["w_out_2"][0])
        w_ba, w_bp = wt(A["w_branch_attn_2"][0]), wt(A["w_branch_pool_2"][0])
        w_pool = A["pool_w_2"][0].rearrange("g c d -> c g d")

        ada(0, 1)
        ada(0, 0)
        for a in range(2):
            weight("dq", w_dq[:, 4 * a:4 * a + 4, :], 4, 384)
        ada(0, 2)
        dkv_parts = [(lambda w: w[:, :, 0:320], lambda w: w), (lambda w: w[:, :, 320:384], lambda w: w[:, :, 256:320])]
        for a in range(2):
            weight("dkv", w_dkv[:, 4 * a:4 * a + 4, :], 4, 320, dkv_parts)
            plan[-1]["wide"] = 384

        def uq_nope(w):
            return w[:, :, 0:256].rearrange("p k (h c) -> p k h c", h=2)

        def uq_rope(w):
            return w[:, :, 256:384].rearrange("p k (h c) -> p k h c", h=2)

        uq_parts = [(uq_nope, lambda w: w.rearrange("p k (h c) -> p k h c", h=2)[:, :, :, 0:128]),
                    (uq_rope, lambda w: w.rearrange("p k (h c) -> p k h c", h=2)[:, :, :, 128:192])]

        def uq_plan(a):
            weight("uq", w_uq[:, :, 384 * a:384 * a + 384], 3, 384, uq_parts)

        def square(name, w, cols=2, per=512, ks=(4, 4), k0=0):
            for n in range(cols):
                k = k0
                for kt in ks:
                    weight(name, w[:, k:k + kt, n * per:(n + 1) * per], kt, per)
                    k += kt

        uq_plan(0)
        uq_plan(1)
        for a in range(2):
            weight("ukv", w_ukv[:, :, 1024 * a:1024 * a + 1024], 2, 1024)
        uq_plan(2)
        uq_plan(3)
        square("mo", w_mo, cols=1, ks=(4,))
        ada(0, 4)
        square("mo", w_mo, cols=1, ks=(4,), k0=4)
        ada(0, 3)
        square("mo", w_mo[:, :, 512:1024], cols=1)
        pend = [(0, 5), (1, 1), (1, 0), (1, 2), (1, 4), (1, 3), (1, 5)]

        def ff_plan(l, extra):
            w1, w2 = wt(A["w_ff1"][l]), wt(A["w_ff2"][l])

            def up(q):
                square(f"up{l}", w1[:, :, 1024 * q:1024 * q + 1024])

            def down(q):
                square(f"down{l}", w2, k0=8 * q)

            up(0)
            for q in range(4):
                if extra:
                    ada(*extra.pop(0))
                if q < 3:
                    up(q + 1)
                if extra:
                    ada(*extra.pop(0))
                down(q)

        ff_plan(0, pend)
        assert not pend

        for n in (0, 2, 1):
            for a in range(2):
                weight("qkv", w_qkv[:, 4 * a:4 * a + 4, 512 * n:512 * n + 512], 4, 512)
        square("so", w_so)
        ff_plan(1, [])

        def glu_plan(w1, w3, w2):
            w1, w3, w2 = wt(w1), wt(w3), wt(w2)

            def up(blk):
                for g in ((0, 4), (4, 8), (8, 11))[blk:blk + 1]:
                    for c in range(*g):
                        weight("w1", w1[:, :, 256 * c:256 * c + 256], 8, 256)
                        weight("w3", w3[:, :, 256 * c:256 * c + 256], 8, 256)

            def down(blk):
                square("w2", w2, ks=((4, 4), (4, 4), (3, 3))[blk], k0=8 * blk)

            up(0)
            for blk in range(3):
                if blk < 2:
                    up(blk + 1)
                down(blk)

        glu_plan(A["ffn1_w1_2"][0], A["ffn1_w3_2"][0], A["ffn1_w2_2"][0])

        def qk_plan(a):
            for c in (0, 768):
                w = w_in[:, :, c:c + 768].rearrange("p k (g a c) -> p k g a c", a=2, c=128)
                for u in range(2):
                    weight("qk", w[:, 4 * u:4 * u + 4, :, a, :], 4, 384)
                    plan[-1]["split3"] = True

        qk_plan(0)
        square("v", w_in[:, :, 1536:2048], cols=1)
        weight("v2", w_in[:, :, 2048:2304], 8, 256)
        qk_plan(1)
        square("pz", w_in[:, :, 2304:2816], cols=1)
        weight("pw", w_pool, 4, 128)
        for n in range(2):
            square("ga", w_in[:, :, 2816 + 512 * n:3328 + 512 * n], cols=1)
            weight("ba", w_ba[:, :, 512 * n:512 * n + 512], 2, 512)
            square("gp", w_in[:, :, 3840 + 512 * n:4352 + 512 * n], cols=1)
            weight("bp", w_bp[:, :, 512 * n:512 * n + 512], 4, 512)
        square("out", w_out)
        glu_plan(A["ffn2_w1_2"][0], A["ffn2_w3_2"][0], A["ffn2_w2_2"][0])

        for _ in range(NRAW):
            load()

        later = []

        def flush():
            while later:
                later.pop(0)()

        def hs(cs):
            return [i for i in range(2) if cs == FULL or cs == HALF[i]]

        def mm3(o, wh, wl, xh, xl, first, last, waits, sig):
            pe(lambda e: e.matmul(o, wh, xh, start=first, stop=False), waits)
            pe(lambda e: e.matmul(o, wh, xl, start=False, stop=False))
            return pe(lambda e: e.matmul(o, wl, xh, start=False, stop=last), sig=sig)

        def linear(name, nunits, outs, xs, evac, swap=False, halves=False, mid=None, frees_h=False):
            its = []
            parts = HALF if halves else (FULL,)
            for hf, cs in enumerate(parts):
                bk = [banks.take() for _ in outs]
                banks.busy.update(bk)
                ends = []
                k0 = 0
                for u in range(nunits):
                    if hf == 0:
                        its.append(use(name))
                    it = its[u]
                    last_unit = u == nunits - 1
                    for n, (c, w) in enumerate(outs):
                        o = PS[:, bk[n], 0:w] if swap else PS[:, bk[n], cs]
                        for k in range(it["kt"]):
                            xh, xl, tx = xs(k0 + k, n, cs)
                            wh, wl = it["hi"][:, k, c:c + w], it["lo"][:, k, c:c + w]
                            end = k == it["kt"] - 1
                            waits = [it["ready"], tx, banks.rel[bk[n]] if u == 0 and k == 0 else None]
                            sig = end and (last_unit or n == len(outs) - 1)
                            first, last = u == 0 and k == 0, last_unit and end
                            if swap:
                                t = mm3(o, xh, xl, wh, wl, first, last, waits, sig)
                            else:
                                t = mm3(o, wh, wl, xh, xl, first, last, waits, sig)
                        if last_unit:
                            ends.append((o, t))
                        if mid and (hf, u, n) in mid:
                            mid[(hf, u, n)]()
                        if n == 0:
                            flush()
                        if last_unit and n == len(outs) - 1 and frees_h:
                            for i in hs(cs):
                                h_rel[i] = t
                    k0 += it["kt"]
                    if hf == len(parts) - 1:
                        done(it, ends[-1][1] if last_unit else t)
                banks.busy.difference_update(bk)
                for n, (o, t) in enumerate(ends):
                    banks.rel[bk[n]] = evac(n, o, t, cs)

        x_tok = [[None, None] for _ in range(8)]
        h_tok = [[None, None] for _ in range(8)]
        h_rel = [None, None]
        ssq_rel, ssq_t = [None, None], [None, None]
        ssq2_rel, ssq2_t = [None, None], [None, None]
        r_rel = [None, None]
        SSQ2 = sb([128, S], F32, AR + 64 * KB)

        def x_at(j, cs):
            return [x_tok[j][i] for i in hs(cs)]

        def sumsq(j, src, t, cs=FULL, acc=SSQ, acc_t=ssq_t, rel_t=ssq_rel, scale=1.0):
            if j == 0:
                new = act(lambda e: e.activation(acc[:, cs], src, ACT.Square, scale=scale), t,
                          [rel_t[i] for i in hs(cs)])
            else:
                i, tm, rel = take_tmp()
                ts = act(lambda e: e.activation(tm[:, cs], src, ACT.Square, scale=scale), t, rel)
                new = dve(lambda e: e.tensor_tensor(acc[:, cs], acc[:, cs], tm[:, cs], ALU.add), ts,
                          [acc_t[i] for i in hs(cs)])
                tmps.rel[i] = new
            for i in hs(cs):
                acc_t[i] = new

        def rsqrt(src, t, n, dst, cs, after):
            i, tm, rel = take_tmp()
            t = dve(lambda e: e.tensor_scalar(tm[:, cs], src, 1.0 / n, EPS, ALU.mult, ALU.add), t, rel)
            t_read = t
            t = act(lambda e: e.activation(tm[:, cs], tm[:, cs], ACT.Sqrt), t)
            t = dve(lambda e: e.reciprocal(dst[:, cs], tm[:, cs]), t, after)
            tmps.rel[i] = t
            return t_read, t

        def rstd(n, cs=FULL):
            b = banks.take()
            t = pe(lambda e: e.matmul(PS[:, b, cs], ones, SSQ[:, cs], start=True, stop=True),
                   [ssq_t[i] for i in hs(cs)], t_ones, banks.rel[b], sig=True)
            for i in hs(cs):
                ssq_rel[i] = t
            banks.rel[b], t = rsqrt(PS[:, b, cs], t, n, RT, cs, [r_rel[i] for i in hs(cs)])
            return t

        def normed(cs, gain, shift, t_r, t_mod, R=RT, rel=r_rel):
            held = {}
            after = [h_rel[i] for i in hs(cs)]
            for j in range(9):
                if j < 8:
                    i, tm, free = take_tmp()
                    t = dve(lambda e, j=j, tm=tm: e.scalar_tensor_tensor(tm[:, cs], X[:, j, cs], gain(j), R[:, cs],
                                                                         ALU.mult, ALU.mult), free, t_r, x_at(j, cs),
                            t_mod)
                    if shift is None:
                        th = act(lambda e, j=j, tm=tm: e.activation(HHI[:, j, cs], tm[:, cs], ACT.Copy), t, after)
                    else:
                        th = act(lambda e, j=j, tm=tm: e.activation(HHI[:, j, cs], tm[:, cs], ACT.Identity,
                                                                    bias=shift(j)), t, after, t_mod)
                    held[j] = (i, tm, t, th)
                    for i in hs(cs):
                        rel[i] = t
                if j >= 1:
                    p = j - 1
                    i, tm, t, th = held.pop(p)
                    if shift is None:
                        tl = dve(lambda e, p=p, tm=tm: e.tensor_tensor(HLO[:, p, cs], tm[:, cs],
                                                                       HHI[:, p, cs].bitcast(F32), ALU.subtract),
                                 t, th, after)
                    else:
                        tl = dve(lambda e, p=p, tm=tm: e.scalar_tensor_tensor(HLO[:, p, cs], tm[:, cs], shift(p),
                                                                              HHI[:, p, cs].bitcast(F32), ALU.add,
                                                                              ALU.subtract), t, th, after)
                    tmps.rel[i] = [th, tl]
                    for i in hs(cs):
                        h_tok[p][i] = [th, tl]

        def modulation(l, v):
            while not ((l, v) in mod_tok and (l, v + 1) in mod_tok):
                if late:
                    late.pop(0)[1]()
                else:
                    split()
            return [mod_tok[(l, v)], mod_tok[(l, v + 1)]]

        def plain_norm(name):
            return lambda hf: normed(HALF[hf], lambda j: col(name, j), None, rstd(D, HALF[hf]), None)

        def mod_norm(l, part):
            v = 3 * part
            t_mod = modulation(l, v)
            return lambda hf: normed(HALF[hf], lambda j: GS[:, 2 * l + part, j:j + 1],
                                     lambda j: MOD[:, l, 8 * v + j:8 * v + j + 1], rstd(D, HALF[hf]), t_mod)

        def hx(k, n, cs):
            return HHI[:, k, cs], HLO[:, k, cs], [h_tok[k][i] for i in hs(cs)]

        def hx_tok(k, n, cs):
            ts = slice(n * 128, n * 128 + 128)
            return HHI[:, k, ts], HLO[:, k, ts], h_tok[k][n // 2]

        def two_parts(hi, lo, src, t, *after):
            th = act(lambda e: e.activation(hi, src, ACT.Copy), t, after)
            tl = dve(lambda e: e.tensor_tensor(lo, src, hi.bitcast(F32), ALU.subtract), t, th, after)
            return [th, tl]

        def add_x(j, o, scale, t, t_scale, cs, stats=True):
            t = dve(lambda e: e.scalar_tensor_tensor(X[:, j, cs], o, scale, X[:, j, cs], ALU.mult, ALU.add),
                    t, x_at(j, cs), t_scale)
            for i in hs(cs):
                x_tok[j][i] = t
            if stats:
                sumsq(j, X[:, j, cs], t, cs)
            return t

        four = [(0, 128), (128, 128), (256, 128), (384, 128)]
        three = four[:3]

        def closing(norm):
            return dict(halves=True, mid={(1, 0, 1): lambda: norm(0)})

        def opening(norm):
            return dict(halves=True, mid={(0, 0, 1): lambda: norm(1)})

        def rotated(o, t, cosv, sinv, rotm, t_tab, then, cs=FULL):
            i, tm, rel = take_tmp()
            ta = act(lambda e: e.activation(tm[:, cs], o, ACT.Copy), t, rel)

            def rest():
                b2 = banks.take()
                tp = pe(lambda e: e.matmul(PS[:, b2, cs], rotm, tm[:, cs], start=True, stop=True), ta, banks.rel[b2],
                        t_tab, sig=True)
                i2, tm2, rel2 = take_tmp()
                t2 = dve(lambda e: e.tensor_tensor(tm2[:, cs], PS[:, b2, cs], sinv, ALU.mult), tp, rel2, t_tab)
                banks.rel[b2] = t2
                t1 = dve(lambda e: e.tensor_tensor(tm[:, cs], tm[:, cs], cosv, ALU.mult), ta, tp, t_tab)
                t3 = dve(lambda e: e.tensor_tensor(tm[:, cs], tm[:, cs], tm2[:, cs], ALU.add), t1, t2)
                tmps.rel[i2] = t3
                tmps.rel[i] = then(tm[:, cs], t3, cs)

            later.append(rest)
            return ta

        def stacked(dst, src, e_half, t, *after):
            a, b = slice(64 * e_half, 64 * e_half + 64), slice(64 - 64 * e_half, 128 - 64 * e_half)
            th = act(lambda e: e.activation(dst[a, :], src[a, :], ACT.Copy), t, after)
            tl = dve(lambda e: e.tensor_tensor(dst[b, :], src[a, :], dst[a, :].bitcast(F32), ALU.subtract), t, th,
                     after)
            return [th, tl]

        def doubled(hi, lo, src, e_half, t, *after):
            a = slice(64 * e_half, 64 * e_half + 64)
            out = []
            for b in (slice(0, 64), slice(64, 128)):
                out.append(act(lambda e, b=b: e.activation(hi[b, :], src[a, :], ACT.Copy), t, after))
            for b in (slice(0, 64), slice(64, 128)):
                out.append(dve(lambda e, b=b: e.tensor_tensor(lo[b, :], src[a, :], hi[a, :].bitcast(F32),
                                                              ALU.subtract), t, out[:2], after))
            return out

        def masked_max(P, src, mask, st, t, *waits, first=-3.0e38):
            return dve(lambda e: e.tensor_tensor_reduce(out=P, in0=src, in1=mask, scale=1.0, scalar=first, op0=ALU.add,
                                                        op1=ALU.max, accum_out=st), t, waits)

        t_x = dma("x", XIN[:, :, :], A["x"].rearrange("b (t p) d -> p (b t) d", p=128))
        for _ in range(4):
            split()
        for j in range(8):
            b = banks.take()
            for t4 in range(4):
                t = pe(lambda e, j=j, b=b, t4=t4: e.transpose(PS[:, b, t4 * 128:(t4 + 1) * 128],
                                                              XIN[:, t4, j * 128:(j + 1) * 128], ident),
                       t_x, t_const, banks.rel[b] if t4 == 0 else None, sig=(t4 == 3))
            t = act(lambda e, j=j, b=b: e.activation(X[:, j, :], PS[:, b, :], ACT.Copy), t)
            banks.rel[b] = t
            x_tok[j] = [t, t]
            sumsq(j, X[:, j, :], t)
        b = banks.take()
        pe(lambda e, b=b: e.transpose(PS[:, b, 0:115], V1[:, :], ident[0:115, 0:115]), t_vec, t_const, banks.rel[b])
        t = pe(lambda e, b=b: e.transpose(PS[:, b, 128:224], V2[:, :], ident[0:96, 0:96]), sig=True)
        t_cols.append(dve(lambda e, b=b: e.tensor_copy(VEC[:, 0:115], PS[:, b, 0:115]), t))
        t_cols.append(dve(lambda e, b=b: e.tensor_copy(VEC[:, 115:211], PS[:, b, 128:224]), t))
        banks.rel[b] = t_cols[1]

        TWO_PI = 6.283185307179586
        C1, C2 = 6.28125, 0.0019350051879882812
        C3 = TWO_PI - C1 - C2
        MAGIC = 12582912.0
        t = dve(lambda e: e.tensor_copy(PA[:, :], POS[:, :]), t_vec)
        t_ang = dve(lambda e: e.tensor_scalar(PB[:, :], PA[:, :], invf, None, ALU.mult), t)
        t_tab = []
        for dst, quarter in ((SIN, 0.0), (COS, 0.25)):
            t = dve(lambda e, quarter=quarter: e.tensor_scalar(PC[:, :], PB[:, :], 1.0 / TWO_PI, quarter, ALU.mult,
                                                               ALU.add), t_ang, t_tab)
            t = dve(lambda e: e.tensor_scalar(PD[:, :], PC[:, :], MAGIC, None, ALU.add), t)
            t = dve(lambda e: e.tensor_scalar(PC[:, :], PD[:, :], MAGIC, None, ALU.subtract), t)
            t = dve(lambda e: e.scalar_tensor_tensor(PD[:, :], PC[:, :], -C1, PB[:, :], ALU.mult, ALU.add), t)
            t = dve(lambda e: e.scalar_tensor_tensor(PA[:, :], PC[:, :], -C2, PD[:, :], ALU.mult, ALU.add), t)
            t = dve(lambda e: e.scalar_tensor_tensor(PD[:, :], PC[:, :], -C3, PA[:, :], ALU.mult, ALU.add), t)
            t = dve(lambda e, quarter=quarter: e.tensor_scalar(PA[:, :], PD[:, :], quarter * TWO_PI, 3.1415925,
                                                               ALU.add, ALU.min), t)
            t = dve(lambda e: e.tensor_scalar(PD[:, :], PA[:, :], -3.1415925, None, ALU.max), t)
            t_tab = [act(lambda e, dst=dst: e.activation(dst[:, :], PD[:, :], ACT.Sin), t)]

        t_mod = modulation(0, 0)
        t_r = rstd(D)
        for hf in range(2):
            normed(HALF[hf], lambda j: GS[:, 0, j:j + 1], lambda j: MOD[:, 0, j:j + 1], t_r, t_mod)
        VV = sb([128, 8, 4, 128], F32, AR)
        QNH = sb([128, 4, S], F32R, AR + 16 * KB)
        QNL = sb([128, 4, S], F32R, AR + 24 * KB)
        QRS = sb([128, 4, S], F32R, AR + 32 * KB)
        CQH = sb([128, 3, S], F32R, AR + 40 * KB)
        CQL = sb([128, 3, S], F32R, AR + 46 * KB)
        CKH = sb([128, 2, S], F32R, AR + 52 * KB)
        CKL = sb([128, 2, S], F32R, AR + 56 * KB)
        PBUF = [sb([128, 1280], F32, AR + 52 * KB), sb([128, 1280], F32, AR + 57 * KB)]
        KRH = sb([128, S], F32R, o_ssq)
        KRL = sb([128, S], F32R, o_r)
        t_arena = now("pe", "dve", "act")

        def low_rank(n, gain, hi, lo, width, toks):
            held = []

            def evac(m, o, t, cs):
                if cs != HALF[1]:
                    held.append([*take_tmp(), []])
                i, tm, rel, ts = held[m]
                t = act(lambda e: e.activation(tm[:, cs], o, ACT.Copy), t, rel)
                ts.append(t)
                sumsq(m, tm[:, cs], t, cs)
                return t

            def norm():
                t_r = rstd(width)
                for j, (i, tm, _, ts) in enumerate(held):
                    t1 = dve(lambda e, j=j, tm=tm: e.scalar_tensor_tensor(tm[:, :], tm[:, :], gain(j), RT[:, :],
                                                                          ALU.mult, ALU.mult), ts, t_r, ssq_t)
                    r_rel[0] = r_rel[1] = t1
                    tt = two_parts(hi[:, j, :], lo[:, j, :], tm[:, :], t1, t_arena)
                    tmps.rel[i] = tt
                    toks.append(tt)

            return evac, norm

        cq_tok, ck_tok, kr_tok = [], [], []
        cq_evac, cq_norm = low_rank(3, lambda j: col("g_q", j), CQH, CQL, 384, cq_tok)
        ck_evac, ck_norm = low_rank(2, lambda j: col("g_kv", j), CKH, CKL, 256, ck_tok)
        linear("dq", 2, list(three), hx, cq_evac, halves=True)

        def kr_then(tm, t, cs):
            kr_tok.extend(two_parts(KRH[:, :], KRL[:, :], tm, t, ssq_rel, r_rel))
            return list(kr_tok)

        def dkv_evac(n, o, t, cs):
            if n < 2:
                return ck_evac(n, o, t, cs)
            return rotated(o, t, COS[:, :], SIN[:, :], rot, t_tab, kr_then)

        linear("dkv", 2, list(three), hx, dkv_evac, mid={(0, 0, 0): cq_norm})

        qn_tok, qr_tok = {}, {}

        def uq(p, mid=None):
            def then(tm, t, cs):
                out = []
                for e_half in range(2):
                    h = 2 * p + e_half
                    qr_tok[h] = stacked(QRS[:, h % 4, :], tm, e_half, t, t_arena)
                    out += qr_tok[h]
                return out

            def evac(n, o, t, cs):
                if n == 0:
                    return rotated(o, t, COS[:, :], SIN[:, :], rot, t_tab, then)
                h = 2 * p + n - 1
                qn_tok[h] = two_parts(QNH[:, h % 4, :], QNL[:, h % 4, :], o, t, t_arena)
                return qn_tok[h]

            linear("uq", 1, [(256, 128), (0, 128), (128, 128)],
                   lambda k, n, cs: (CQH[:, k, :], CQL[:, k, :], cq_tok[k]), evac, mid=mid)

        uq(0, {(0, 0, 0): ck_norm})
        uq(1)
        kn_tok, vv_tok = {}, {}
        for hb in range(2):
            it = use("ukv")
            for hh in range(4):
                h = 4 * hb + hh
                b = banks.take()
                for k in range(2):
                    t = mm3(PS[:, b, :], it["hi"][:, k, 256 * hh:256 * hh + 128],
                            it["lo"][:, k, 256 * hh:256 * hh + 128], CKH[:, k, :], CKL[:, k, :], k == 0, k == 1,
                            [it["ready"], ck_tok[k], banks.rel[b] if k == 0 else None], k == 1)
                kn_tok[h] = banks.rel[b] = two_parts(HHI[:, h, :], HLO[:, h, :], PS[:, b, :], t)
                flush()
            vh = it["hi"].rearrange("p k (h c) -> p k h c", c=256)
            vl = it["lo"].rearrange("p k (h c) -> p k h c", c=256)
            for t4 in range(4):
                b = banks.take()
                ts = slice(t4 * 128, t4 * 128 + 128)
                o = PS[:, b, :].rearrange("p (h c) -> p h c", c=128)
                for k in range(2):
                    t = mm3(o, CKH[:, k, ts], CKL[:, k, ts], vh[:, k, :, 128:256], vl[:, k, :, 128:256],
                            k == 0, k == 1, [banks.rel[b] if k == 0 else None], k == 1)
                tv = act(lambda e, hb=hb, t4=t4, o=o: e.activation(VV[:, 4 * hb:4 * hb + 4, t4, :], o, ACT.Copy), t,
                         t_arena)
                banks.rel[b] = tv
                vv_tok[(hb, t4)] = tv
            done(it, t)

        MSCALE = 192.0 ** -0.5
        SPOS = {3: (0, 0, 512), 2: (1, 0, 384), 0: (2, 0, 256), 1: (2, 256, 256)}
        POFF = [0, 128, 384, 768]
        TPOS = {0: (3, 0), 1: (4, 0), 2: (5, 0), 3: (4, 384)}
        p_rel = [None, None]
        soft, pt_of = {}, {}
        o_tok = [None] * 8
        state["reach"] = 0

        def m_scores(h):
            st = ST[:, 16 * (h % 4):16 * (h % 4) + 16]
            P = PBUF[h % 2]
            tx, s_tok = [], {}
            for i in (3, 2, 0, 1):
                bk, c, w = SPOS[i]
                o = PS[:, bk, c:c + w]
                qs = slice(i * 128, i * 128 + 128)
                qh, ql, qr = QNH[:, h % 4, qs], QNL[:, h % 4, qs], QRS[:, h % 4, qs]
                kh, kl = HHI[:, h, 0:w], HLO[:, h, 0:w]
                prods = ((qh, kh), (ql, kh), (qh, kl), (qr, KRH[:, 0:w]), (qr, KRL[:, 0:w]))
                for m, (lhs, rhs) in enumerate(prods):
                    t = pe(lambda e, o=o, lhs=lhs, rhs=rhs, m=m: e.matmul(o, lhs, rhs, start=(m == 0), stop=(m == 4)),
                           banks.rel[bk] if m == 0 else None, qn_tok[h], kn_tok[h], qr_tok[h], kr_tok, sig=(m == 4))
                s_tok[i] = t
            s_tok[0] = s_tok[1]
            tm = {}
            for i in (3, 2, 0, 1):
                bk, c, _ = SPOS[i]
                d = 128 * i
                cur = masked_max(P[:, POFF[i] + d:POFF[i] + d + 128], PS[:, bk, c + d:c + d + 128], causal, st[:, i:i + 1],
                                 s_tok[i], p_rel[h % 2], t_const)
                if i:
                    cur = masked_max(P[:, POFF[i]:POFF[i] + d], PS[:, bk, c:c + d],
                                     ZERO.to_broadcast([128, d]), st[:, 4 + i:5 + i], cur, first=st[:, i:i + 1])
                tm[i] = cur
            banks.rel[0], banks.rel[1], banks.rel[2] = tm[3], tm[2], [tm[0], tm[1]]
            t0 = dve(lambda e: e.tensor_scalar(st[:, 0:1], st[:, 0:1], -MSCALE, None, ALU.mult), tm[0])
            tn = dve(lambda e: e.tensor_scalar(st[:, 1:4], st[:, 5:8], -MSCALE, None, ALU.mult), list(tm.values()))
            te = []
            for i in (3, 2, 1, 0):
                Pi = P[:, POFF[i]:POFF[i] + 128 * (i + 1)]
                te.append(act(lambda e, i=i, Pi=Pi: e.activation(Pi, Pi, ACT.Exp, bias=st[:, i:i + 1], scale=MSCALE,
                                                                 accum_out=st[:, 8 + i:9 + i]), tn, t0))
            tr = dve(lambda e: e.reciprocal(st[:, 12:16], st[:, 8:12]), te)
            soft[h] = {}
            for i in (0, 1, 2, 3):
                Pi = P[:, POFF[i]:POFF[i] + 128 * (i + 1)]
                soft[h][i] = dve(lambda e, Pi=Pi, i=i: e.tensor_scalar(Pi, Pi, st[:, 12 + i:13 + i], None, ALU.mult),
                                 tr)

        def m_turn(h):
            P = PBUF[h % 2]
            tl = {}
            for j in (0, 1, 3, 2):
                bk, c = TPOS[j]
                for i in range(j, 4):
                    t = pe(lambda e, bk=bk, c=c, i=i, j=j: e.transpose(
                        PS[:, bk, c + (i - j) * 128:c + (i - j) * 128 + 128],
                        P[:, POFF[i] + j * 128:POFF[i] + j * 128 + 128], ident), banks.rel[bk], soft[h][i],
                        sig=(i == 3))
                tl[j] = t
            p_rel[h % 2] = t
            pt_of[h] = {}
            for bk, n, tok, on in ((3, 512, tl[0], act), (4, 512, tl[3], dve), (5, 256, tl[2], act)):
                i, tm, rel = take_tmp()
                if on is act:
                    t = act(lambda e, bk=bk, n=n, tm=tm: e.activation(tm[:, 0:n], PS[:, bk, 0:n], ACT.Copy), tok, rel)
                else:
                    t = dve(lambda e, bk=bk, n=n, tm=tm: e.tensor_copy(tm[:, 0:n], PS[:, bk, 0:n]), tok, rel)
                banks.rel[bk] = t
                pt_of[h][bk] = (i, tm, t)

        def m_values(h):
            ob = 6 + h % 2
            for j in range(4):
                bk, c = TPOS[j]
                w = 512 - 128 * j
                i, tm, t = pt_of[h][bk]
                tpv = pe(lambda e, j=j, c=c, w=w, tm=tm: e.matmul(PS[:, ob, 128 * j:512], VV[:, h, j, :], tm[:, c:c + w],
                                                                  start=(j == 0), stop=(j == 3),
                                                                  skip_group_check=True),
                         t, banks.rel[ob] if j == 0 else None, vv_tok[(h // 4, j)], sig=(j == 3))
            for i, tm, t in pt_of[h].values():
                tmps.rel[i] = tpv
            o_tok[h] = banks.rel[ob] = two_parts(HHI[:, h, :], HLO[:, h, :], PS[:, ob, :], tpv)

        ZERO = GS[:, 0, 0:1]
        t_zero = dve(lambda e: e.memset(ZERO, 0.0), now("dve"))
        m_scores(0)
        m_scores(1)
        banks.only(3, 4, 5, 6)
        uq(2)
        for h in range(8):
            if h == 2:
                uq(3)
            m_turn(h)
            flush()
            if h < 6:
                m_scores(h + 2)
            if h == 5:
                ssq_rel[:] = r_rel[:] = now("pe") * 2
            m_values(h)
            if h >= 1:
                ahead()
        banks.only(*range(8))
        state["reach"] = 4

        def ox(k, n, cs):
            return HHI[:, k, cs], HLO[:, k, cs], o_tok[k]

        def mo_evac(n2):
            return lambda n, o, t, cs: add_x(4 * n2 + n, o, MOD[:, 0, 16 + 4 * n2 + n:17 + 4 * n2 + n], t,
                                             mod_tok[(0, 2)], cs)

        linear("mo", 2, list(four), ox, mo_evac(0))
        norm = mod_norm(0, 1)
        linear("mo", 2, list(four), ox, mo_evac(1), frees_h=True, **closing(norm))

        HID = [[sb([128, 8, S], F32R, AR + (2 * i + k) * 16 * KB) for k in range(2)] for i in range(2)]
        hid_tok = [[[None, None] for _ in range(8)] for _ in range(2)]
        hid_rel = [None, None]

        def hid(i):
            return lambda k, n, cs: (HID[i][0][:, k, cs], HID[i][1][:, k, cs], [hid_tok[i][k][f] for f in hs(cs)])

        def hidden(i, j, tm, t, cs):
            tt = two_parts(HID[i][0][:, j, cs], HID[i][1][:, j, cs], tm[:, cs], t, hid_rel[i])
            for f in hs(cs):
                hid_tok[i][j][f] = tt
            return tt

        def ff(l, norm, closing_norm, extra=None):
            hid_rel[:] = [now("pe", "dve", "act")] * 2

            def up(q):
                for n2 in range(2):
                    def evac(n, o, t, cs, n2=n2):
                        i, tm, rel = take_tmp()
                        ta = act(lambda e: e.activation(tm[:, cs], o, ACT.Relu), t, rel)
                        td = dve(lambda e: e.tensor_tensor(tm[:, cs], tm[:, cs], tm[:, cs], ALU.mult), ta)
                        tmps.rel[i] = hidden(q % 2, 4 * n2 + n, tm, td, cs)
                        return ta
                    linear(f"up{l}", 2, list(four), hx, evac, **(opening(norm) if q == 0 and n2 == 0 else {}))

            def down(q):
                for n2 in range(2):
                    def evac(n, o, t, cs, n2=n2):
                        j = 4 * n2 + n
                        t = add_x(j, o, MOD[:, l, 40 + j:41 + j], t, mod_tok[(l, 5)], cs, q == 3)
                        if extra and q == 3:
                            extra(j, cs, t)
                        return t
                    last = closing(closing_norm()) if q == 3 and n2 else {}
                    linear(f"down{l}", 2, list(four), hid(q % 2), evac, **last)
                hid_rel[q % 2] = now("pe")

            up(0)
            for q in range(4):
                if q < 3:
                    up(q + 1)
                if q == 2:
                    h_rel[:] = now("pe") * 2
                down(q)

        box = {}

        def then_norm(make):
            def go():
                box["norm"] = make()
                return box["norm"]
            return go

        ff(0, norm, then_norm(lambda: mod_norm(1, 0)))

        settle(True)
        t_arena = now("pe", "act", "dve")
        QS = sb([128, 16, S], F32R, AR)
        KH = sb([128, 4, S], F32R, AR + 32 * KB)
        KL = sb([128, 4, S], F32R, AR + 40 * KB)
        SV = sb([128, 4, 256], F32, AR + 48 * KB)
        SB2 = [sb([128, 4, 256], F32, AR + 52 * KB), sb([128, 4, 256], F32, AR + 56 * KB)]
        BT = [sb([128, 512], F32, AR + 60 * KB), sb([128, 512], F32, AR + 62 * KB)]
        DIST = sb([128, 512], F32, o_acc)
        BV = sb([128, 256], F32, o_acc + 2 * KB)
        SINK = sb([128, 16], F32, o_acc + 3 * KB)
        NSINK = sb([128, 16], F32, o_acc + 3 * KB + 64)
        GB = sb([128, 8], F32, o_acc + 3 * KB + 128)
        t_swa = dma("swa", DIST[:, :], A["k_dist"], acc_rel, t_arena, eng="pool")
        t_swa = dma("swa", BV[:, :], A["swa_b_qkv"][:, 1280:1536].to_broadcast([128, 256]), eng="pool")
        t_swa = dma("swa", SINK[:, :], A["swa_sinks"].to_broadcast([128, 16]), eng="pool")

        sq_tok, sk_tok, sv_tok = {}, {}, {}

        def q_evac(half):
            def evac(n, o, t, cs):
                out = []
                for e_half in range(2):
                    h = 8 * half + 2 * n + e_half
                    a, b = slice(64 * e_half, 64 * e_half + 64), slice(64 - 64 * e_half, 128 - 64 * e_half)
                    src, bias, d = o[a, :], col("bq", h)[a, :], QS[:, h, cs]
                    th = act(lambda e, d=d, a=a, src=src, bias=bias: e.activation(d[a, :], src, ACT.Identity, bias=bias),
                             t, t_arena, t_cols)
                    tl = dve(lambda e, d=d, a=a, b=b, src=src, bias=bias: e.scalar_tensor_tensor(
                        d[b, :], src, bias, d[a, :].bitcast(F32), ALU.add, ALU.subtract), t, th, t_arena, t_cols)
                    sq_tok.setdefault(h, []).extend([th, tl])
                    out += [th, tl]
                return out
            return evac

        linear("qkv", 2, list(four), hx, q_evac(0), **opening(box["norm"]))
        t_nsink = dve(lambda e: e.tensor_scalar(NSINK[:, :], SINK[:, :], -1.0, None, ALU.mult), t_swa)
        t_gb = dve(lambda e: e.tensor_tensor(GB[:, :], MOD[:, 1, 16:24], col("b_o", 0, 8), ALU.mult), mod_tok[(1, 2)],
                   t_cols, t_swa)
        ia, ib = use("qkv"), use("qkv")
        for n in range(2):
            b = banks.take()
            for k in range(8):
                it = (ia, ib)[k // 4]
                cs = slice(128 * n, 128 * n + 128)
                t = mm3(PS[:, b, :], it["hi"][:, k % 4, cs], it["lo"][:, k % 4, cs], HHI[:, k, :], HLO[:, k, :],
                        k == 0, k == 7, [it["ready"], h_tok[k], banks.rel[b] if k == 0 else None], k == 7)
            i, tm, rel = take_tmp()
            t = act(lambda e, n=n, b=b, tm=tm: e.activation(tm[:, :], PS[:, b, :], ACT.Identity, bias=col("bk", n)),
                    t, rel)
            banks.rel[b] = t
            for e_half in range(2):
                g = 2 * n + e_half
                sk_tok[g] = doubled(KH[:, g, :], KL[:, g, :], tm, e_half, t, t_arena)
            tmps.rel[i] = [sk_tok[2 * n], sk_tok[2 * n + 1]]
        for t4 in range(4):
            b = banks.take()
            ts = slice(128 * t4, 128 * t4 + 128)
            for k in range(8):
                it = (ia, ib)[k // 4]
                t = mm3(PS[:, b, 0:256], HHI[:, k, ts], HLO[:, k, ts], it["hi"][:, k % 4, 256:512],
                        it["lo"][:, k % 4, 256:512], k == 0, k == 7, [banks.rel[b] if k == 0 else None], k == 7)
            sv_tok[t4] = dve(lambda e, t4=t4, b=b: e.tensor_tensor(SV[:, t4, :], PS[:, b, 0:256], BV[:, :], ALU.add), t,
                             t_swa, t_arena)
            banks.rel[b] = sv_tok[t4]
        done(ia, t)
        done(ib, t)

        sb_rel, bt_rel = [None, None], [None, None]
        soft2, pt2_of = {}, {}

        def s_scores(h):
            g, bk = h // 4, 2 * (h % 2)
            slope = 2.0 ** (-8.0 * (h + 1) / 16)
            B, T = SB2[h % 2], BT[h % 2]
            st = ST[:, 16 * (h % 4):16 * (h % 4) + 16]
            t_bias = pool(lambda e: e.tensor_scalar(T[:, :], DIST[:, :], -8.0 * slope, None, ALU.mult), t_swa,
                          bt_rel[h % 2], t_arena)
            tx = []
            for n in range(4):
                ks = slice(128 * max(n - 1, 0), 128 * max(n - 1, 0) + 256)
                qs = slice(128 * n, 128 * n + 128)
                o = PS[:, bk + n // 2, 256 * (n % 2):256 * (n % 2) + 256]
                pe(lambda e, o=o, qs=qs, ks=ks: e.matmul(o, QS[:, h, qs], KH[:, g, ks], start=True, stop=False),
                   banks.rel[bk], banks.rel[bk + 1], sq_tok[h], sk_tok[g])
                t = pe(lambda e, o=o, qs=qs, ks=ks: e.matmul(o, QS[:, h, qs], KL[:, g, ks], start=False, stop=True),
                       sig=True)
                if n % 2 == 0:
                    continue
                for m in (n - 1, n):
                    o = PS[:, bk + n // 2, 256 * (m % 2):256 * (m % 2) + 256]
                    tx.append(masked_max(B[:, m, :], o, T[:, 256 * (m > 0):256 * (m > 0) + 256], st[:, m:m + 1], t,
                                         t_bias, sb_rel[h % 2], t_arena))
            banks.rel[bk] = banks.rel[bk + 1] = bt_rel[h % 2] = tx[-1]
            t = dve(lambda e: e.tensor_scalar(st[:, 4:8], st[:, 0:4], -0.125, NSINK[:, h:h + 1], ALU.mult, ALU.min), tx,
                    t_nsink)
            te = []
            for n in range(4):
                te.append(act(lambda e, n=n: e.activation(B[:, n, :], B[:, n, :], ACT.Exp, bias=st[:, 4 + n:5 + n],
                                                          scale=0.125, accum_out=st[:, 8 + n:9 + n]), t))
            te.append(act(lambda e: e.activation(st[:, 12:16], st[:, 4:8], ACT.Exp, bias=SINK[:, h:h + 1]), t))
            t = dve(lambda e: e.tensor_tensor(st[:, 8:12], st[:, 8:12], st[:, 12:16], ALU.add), te)
            t = dve(lambda e: e.reciprocal(st[:, 0:4], st[:, 8:12]), t)
            soft2[h] = [dve(lambda e, n=n: e.tensor_scalar(B[:, n, :], B[:, n, :], st[:, n:n + 1], None, ALU.mult), t)
                        for n in range(4)]

        SPAIRS = [(0, 0, 0)] + [(n, w, n - 1 + w) for n in range(1, 4) for w in range(2)]

        def s_turn(h):
            B = SB2[h % 2]
            pt2_of[h] = []
            for bk, lo, hi in ((4, 0, 4), (5, 4, 7)):
                for m in range(lo, hi):
                    n, w, _ = SPAIRS[m]
                    t = pe(lambda e, m=m, n=n, w=w, bk=bk, lo=lo: e.transpose(
                        PS[:, bk, 128 * (m - lo):128 * (m - lo) + 128], B[:, n, 128 * w:128 * w + 128], ident),
                        banks.rel[bk], soft2[h][n], sig=(m == hi - 1))
                i, tm, rel = take_tmp()
                c = 128 * (hi - lo)
                t2 = act(lambda e, bk=bk, c=c, tm=tm: e.activation(tm[:, 0:c], PS[:, bk, 0:c], ACT.Copy), t, rel)
                banks.rel[bk] = t2
                pt2_of[h].append((i, tm, t2))
            sb_rel[h % 2] = t

        def s_values(h):
            g = h // 4
            ob, off = 6 + (h // 2) % 2, 64 * (h % 2)
            for m, (n, w, kb) in enumerate(SPAIRS):
                i, tm, t = pt2_of[h][m // 4]
                tv = pe(lambda e, n=n, m=m, kb=kb, tm=tm, w=w: e.matmul(
                    PS[off:off + 64, ob, 128 * n:128 * n + 128], SV[:, kb, 64 * g:64 * g + 64],
                    tm[:, 128 * (m % 4):128 * (m % 4) + 128], start=(m == 0 or w == 0), stop=(m == 0 or w == 1)),
                    t, banks.rel[ob], sv_tok[kb], sig=(m == 6))
            for i, tm, t in pt2_of[h]:
                tmps.rel[i] = tv
            if h % 2:
                j = h // 2
                o_tok[j] = banks.rel[ob] = two_parts(HHI[:, j, :], HLO[:, j, :], PS[:, ob, :], tv, t_h)

        s_scores(0)
        s_scores(1)
        banks.only(4, 5, 6, 7)
        linear("qkv", 2, list(four), hx, q_evac(1))
        banks.only(*range(8))
        t_h = now("pe")
        for h in range(16):
            s_turn(h)
            if h < 14:
                s_scores(h + 2)
            s_values(h)
            ahead()

        def so_evac(n2):
            def evac(n, o, t, cs):
                j = 4 * n2 + n
                i, tm, rel = take_tmp()
                t = dve(lambda e: e.tensor_scalar(tm[:, cs], o, MOD[:, 1, 16 + j:17 + j], GB[:, j:j + 1], ALU.mult,
                                                  ALU.add), t, rel, t_gb)
                t2 = dve(lambda e: e.tensor_tensor(X[:, j, cs], X[:, j, cs], tm[:, cs], ALU.add), t, x_at(j, cs))
                tmps.rel[i] = t2
                for f in hs(cs):
                    x_tok[j][f] = t2
                sumsq(j, X[:, j, cs], t2, cs)
                return t
            return evac

        linear("so", 2, list(four), ox, so_evac(0))
        norm = mod_norm(1, 1)
        linear("so", 2, list(four), ox, so_evac(1), frees_h=True, **closing(norm))

        def g_final(j):
            return col("g_final", j)

        def weighted(j, cs, t):
            sumsq(j, X[:, j, cs], t, cs, SSQ2, ssq2_t, ssq2_rel, g_final(j))

        def final_norm(hf):
            cs = HALF[hf]
            t_r = rstd(D, cs)
            b = banks.take()
            t = pe(lambda e: e.matmul(PS[:, b, cs], ones, SSQ2[:, cs], start=True, stop=True), ssq2_t[hf],
                   banks.rel[b], sig=True)
            i, tm, rel = take_tmp()
            t1 = dve(lambda e: e.tensor_tensor(tm[:, cs], PS[:, b, cs], RT[:, cs], ALU.mult), t, t_r, rel)
            banks.rel[b] = t1
            t2 = dve(lambda e: e.tensor_tensor(tm[:, cs], tm[:, cs], RT[:, cs], ALU.mult), t1)
            ssq2_rel[hf], t_r2 = rsqrt(tm[:, cs], t2, D, SSQ2, cs, t)
            tmps.rel[i] = ssq2_rel[hf]
            for j in range(8):
                x_tok[j][hf] = dve(lambda e, j=j: e.scalar_tensor_tensor(X[:, j, cs], X[:, j, cs], g_final(j),
                                                                         RT[:, cs], ALU.mult, ALU.mult), t_r,
                                   x_tok[j][hf], ssq_t[hf], ssq2_t[hf])
                r_rel[hf] = x_tok[j][hf]
            normed(cs, lambda j: col("ffn1_norm", j), None, t_r2, None, SSQ2, ssq2_rel)

        ff(1, norm, lambda: final_norm, weighted)

        def glu(norm, closing_norm):
            hid_rel[:] = [now("pe", "dve", "act")] * 2

            def up(blk):
                for c in range((4, 4, 3)[blk]):
                    parts = HALF if blk == 0 and c == 0 else (FULL,)
                    its = []
                    for hf, cs in enumerate(parts):
                        bk = [banks.take() for _ in range(4)]
                        banks.busy.update(bk)
                        tk = []
                        for w, name in enumerate(("w1", "w3")):
                            if hf == 0:
                                its.append(use(name))
                            it = its[w]
                            for n in range(2):
                                b = bk[2 * w + n]
                                for k in range(8):
                                    ws = slice(128 * n, 128 * n + 128)
                                    xh, xl, tx = hx(k, n, cs)
                                    t = mm3(PS[:, b, cs], it["hi"][:, k, ws], it["lo"][:, k, ws], xh, xl, k == 0,
                                            k == 7, [it["ready"], tx, banks.rel[b] if k == 0 else None], k == 7)
                                tk.append(t)
                                if len(parts) == 2 and (hf, w, n) == (0, 0, 0):
                                    norm(1)
                            if hf == len(parts) - 1:
                                done(it, t)
                        banks.busy.difference_update(bk)
                        for n in range(2):
                            b1, b3 = bk[n], bk[2 + n]
                            i, tm, rel = take_tmp()
                            ta = act(lambda e, tm=tm, b1=b1, cs=cs: e.activation(tm[:, cs], PS[:, b1, cs], ACT.Silu),
                                     tk[n], rel)
                            banks.rel[b1] = ta
                            td = dve(lambda e, tm=tm, b3=b3, cs=cs: e.tensor_tensor(tm[:, cs], tm[:, cs], PS[:, b3, cs],
                                                                                    ALU.mult), ta, tk[2 + n])
                            banks.rel[b3] = td
                            tmps.rel[i] = hidden(blk % 2, 2 * c + n, tm, td, cs)

            def down(blk):
                for n2 in range(2):
                    last = closing(closing_norm) if blk == 2 and n2 else {}
                    linear("w2", 2, list(four), hid(blk % 2),
                           lambda n, o, t, cs: add_x(4 * n2 + n, o, 0.5, t, None, cs, blk == 2), **last)
                hid_rel[blk % 2] = now("pe")

            up(0)
            for blk in range(3):
                if blk < 2:
                    up(blk + 1)
                if blk == 1:
                    h_rel[:] = now("pe") * 2
                down(blk)

        norm = plain_norm("mix_norm")
        glu(final_norm, norm)

        t_arena = now("pe", "dve", "act")
        DQ = sb([128, 6, S], F32R, AR)
        DKH = sb([128, 6, S], F32R, AR + 12 * KB)
        DKL = sb([128, 6, S], F32R, AR + 24 * KB)
        DV = sb([128, 4, 768], F32, AR + 36 * KB)
        DM = sb([128, 10, 128], F32, AR + 48 * KB)
        SB3 = [sb([128, 1280], F32, AR + 53 * KB), sb([128, 1280], F32, AR + 58 * KB)]
        DCOS = sb([128, S], F32, o_acc)
        DSIN = sb([128, S], F32, o_acc + 2 * KB)
        OHI = [sb([128, S], F32R, o_ssq), sb([128, S], F32R, AR)]
        OLO = [sb([128, S], F32R, o_r), sb([128, S], F32R, AR + 2 * KB)]
        t_dm = dma("dil", DCOS[:, :], A["k_dcos"], t_arena, eng="pool")
        t_dm = dma("dil", DSIN[:, :], A["k_dsin"], eng="pool")
        t_dm = dma("dil", rot, A["k_drot"], eng="pool")
        t_dm = dma("dil", DM[:, :, :], A["k_dil"], eng="pool")
        dq_tok, dk_tok = {}, {}

        def qk(a, kind):
            def then_of(g):
                def then(tm, t, cs):
                    out = []
                    for e_half in range(2):
                        s = 2 * g + e_half
                        if kind == "q":
                            tt = stacked(DQ[:, s, cs], tm, e_half, t, t_arena)
                            dq_tok.setdefault((a, s), []).extend(tt)
                        else:
                            tt = doubled(DKH[:, s, cs], DKL[:, s, cs], tm, e_half, t, t_arena)
                            dk_tok.setdefault((a, s), []).extend(tt)
                        out += tt
                    return out
                return then

            return lambda n, o, t, cs: rotated(o, t, DCOS[:, cs], DSIN[:, cs], rot, t_dm, then_of(n), cs)

        dv_tok = {}

        def v_evac(c, w):
            def evac(n, o, t, cs):
                tv = act(lambda e: e.activation(DV[:, n, c:c + w], o, ACT.Copy), t, t_arena)
                dv_tok.setdefault(n, []).append(tv)
                return tv
            return evac

        sb3_rel = [None, None]
        soft3, pt3_of = {}, {}
        SALL = PS[:, 0:3, :].rearrange("p n k -> p (n k)")
        TALL = PS[:, 3:6, :].rearrange("p n k -> p (n k)")

        def blocks(i):
            out = [(0, kb) for kb in ((i - 1, i) if i else (0,))]
            return out + [(1, kb) for kb in range(i + 1)] + [(2, kb) for kb in range(i + 1)]

        def d_scores(s):
            j, i = s // 4, s % 4
            a, e_half = j // 2, j % 2
            bl = blocks(i)
            runs = []
            for c, (g, kb) in enumerate(bl):
                if runs and runs[-1][1] == g and c % 4:
                    runs[-1][3] += 1
                else:
                    runs.append([c, g, kb, 1])
            for m, (c, g, kb, n) in enumerate(runs):
                q, kh, kl = (T[:, 2 * g + e_half, :] for T in (DQ, DKH, DKL))
                qs, ks = slice(128 * i, 128 * i + 128), slice(128 * kb, 128 * (kb + n))
                o = SALL[:, 128 * c:128 * (c + n)]
                pe(lambda e, o=o, q=q, kh=kh, qs=qs, ks=ks: e.matmul(o, q[:, qs], kh[:, ks], start=True, stop=False),
                   [banks.rel[b] for b in range(3)], dq_tok[(a, 2 * g + e_half)], dk_tok[(a, 2 * g + e_half)])
                t = pe(lambda e, o=o, q=q, kl=kl, qs=qs, ks=ks: e.matmul(o, q[:, qs], kl[:, ks], start=False,
                                                                         stop=True), sig=(m == len(runs) - 1))
            B = SB3[s % 2]
            st = ST[:, 16 * (s % 4):16 * (s % 4) + 16]
            g0 = 2 if i else 1
            tm = []
            for m, (c, n, m0) in enumerate(((0, g0, 2 - g0), (g0, i + 1, 5 - i), (g0 + i + 1, i + 1, 9 - i))):
                tm = [masked_max(B[:, 128 * c:128 * (c + n)], SALL[:, 128 * c:128 * (c + n)],
                                 DM[:, m0:m0 + n, :].rearrange("p n k -> p (n k)"), st[:, m:m + 1], t, t_dm,
                                 sb3_rel[s % 2], t_arena, tm, first=st[:, m - 1:m] if m else -3.0e38)]
            for b in range(3):
                banks.rel[b] = tm[0]
            w = 128 * len(bl)
            t = dve(lambda e: e.tensor_scalar(st[:, 4:5], st[:, 2:3], -0.125, None, ALU.mult), tm)
            t = act(lambda e: e.activation(B[:, 0:w], B[:, 0:w], ACT.Exp, bias=st[:, 4:5], scale=0.125,
                                           accum_out=st[:, 5:6]), t)
            t = dve(lambda e: e.reciprocal(st[:, 6:7], st[:, 5:6]), t)
            soft3[s] = dve(lambda e: e.tensor_scalar(B[:, 0:w], B[:, 0:w], st[:, 6:7], None, ALU.mult), t)

        do_tok = [None, None]

        def d_turn(s):
            bl = blocks(s % 4)
            B = SB3[s % 2]
            n = len(bl)
            pt3_of[s] = []
            for q in range(-(-n // 4)):
                c0, c1 = 4 * q, min(4 * q + 4, n)
                for c in range(c0, c1):
                    t = pe(lambda e, c=c: e.transpose(TALL[:, 128 * c:128 * c + 128], B[:, 128 * c:128 * c + 128],
                                                      ident), banks.rel[3 + q], soft3[s], sig=(c == c1 - 1))
                i, tm, rel = take_tmp()
                w = 128 * (c1 - c0)
                src = TALL[:, 128 * c0:128 * c1]
                if q == 1:
                    t2 = dve(lambda e, tm=tm, w=w, src=src: e.tensor_copy(tm[:, 0:w], src), t, rel)
                else:
                    t2 = act(lambda e, tm=tm, w=w, src=src: e.activation(tm[:, 0:w], src, ACT.Copy), t, rel)
                banks.rel[3 + q] = t2
                pt3_of[s].append((i, tm, t2))
            sb3_rel[s % 2] = t

        def d_values(s):
            j, i = s // 4, s % 4
            a, off = j // 2, 64 * (j % 2)
            bl = blocks(i)
            ob = 6 + a
            o = PS[off:off + 64, ob, 128 * i:128 * i + 128]
            for c, (g, kb) in enumerate(bl):
                vc = 64 * (4 * g + j)
                _, tm, t = pt3_of[s][c // 4]
                tv = pe(lambda e, c=c, kb=kb, vc=vc, tm=tm: e.matmul(
                    o, DV[:, kb, vc:vc + 64], tm[:, 128 * (c % 4):128 * (c % 4) + 128], start=(c == 0),
                    stop=(c == len(bl) - 1)), t, banks.rel[ob], dv_tok[kb], sig=(c == len(bl) - 1))
            for idx, _, _ in pt3_of[s]:
                tmps.rel[idx] = tv
            if i == 3 and j % 2:
                do_tok[a] = banks.rel[ob] = two_parts(OHI[a][:, :], OLO[a][:, :], PS[:, ob, :], tv, ssq_rel, r_rel)

        linear("qk", 2, list(three), hx, qk(0, "q"), **opening(norm))
        linear("qk", 2, list(three), hx, qk(0, "k"))
        linear("v", 2, [(0, 512)] * 4, hx_tok, v_evac(0, 512), swap=True)
        d_scores(0)
        d_scores(1)
        banks.only(3, 4, 5, 6)
        linear("v2", 1, [(0, 256)] * 4, hx_tok, v_evac(512, 256), swap=True)

        PZ = sb([128, 2, 16 + S], F32, AR + 4 * KB)
        DH = sb([128, 4, S], F32R, AR + 9 * KB)
        DL = sb([128, 4, S], F32R, AR + 17 * KB)
        CNT = sb([128, 4, S], F32, AR + 25 * KB)
        d_tok = {}
        pz_rel = [None]
        t_pz = []

        def pz_evac(n, o, t, cs):
            i, tm, rel = take_tmp()
            p0 = act(lambda e: e.activation(tm[:, :], o, ACT.Copy), t, rel)
            cur = act(lambda e: e.activation(PZ[:, 0, 16:16 + S], tm[:, :], ACT.Copy), p0, pz_rel, t_pz)
            for step in range(n + 1):
                w = 1 << step
                src, dst = step % 2, 1 - step % 2
                cur = dve(lambda e, w=w, src=src, dst=dst: e.tensor_tensor(
                    PZ[:, dst, 16:16 + S], PZ[:, src, 16:16 + S], PZ[:, src, 16 - w:16 - w + S], ALU.add), cur, t_pz,
                    pz_rel)
            fin = (n + 1) % 2
            i2, tm2, rel2 = take_tmp()
            t1 = dve(lambda e: e.tensor_tensor(tm2[:, :], PZ[:, fin, 16:16 + S], CNT[:, n, :], ALU.mult), cur, t_pz,
                     rel2)
            pz_rel[0] = t1
            t2 = dve(lambda e: e.tensor_tensor(tm2[:, :], tm2[:, :], tm[:, :], ALU.subtract), t1, p0)
            tmps.rel[i] = t2
            d_tok[n] = two_parts(DH[:, n, :], DL[:, n, :], tm2[:, :], t2, t_pz)
            tmps.rel[i2] = d_tok[n]
            return p0

        for s in range(16):
            if s == 6:
                banks.only(3, 4, 5, 7)
                linear("qk", 2, list(three), hx, qk(1, "q"))
                linear("qk", 2, list(three), hx, qk(1, "k"))
            if s == 14:
                t_pz.extend(now("pe", "act", "dve"))
                t_pz.append(dma("cnt", CNT[:, :, :], A["k_cnt"].to_broadcast([128, 4, S]), list(t_pz), eng="pool"))
                t_pz.append(dve(lambda e: e.memset(PZ[:, :, 0:16], 0.0), t_pz))
                banks.only(0, 1, 2, 6)
                linear("pz", 2, list(four), hx, pz_evac)
            flush()
            d_turn(s)
            if s < 14:
                d_scores(s + 2)
            d_values(s)
        banks.only(*range(8))

        YH = sb([128, 4, S], F32R, AR + 33 * KB)
        YL = sb([128, 4, S], F32R, AR + 41 * KB)
        MH = [sb([128, S], F32R, AR + (49 + 2 * j) * KB) for j in range(8)]
        ML = [sb([128, S], F32R, AR + (9 + 2 * j) * KB) for j in range(8)]
        GA = [sb([128, S], F32, AR + (25 + 2 * n) * KB) for n in range(4)]
        t_att = now("pe", "dve", "act")
        ga_rel = [None] * 4
        y_tok, m_tok = {}, {}

        def pool_out():
            it = use("pw")
            for g in range(4):
                b = banks.take()
                t = mm3(PS[:, b, :], it["hi"][:, g, :], it["lo"][:, g, :], DH[:, g, :], DL[:, g, :], True, True,
                        [it["ready"], d_tok[g], banks.rel[b]], True)
                i, tm, rel = take_tmp()
                t1 = dve(lambda e, g=g, b=b, tm=tm: e.tensor_scalar(tm[:, :], PS[:, b, :], col("pool_scale", g), None,
                                                                    ALU.mult), t, rel)
                banks.rel[b] = t1
                y_tok[g] = two_parts(YH[:, g, :], YL[:, g, :], tm[:, :], t1, t_att)
                tmps.rel[i] = y_tok[g]
            done(it, t)
            return now("pe", "dve", "act")

        t_pool = pool_out()
        for n2 in range(2):
            g_tok, a_tok, gp = {}, {}, {}

            def ga_evac(n, o, t, cs):
                g_tok[n] = act(lambda e: e.activation(GA[n][:, :], o, ACT.Sigmoid), t, t_pool, ga_rel[n])
                return g_tok[n]

            def ba_evac(n, o, t, cs):
                a_tok[n] = dve(lambda e: e.tensor_tensor(GA[n][:, :], GA[n][:, :], o, ALU.mult), t, g_tok[n])
                return a_tok[n]

            def gp_evac(n, o, t, cs):
                i, tm, rel = take_tmp()
                ta = act(lambda e: e.activation(tm[:, :], o, ACT.Sigmoid), t, rel)
                gp[n] = (i, tm, ta)
                return ta

            def bp_evac(n, o, t, cs, n2=n2):
                j = 4 * n2 + n
                i, tm, ta = gp[n]
                t1 = dve(lambda e: e.tensor_tensor(tm[:, :], tm[:, :], o, ALU.mult), t, ta)
                t2 = dve(lambda e: e.tensor_tensor(tm[:, :], tm[:, :], GA[n][:, :], ALU.add), t1, a_tok[n])
                ga_rel[n] = t2
                m_tok[j] = two_parts(MH[j][:, :], ML[j][:, :], tm[:, :], t2, t_pool)
                tmps.rel[i] = m_tok[j]
                return t1

            linear("ga", 2, list(four), hx, ga_evac)
            linear("ba", 1, list(four), lambda k, n, cs: (OHI[k][:, :], OLO[k][:, :], do_tok[k]), ba_evac)
            linear("gp", 2, list(four), hx, gp_evac)
            linear("bp", 1, list(four), lambda k, n, cs: (YH[:, k, :], YL[:, k, :], y_tok[k]), bp_evac)
        ssq_rel[:] = r_rel[:] = h_rel[:] = now("pe") * 2

        def m_x(k, n, cs):
            return MH[k][:, cs], ML[k][:, cs], m_tok[k]

        norm = plain_norm("ffn2_norm")
        for n2 in range(2):
            linear("out", 2, list(four), m_x, lambda n, o, t, cs: add_x(4 * n2 + n, o, 1.0, t, None, cs),
                   **(closing(norm) if n2 else {}))

        OUT = sb([128, 4, D], F32, AR + 32 * KB)

        def last_norm(hf):
            cs = HALF[hf]
            t_r = rstd(D, cs)
            for j in range(8):
                x_tok[j][hf] = dve(lambda e, j=j: e.scalar_tensor_tensor(X[:, j, cs], X[:, j, cs],
                                                                         col("final_norm", j), RT[:, cs], ALU.mult,
                                                                         ALU.mult), t_r, x_tok[j][hf], ssq_t[hf])

        glu(norm, last_norm)

        for hf in range(2):
            if hf:
                last_norm(1)
            for t4 in (2 * hf, 2 * hf + 1):
                t_o = []
                for jb in range(2):
                    b = banks.take()
                    for jj in range(4):
                        t = pe(lambda e, b=b, t4=t4, jj=jj, j=4 * jb + jj: e.transpose(
                            PS[:, b, jj * 128:jj * 128 + 128], X[:, j, t4 * 128:t4 * 128 + 128], ident),
                            x_tok[4 * jb + jj][hf], banks.rel[b], sig=(jj == 3))
                    dst = OUT[:, t4, 512 * jb:512 * jb + 512]
                    if jb:
                        t = dve(lambda e, b=b, dst=dst: e.tensor_copy(dst, PS[:, b, :]), t, hid_rel[1])
                    else:
                        t = act(lambda e, b=b, dst=dst: e.activation(dst, PS[:, b, :], ACT.Copy), t, hid_rel[1])
                    banks.rel[b] = t
                    t_o.append(t)
                t_out = dma("out", out[0, 128 * t4:128 * t4 + 128, :], OUT[:, t4, :], t_o)
        assert state["split"] == len(plan) and not late and not later

        sems = {s: ctx.enter_context(nc.semaphore(f"s_{s}")) for s in Q.n}
        block = ctx.enter_context(nc.Block())

        @block.sync
        def _(e):
            Q.play("sp", e, sems)
            e.wait_ge(sems[t_out[0]], t_out[1])

        @block.scalar
        def _(e):
            Q.play("act", e, sems)

        @block.vector
        def _(e):
            Q.play("dve", e, sems)

        @block.tensor
        def _(e):
            Q.play("pe", e, sems)

        @block.gpsimd
        def _(e):
            Q.play("pool", e, sems)


_INS = ['x', 'c', 'positions', 'w_ada', 'b_ada', 'g_mix', 'g_mlp', 'mla_w_dq', 'mla_g_q', 'mla_w_uq', 'mla_w_dkv',
        'mla_g_kv', 'mla_w_ukv', 'mla_w_o', 'swa_w_qkv', 'swa_b_qkv', 'swa_sinks', 'swa_w_o', 'swa_b_o', 'w_ff1',
        'w_ff2', 'g_final', 'ffn1_norm_2', 'ffn1_w1_2', 'ffn1_w3_2', 'ffn1_w2_2', 'mix_norm_2', 'w_in_2',
        'w_branch_attn_2', 'w_branch_pool_2', 'pool_w_2', 'pool_scale_2', 'w_out_2', 'ffn2_norm_2', 'ffn2_w1_2',
        'ffn2_w3_2', 'ffn2_w2_2', 'final_norm_2']


def shape_constants():
    import numpy as np

    f = np.float32
    NEG = f(-2.0e38)
    p = np.arange(128)
    q, k = p[:, None], p[None, :]
    ident = np.eye(128, dtype=f)
    rot = np.zeros((128, 128), f)
    drot = np.zeros((128, 128), f)
    for m in range(128):
        d = m % 64
        rot[m + 32 if d < 32 else m - 32, m] = -1.0 if d < 32 else 1.0
        if d < 8:
            drot[m + 8, m] = -1.0
        elif d < 16:
            drot[m - 8, m] = 1.0
    causal = np.where(k <= q, f(0), NEG).astype(f)
    invf = (f(10000.0) ** (-np.arange(32, dtype=f) / f(32))).astype(f)[p % 32][:, None]
    BIG = f(1.0e37)
    own = np.where(k <= q, q - k, BIG).astype(f)
    prev = np.where(q + 128 - k < 128, q + 128 - k, BIG).astype(f)
    pair = np.concatenate([prev, own], 1)
    first = np.concatenate([own, np.full((128, 128), BIG, f)], 1)
    dist = np.concatenate([first, pair], 1)

    def mask(ok):
        return np.where(ok, f(0), NEG).astype(f)

    m4, m16 = (q - k) % 4 == 0, (q - k) % 16 == 0
    low = k <= q
    dil = np.stack([mask(k >= q), mask(low)] + [mask(m4)] * 3 + [mask(m4 & low)] + [mask(m16)] * 3
                   + [mask(m16 & low)], 1)
    inv = (f(500000.0) ** (-np.arange(0, 16, 2, dtype=f) / f(16))).astype(f)
    ang = (np.arange(512, dtype=f)[None, :] * inv[:, None]).astype(f)
    dcos, dsin = np.ones((128, 512), f), np.zeros((128, 512), f)
    for m in range(128):
        if m % 64 < 16:
            dcos[m] = np.cos(ang[m % 8])
            dsin[m] = np.sin(ang[m % 8])
    cnt = np.stack([f(1) / np.minimum(np.arange(1, 513), w).astype(f) for w in (2, 4, 8, 16)])[None]
    return {"k_const": np.stack([ident, causal, rot], 1), "k_invf": invf,
            "k_dist": dist, "k_dil": dil, "k_dcos": dcos, "k_dsin": dsin, "k_drot": drot, "k_cnt": cnt.astype(f)}


def kernel(**inputs):
    import numpy as _np
    import concourse.bacc as _bacc
    from concourse import mybir as _mybir
    from concourse.bass_utils import run_bass_kernel_spmd as _run

    nc = _bacc.Bacc("TRN2", target_bir_lowering=False, num_devices=1)
    arrays, aps = {}, {}
    given = {name: _np.ascontiguousarray(inputs[name]) for name in _INS}
    for name, a in {**given, **shape_constants()}.items():
        a = _np.ascontiguousarray(a)
        arrays[f"in_{name}_dram"] = a
        aps[name] = nc.dram_tensor(f"in_{name}_dram", a.shape, _mybir.dt.from_np(a.dtype), kind="ExternalInput").ap()
    out = nc.dram_tensor("out_0_dram", (1, 512, 1024), _mybir.dt.from_np(_np.dtype("float32")),
                         kind="ExternalOutput").ap()
    bass_two_blocks(nc, aps, out)
    r = _run(nc, [arrays], core_ids=[0])
    return r.results[0]["out_0_dram"]
```

```python
import concourse.bass as bass
from concourse import mybir
from contextlib import ExitStack

S = 512
D = 1024
F32 = mybir.dt.float32
F32R = mybir.dt.float32r
I32 = mybir.dt.int32
ALU = mybir.AluOpType
ACT = mybir.ActivationFunctionType
AX = mybir.AxisListType
EPS = 1e-6
KB = 1024
NRAW = 3
NW = 3
NTMP = 5
FULL = slice(0, 512)
HALF = (slice(0, 256), slice(256, 512))


def flat(w):
    if w is None:
        return []
    if isinstance(w, tuple) and w and isinstance(w[0], str):
        return [w]
    return [t for x in w for t in flat(x)]


class Queues:

    def __init__(self):
        self.q = {e: [] for e in ("sp", "act", "dve", "pool", "pe")}
        self.n = {}

    def _add(self, eng, sem, by, fn, waits):
        tok = None
        if sem is not None:
            self.n[sem] = self.n.get(sem, 0) + by
            tok = (sem, self.n[sem])
        self.q[eng].append((flat(waits), fn, sem, by))
        return tok

    def act(self, fn, *waits):
        return self._add("act", "act", 1, fn, waits)

    def dve(self, fn, *waits):
        return self._add("dve", "dve", 1, fn, waits)

    def pe(self, fn, *waits, sig=False):
        return self._add("pe", "pe" if sig else None, 1, fn, waits)

    def pool(self, fn, *waits):
        return self._add("pool", "pool", 1, fn, waits)

    def dma(self, sem, out, in_, *waits, eng="sp"):
        return self._add(eng, sem, 16, lambda e: e.dma_start(out, in_), waits)

    def now(self, *engs):
        return [(e, self.n[e]) for e in engs]

    def play(self, eng, engine, sems):
        seen = {}
        for waits, fn, sem, by in self.q[eng]:
            for s, v in waits:
                if seen.get(s, 0) < v:
                    engine.wait_ge(sems[s], v)
                    seen[s] = v
            ins = fn(engine)
            if sem is not None:
                ins.then_inc(sems[sem], by)


class Ring:

    def __init__(self, n):
        self.ids, self.at, self.rel, self.busy = list(range(n)), 0, [None] * n, set()

    def only(self, *ids):
        self.ids, self.at = list(ids), 0

    def next(self):
        return self.ids[self.at % len(self.ids)]

    def take(self):
        for _ in self.ids:
            i = self.next()
            self.at += 1
            if i not in self.busy:
                return i
        assert False, "no slot is free"


def bass_two_blocks(nc, A, out):
    Q = Queues()
    act, dve, pe, pool, dma, now = Q.act, Q.dve, Q.pe, Q.pool, Q.dma, Q.now

    ctx = ExitStack()
    with ctx:
        base = -(-nc.sbuf_base // 64) * 64
        at = [base]

        def place(nbytes):
            o = at[0]
            at[0] += nbytes
            return o

        names = [0]

        def sb(shape, dt, offset):
            names[0] += 1
            return nc.alloc_sbuf_tensor_at(f"t{names[0]}", shape, dt, offset=offset)

        o_raw = place(NRAW * 8 * KB)
        o_hi = place(NW * 8 * KB)
        o_lo = place(NW * 8 * KB)
        o_x = place(16 * KB)
        o_h = place(32 * KB)
        AR = place(66 * KB + 512)
        o_tmp = place(NTMP * 2 * KB)
        o_r = place(2 * KB)
        o_ssq = place(2 * KB)
        o_acc = place(4 * KB)
        o_c = place(4 * 512)
        o_v = place(120 * 4)
        o_mod = place(2 * 48 * 4)
        o_gs = place(4 * 8 * 4)
        o_st = place(96 * 4)
        assert at[0] <= nc.sbuf_usable_end, at[0]

        RAW = [sb([128, 2048], F32, o_raw + i * 8 * KB) for i in range(NRAW)]
        WHI = [sb([128, 2048], F32R, o_hi + i * 8 * KB) for i in range(NW)]
        WLO = [sb([128, 2048], F32R, o_lo + i * 8 * KB) for i in range(NW)]
        X = sb([128, 8, S], F32, o_x)
        HHI = sb([128, 8, S], F32R, o_h)
        HLO = sb([128, 8, S], F32R, o_h + 16 * KB)
        TMP = [sb([128, S], F32, o_tmp + i * 2 * KB) for i in range(NTMP)]
        TMPR = [sb([128, S], F32R, o_tmp + i * 2 * KB) for i in range(NTMP)]
        RT = sb([128, S], F32, o_r)
        SSQ = sb([128, S], F32, o_ssq)
        ACC = sb([128, D], F32, o_acc)
        ACCR = sb([128, D], F32R, o_acc)
        CONST = sb([128, 3, 128], F32, o_c)
        ident, causal, rot = CONST[:, 0, :], CONST[:, 1, :], CONST[:, 2, :]
        ONESR = sb([128, 128], F32R, o_c + 3 * 512)
        ones = ONESR[:, :].bitcast(F32)
        VEC = sb([128, 116], F32, o_v)
        MOD = sb([128, 2, 48], F32, o_mod)
        GS = sb([128, 4, 8], F32, o_gs)
        ST = sb([128, 64], F32, o_st)
        RS = sb([128, 16], F32, o_st + 80 * 4)

        PS = ctx.enter_context(nc.psum_tensor("PS", [128, 8, 512], F32))

        tmps = Ring(NTMP)
        banks = Ring(8)

        XIN = sb([128, 4, D], F32, AR)
        V1 = sb([115, 128], F32, AR + 16 * KB)
        V2 = sb([96, 128], F32, AR + 17 * KB)
        V0 = sb([8, 128], F32, AR + 18 * KB)
        SC = sb([128, 8], F32, AR + 19 * KB)
        CC = sb([128, 8], F32, AR + 19 * KB + 64)
        POS = sb([128, S], I32, AR + 20 * KB)
        PA = sb([128, S], F32, AR + 22 * KB)
        PB = sb([128, S], F32, AR + 24 * KB)
        PC = sb([128, S], F32, AR + 26 * KB)
        PD = sb([128, S], F32, AR + 28 * KB)
        COS = sb([128, S], F32, AR + 62 * KB)
        SIN = sb([128, S], F32, AR + 64 * KB)

        t_c = dma("c", V0[:, :], A["c"].rearrange("b (j p) -> (b j) p", p=128))
        t_const = dma("const", CONST[:, 0:3, :], A["k_const"])
        t_x = dma("x", XIN[:, :, :], A["x"].rearrange("b (t p) d -> p (b t) d", p=128))

        rows = {}
        r = 0
        for name, ap, k in (
            ("c", None, 8),
            ("g_mix", A["g_mix"].rearrange("l (j p) -> (l j) p", p=128), 16),
            ("g_mlp", A["g_mlp"].rearrange("l (j p) -> (l j) p", p=128), 16),
            ("g_q", A["mla_g_q"].rearrange("l (j p) -> (l j) p", p=128), 3),
            ("g_kv", A["mla_g_kv"].rearrange("l (j p) -> (l j) p", p=128), 2),
            ("g_final", A["g_final"].rearrange("(j p) -> j p", p=128), 8),
            ("ffn1_norm", A["ffn1_norm_2"].rearrange("l (j p) -> (l j) p", p=128), 8),
            ("mix_norm", A["mix_norm_2"].rearrange("l (j p) -> (l j) p", p=128), 8),
            ("ffn2_norm", A["ffn2_norm_2"].rearrange("l (j p) -> (l j) p", p=128), 8),
            ("final_norm", A["final_norm_2"].rearrange("(j p) -> j p", p=128), 8),
            ("pool_scale", A["pool_scale_2"].rearrange("l (j p) -> (l j) p", p=128), 4),
            ("bq", A["swa_b_qkv"][:, 0:1024].rearrange("l (h d) -> (l h) d", d=64), 16),
            ("bk", A["swa_b_qkv"][:, 1024:1280].rearrange("l (j p) -> (l j) p", p=128), 2),
            ("b_o", A["swa_b_o"].rearrange("l (j p) -> (l j) p", p=128), 8),
        ):
            rows[name] = r
            if name == "c":
                ap = A["c"].rearrange("b (j p) -> (b j) p", p=128)
            if name == "bq":
                dma("vec", V1[r:r + k, 0:64], ap, eng="act")
                dma("vec", V1[r:r + k, 64:128], ap, eng="act")
            else:
                dma("vec", V1[r:r + k, :], ap, eng="act")
            r += k
        assert r == 115
        dma("vec", V2[:, :], A["b_ada"].rearrange("l (j p) -> (l j) p", p=128), eng="act")
        dma("vec", VEC[:, 115:116], A["k_invf"], eng="act")
        t_vec = dma("vec", POS[:, :], A["positions"].to_broadcast([128, S]), eng="act")

        def col(name, j=0, k=1):
            return VEC[:, rows[name] + j:rows[name] + j + k]

        invf = VEC[:, 115:116]
        SILUC = sb([128, 8], F32, o_st + 64 * 4)
        SUMS = sb([128, 8], F32, o_st + 72 * 4)

        b = banks.take()
        t = pe(lambda e, b=b: e.transpose(PS[:, b, 0:8], V0[:, :], ident[0:8, 0:8]), t_c, t_const, sig=True)
        t_e = act(lambda e, b=b: e.activation(SC[:, :], PS[:, b, 0:8], ACT.Exp, scale=-1.0), t)
        t = dve(lambda e: e.tensor_scalar(CC[:, :], SC[:, :], 1.0, None, ALU.add), t_e)
        t = dve(lambda e: e.reciprocal(SC[:, :], CC[:, :]), t)
        t_silu = dve(lambda e, b=b: e.tensor_tensor(SILUC[:, :], PS[:, b, 0:8], SC[:, :], ALU.mult), t)
        banks.rel[b] = [t_e, t_silu]
        t = dve(lambda e: e.memset(TMP[0][:, 0:128], 1.0))
        t_ones = dve(lambda e: e.tensor_copy(ONESR[:, :], TMP[0][:, 0:128]), t)
        tmps.rel[0] = t_ones

        raw_ring = Ring(NRAW)
        w_ring = Ring(NW)
        plan = []
        state = {"loaded": 0, "split": 0, "used": 0, "uses": 0, "reach": 4}
        late = []
        t_cols = []
        mod_tok = {}
        mod_used = {}
        acc_rel = [None]

        def weight(name, ap, kt, ncol, parts=None):
            plan.append(dict(kind="w", name=name, ap=ap, kt=kt, nc=ncol, parts=parts))

        def ada(l, v, kind="a"):
            w = A["w_ada"][l].rearrange("(k p) n -> p k n", p=128)
            for u in range(4):
                plan.append(dict(kind=kind, l=l, v=v, u=u, kt=2, nc=D,
                                 ap=w[:, 2 * u:2 * u + 2, v * D:(v + 1) * D]))

        def load():
            it = plan[state["loaded"]]
            state["loaded"] += 1
            i = raw_ring.take()
            it["raw"] = i
            n = it["kt"] * it["nc"]
            it["rawv"] = RAW[i][:, 0:n].rearrange("p (k n) -> p k n", k=it["kt"])
            ap, dst = it["ap"], it["rawv"]
            pieces = [(dst, ap)]
            if it.get("split3"):
                pieces = [(dst[:, :, 128 * g:128 * g + 128], ap[:, :, g, :]) for g in range(3)]
            for dst, ap in pieces:
                it["landed"] = dma(f"raw{i}", dst, ap, raw_ring.rel[i])

        def take_tmp():
            for _ in range(NTMP):
                i = tmps.take()
                if tmps.rel[i] != "held":
                    break
            rel, tmps.rel[i] = tmps.rel[i], "held"
            assert rel != "held"
            return i, TMP[i], rel

        def begin_mod(l, v, t_acc):
            held = []
            for hf in range(2):
                cs = slice(512 * hf, 512 * hf + 512)
                i, _, rel = take_tmp()
                th = act(lambda e, i=i, cs=cs: e.activation(TMPR[i][:, :], ACC[:, cs], ACT.Copy), t_acc, rel)
                tl = dve(lambda e, i=i, cs=cs: e.tensor_tensor(ACCR[:, cs], ACC[:, cs], TMPR[i][:, :].bitcast(F32),
                                                               ALU.subtract), th)
                held.append((i, cs, th, tl))
            late.append((state["uses"] + 2, lambda: end_mod(l, v, held)))

        def end_mod(l, v, held):
            dst = MOD[:, l, v * 8:v * 8 + 8]
            freed = []
            for hf, (i, cs, th, tl) in enumerate(held):
                b = banks.take()
                pe(lambda e, i=i, b=b: e.matmul(PS[:, b, :], ONESR[:, :], TMPR[i][:, :], start=True, stop=False),
                   th, t_ones, banks.rel[b])
                t = pe(lambda e, b=b, cs=cs: e.matmul(PS[:, b, :], ONESR[:, :], ACCR[:, cs], start=False, stop=True),
                       tl, sig=True)
                tmps.rel[i] = t
                freed.append(t)
                sq = PS[:, b, :].rearrange("p (j c) -> p j c", c=128)
                t = dve(lambda e, sq=sq: e.tensor_tensor(sq, sq, ident.unsqueeze(1).to_broadcast([128, 4, 128]),
                                                         ALU.mult), t)
                t = dve(lambda e, sq=sq, hf=hf: e.tensor_reduce(SUMS[:, 4 * hf:4 * hf + 4], sq, AX.X, ALU.add), t)
                banks.rel[b] = t
            acc_rel[0] = freed
            t = dve(lambda e: e.tensor_tensor(dst, dst, SUMS[:, :], ALU.add), t, t_cols)
            if v in (1, 4):
                which = 2 * l + (v == 4)
                g = col("g_mix" if v == 1 else "g_mlp", 8 * l, 8)
                t = dve(lambda e: e.scalar_tensor_tensor(GS[:, which, :], dst, 1.0, g, ALU.add, ALU.mult), t, t_cols)
            mod_tok[(l, v)] = t

        def settle(everything=False):
            while late and (everything or late[0][0] <= state["uses"]):
                late.pop(0)[1]()

        row_banks, low_part = [], []

        def turn_row(l, v, t_row):
            b = banks.take()
            for hf in range(2):
                i, tm, rel = take_tmp()
                ta = act(lambda e, hf=hf, tm=tm: e.activation(tm[0:1, :], PS[0:1, row_banks[hf], :], ACT.Copy), t_row,
                         rel)
                for j in range(4):
                    t = pe(lambda e, j=j, hf=hf, tm=tm: e.matmul(
                        PS[:, b, 4 * hf + j:4 * hf + j + 1], tm[0:1, 128 * j:128 * j + 128], ones[0:1, 0:1],
                        start=True, stop=True), ta, t_ones, banks.rel[b], sig=(j == 3))
                tmps.rel[i] = t
                banks.rel[row_banks[hf]] = ta
                banks.busy.discard(row_banks[hf])
            dst = MOD[:, l, v * 8:v * 8 + 8]
            t = dve(lambda e: e.tensor_tensor(dst, PS[:, b, 0:8], dst, ALU.add), t, t_cols)
            banks.rel[b] = t
            mod_tok[(l, v)] = t

        def settle_low():
            if low_part:
                low_part.pop(0)()

        def split(later=False):
            settle_low()
            it = plan[state["split"]]
            state["split"] += 1
            raw = it["rawv"]
            if it["kind"] == "a":
                t = it.get("prev")
                for kk in range(2):
                    k = 2 * it["u"] + kk
                    c = SILUC[:, k:k + 1]
                    if k == 0:
                        settle(True)
                        t = dve(lambda e, kk=kk, c=c: e.tensor_scalar(ACC[:, :], raw[:, kk, :], c, None, ALU.mult),
                                it["landed"], acc_rel[0], t_silu)
                    else:
                        t = dve(lambda e, kk=kk, c=c: e.scalar_tensor_tensor(ACC[:, :], raw[:, kk, :], c, ACC[:, :],
                                                                             ALU.mult, ALU.add),
                                it["landed"], state["acc"])
                    state["acc"] = t
                raw_ring.rel[it["raw"]] = t
                if it["u"] == 3:
                    late.append((state["uses"], lambda l=it["l"], v=it["v"], t=t: begin_mod(l, v, t)))
            elif it["kind"] == "p":
                for kk in range(2):
                    k = 2 * it["u"] + kk
                    for hf in range(2):
                        if k == 0:
                            row_banks.append(banks.take())
                            banks.busy.add(row_banks[hf])
                        t = pe(lambda e, k=k, kk=kk, hf=hf: e.matmul(
                            PS[0:1, row_banks[hf], :], SILUC[:, k:k + 1], raw[:, kk, 512 * hf:512 * hf + 512],
                            start=(k == 0), stop=(k == 7)), it["landed"], t_silu, banks.rel[row_banks[hf]], sig=True)
                raw_ring.rel[it["raw"]] = t
                if it["u"] == 3:
                    late.append((0, lambda l=it["l"], v=it["v"], t=t: turn_row(l, v, t)))
            else:
                i = w_ring.take()
                it["slot"] = i
                width = it.get("wide", it["nc"])
                parts = it["parts"] or [(lambda w: w, lambda w: w)]
                wd = it["wd"] = it["kt"] * width
                hi = WHI[i][:, 0:wd].rearrange("p (k n) -> p k n", k=it["kt"])
                lo = WLO[i][:, 0:wd].rearrange("p (k n) -> p k n", k=it["kt"])
                it["hi"], it["lo"] = hi, lo
                th, tl = [], []
                for dst, src in parts:
                    th.append(act(lambda e, d=dst(hi), s=src(raw): e.activation(d, s, ACT.Copy),
                                  it["landed"], w_ring.rel[i]))
                w_ring.rel[i] = "held"

                def low():
                    for (dst, src), t in zip(parts, th):
                        tl.append(dve(lambda e, d=dst(lo), h=dst(hi), s=src(raw):
                                      e.tensor_tensor(d, s, h.bitcast(F32), ALU.subtract), it["landed"], t))
                    it["ready"] = [th[-1], tl[-1]]
                    raw_ring.rel[it["raw"]] = [th[-1], tl[-1]]
                    if state["loaded"] < len(plan):
                        load()

                if later:
                    low_part.append(low)
                else:
                    low()
                return
            if state["loaded"] < len(plan):
                load()

        def use(name, most=9):
            k = state["used"]
            while plan[k]["kind"] != "w":
                k += 1
            it = plan[k]
            assert it["name"] == name, (it["name"], name)
            state["used"] = k + 1
            settle_low()
            state["uses"] += 1
            while state["split"] < len(plan) and not (most == 0 and "ready" in it):
                nxt = plan[state["split"]]
                if nxt["kind"] == "w" and w_ring.rel[w_ring.next()] == "held":
                    break
                if nxt["kind"] == "a" and state["split"] > k + state["reach"]:
                    break
                split()
                most -= 1
                if most == 0 and "ready" in it:
                    break
            assert "ready" in it
            return it

        def ahead(later=False):
            if low_part:
                return settle_low()
            if late and state["reach"] == 0:
                late.pop(0)[1]()
            if state["split"] < len(plan):
                it = plan[state["split"]]
                if (it["u"] or not late) if it["kind"] == "a" else w_ring.rel[w_ring.next()] != "held":
                    split(later)

        def done(it, t):
            w_ring.rel[it["slot"]] = t
            settle()

        wt = lambda ap: ap.rearrange("(k p) n -> p k n", p=128)
        w_dq, w_dkv = wt(A["mla_w_dq"][0]), wt(A["mla_w_dkv"][0])
        w_uq, w_ukv, w_mo = wt(A["mla_w_uq"][0]), wt(A["mla_w_ukv"][0]), wt(A["mla_w_o"][0])
        w_qkv, w_so = wt(A["swa_w_qkv"][0]), wt(A["swa_w_o"][0])
        w_in, w_out = wt(A["w_in_2"][0]), wt(A["w_out_2"][0])
        w_ba, w_bp = wt(A["w_branch_attn_2"][0]), wt(A["w_branch_pool_2"][0])
        w_pool = A["pool_w_2"][0].rearrange("g c d -> c g d")

        ada(0, 1)
        ada(0, 0, "p")
        for a in range(2):
            weight("dq", w_dq[:, 4 * a:4 * a + 4, :], 4, 384)
        dkv_parts = [(lambda w: w[:, :, 0:320], lambda w: w), (lambda w: w[:, :, 320:384], lambda w: w[:, :, 256:320])]
        for a in range(2):
            weight("dkv", w_dkv[:, 4 * a:4 * a + 4, :], 4, 320, dkv_parts)
            plan[-1]["wide"] = 384

        def uq_nope(w):
            return w[:, :, 0:256].rearrange("p k (h c) -> p k h c", h=2)

        def uq_rope(w):
            return w[:, :, 256:384].rearrange("p k (h c) -> p k h c", h=2)

        uq_parts = [(uq_nope, lambda w: w.rearrange("p k (h c) -> p k h c", h=2)[:, :, :, 0:128]),
                    (uq_rope, lambda w: w.rearrange("p k (h c) -> p k h c", h=2)[:, :, :, 128:192])]

        def uq_plan(a):
            weight("uq", w_uq[:, :, 384 * a:384 * a + 384], 3, 384, uq_parts)

        def square(name, w, cols=2, per=512, ks=(4, 4), k0=0):
            for n in range(cols):
                k = k0
                for kt in ks:
                    weight(name, w[:, k:k + kt, n * per:(n + 1) * per], kt, per)
                    k += kt

        uq_plan(0)
        uq_plan(1)
        for a in range(2):
            weight("ukv", w_ukv[:, :, 1024 * a:1024 * a + 1024], 2, 1024)
        uq_plan(2)
        uq_plan(3)
        ada(0, 2)
        square("mo", w_mo, cols=1, ks=(4,))
        ada(0, 4)
        square("mo", w_mo, cols=1, ks=(4,), k0=4)
        ada(0, 3)
        square("mo", w_mo[:, :, 512:1024], cols=1)
        pend = [(0, 5), (1, 1), (1, 0), (1, 2), (1, 4), (1, 3), (1, 5)]

        def ff_plan(l, extra):
            w1, w2 = wt(A["w_ff1"][l]), wt(A["w_ff2"][l])

            def up(q):
                square(f"up{l}", w1[:, :, 1024 * q:1024 * q + 1024])

            def down(q):
                square(f"down{l}", w2, k0=8 * q)

            up(0)
            for q in range(4):
                if extra:
                    ada(*extra.pop(0))
                if q < 3:
                    up(q + 1)
                if extra:
                    ada(*extra.pop(0))
                down(q)

        ff_plan(0, pend)
        assert not pend

        for n in (0, 2, 1):
            for a in range(2):
                weight("qkv", w_qkv[:, 4 * a:4 * a + 4, 512 * n:512 * n + 512], 4, 512)
        square("so", w_so)
        ff_plan(1, [])

        def glu_plan(w1, w3, w2):
            w1, w3, w2 = wt(w1), wt(w3), wt(w2)

            def up(blk):
                for g in ((0, 4), (4, 8), (8, 11))[blk:blk + 1]:
                    for c in range(*g):
                        weight("w1", w1[:, :, 256 * c:256 * c + 256], 8, 256)
                        weight("w3", w3[:, :, 256 * c:256 * c + 256], 8, 256)

            def down(blk):
                square("w2", w2, ks=((4, 4), (4, 4), (3, 3))[blk], k0=8 * blk)

            up(0)
            for blk in range(3):
                if blk < 2:
                    up(blk + 1)
                down(blk)

        glu_plan(A["ffn1_w1_2"][0], A["ffn1_w3_2"][0], A["ffn1_w2_2"][0])

        def qk_plan(a):
            for c in (768, 0):
                w = w_in[:, :, c:c + 768].rearrange("p k (g a c) -> p k g a c", a=2, c=128)
                for u in range(2):
                    weight("qk", w[:, 4 * u:4 * u + 4, :, a, :], 4, 384)
                    plan[-1]["split3"] = True

        square("v", w_in[:, :, 1536:2048], cols=1)
        qk_plan(0)
        weight("v2", w_in[:, :, 2048:2304], 8, 256)
        qk_plan(1)
        for n in range(2):
            weight("pz", w_in[:, :, 2304 + 256 * n:2560 + 256 * n], 8, 256)
        for n in range(2):
            square("ga", w_in[:, :, 2816 + 512 * n:3328 + 512 * n], cols=1)
            if n == 0:
                weight("pw", w_pool, 4, 128)
            weight("ba", w_ba[:, :, 512 * n:512 * n + 512], 2, 512)
            square("gp", w_in[:, :, 3840 + 512 * n:4352 + 512 * n], cols=1)
            weight("bp", w_bp[:, :, 512 * n:512 * n + 512], 4, 512)
        square("out", w_out)
        glu_plan(A["ffn2_w1_2"][0], A["ffn2_w3_2"][0], A["ffn2_w2_2"][0])

        for _ in range(NRAW):
            load()

        later = []

        def flush():
            work, later[:] = later[:], []
            for go in work:
                go()

        def flush_all():
            while later:
                flush()

        def hs(cs):
            return [i for i in range(2) if cs == FULL or cs == HALF[i]]

        def mm3(o, wh, wl, xh, xl, first, last, waits, sig):
            pe(lambda e: e.matmul(o, wh, xh, start=first, stop=False), waits)
            pe(lambda e: e.matmul(o, wh, xl, start=False, stop=False))
            return pe(lambda e: e.matmul(o, wl, xh, start=False, stop=last), sig=sig)

        def linear(name, nunits, outs, xs, evac, swap=False, halves=False, mid=None, frees_h=False, first=None):
            its = []
            parts = HALF if halves else (FULL,)
            for hf, cs in enumerate(parts):
                tiles = [n for n in range(len(outs)) if not (swap and halves) or n // 2 == hf]
                bk = {}
                for n in tiles:
                    bk[n] = banks.take()
                    banks.busy.add(bk[n])
                k0 = 0
                for u in range(nunits):
                    if hf == 0:
                        if first and u == 0:
                            first()
                        its.append(use(name, 0 if first and u == 0 else 9))
                    it = its[u]
                    last_unit = u == nunits - 1
                    for n in tiles:
                        c, w = outs[n]
                        o = PS[:, bk[n], 0:w] if swap else PS[:, bk[n], cs]
                        for k in range(it["kt"]):
                            xh, xl, tx = xs(k0 + k, n, cs)
                            wh, wl = it["hi"][:, k, c:c + w], it["lo"][:, k, c:c + w]
                            end = k == it["kt"] - 1
                            waits = [it["ready"], tx, banks.rel[bk[n]] if u == 0 and k == 0 else None]
                            sig = end and (last_unit or n == tiles[-1])
                            first, last = u == 0 and k == 0, last_unit and end
                            if swap:
                                t = mm3(o, xh, xl, wh, wl, first, last, waits, sig)
                            else:
                                t = mm3(o, wh, wl, xh, xl, first, last, waits, sig)
                        flush()
                        if last_unit:
                            banks.rel[bk[n]] = evac(n, o, t, cs)
                            banks.busy.discard(bk[n])
                        if mid and (hf, u, n) in mid:
                            mid[(hf, u, n)]()
                        if last_unit and n == tiles[-1] and frees_h:
                            for i in hs(cs):
                                h_rel[i] = t
                    k0 += it["kt"]
                    if hf == len(parts) - 1:
                        done(it, t)

        x_tok = [[None, None] for _ in range(8)]
        h_tok = [[None, None] for _ in range(8)]
        h_rel = [None, None]
        ssq_rel, ssq_t = [None, None], [None, None]
        ssq2_rel, ssq2_t = [None, None], [None, None]
        r_rel = [None, None]
        SSQ2 = sb([128, S], F32, AR + 64 * KB)

        def x_at(j, cs):
            return [x_tok[j][i] for i in hs(cs)]

        adds = []

        def add_up():
            while adds:
                adds.pop(0)[-1]()

        def sumsq(j, src, t, cs=FULL, acc=SSQ, acc_t=ssq_t, rel_t=ssq_rel, scale=1.0, on=dve):
            if j == 0:
                new = act(lambda e: e.activation(acc[:, cs], src, ACT.Square, scale=scale), t,
                          [rel_t[i] for i in hs(cs)])
                for i in hs(cs):
                    acc_t[i] = new
                return
            i, tm, rel = take_tmp()
            ts = act(lambda e: e.activation(tm[:, cs], src, ACT.Square, scale=scale), t, rel)

            def add():
                new = on(lambda e: e.tensor_tensor(acc[:, cs], acc[:, cs], tm[:, cs], ALU.add), ts,
                          [acc_t[f] for f in hs(cs)])
                tmps.rel[i] = new
                for f in hs(cs):
                    acc_t[f] = new

            adds.append((acc, cs, tm, i, ts, add))

        EPSC = RS[:, 8:9]
        t_eps = dve(lambda e: e.memset(EPSC, EPS))
        rs_rel = [None, None]

        def sums(cs, acc, acc_t, rel_t, b, c):
            mine, hf = None, HALF.index(cs)
            for entry in [entry for entry in adds if entry[0] is acc]:
                adds.remove(entry)
                if entry[1] == cs:
                    mine = entry
                else:
                    entry[-1]()
            for m in range(2):
                ts = slice(cs.start + 128 * m, cs.start + 128 * m + 128)
                o = PS[:, b, c + m:c + m + 1]
                t = pe(lambda e, o=o, ts=ts: e.matmul(o, acc[:, ts], ones[:, 0:1], start=True, stop=mine is None),
                       acc_t[hf], t_ones, banks.rel[b], sig=(m == 1))
                if mine:
                    t = pe(lambda e, o=o, ts=ts: e.matmul(o, mine[2][:, ts], ones[:, 0:1], start=False, stop=True),
                           mine[4], sig=(m == 1))
            if mine:
                tmps.rel[mine[3]] = t
            acc_t[hf] = rel_t[hf] = t
            return t

        def diagonals(col0, n, t, place=None):
            i, tm, rel = place or take_tmp()
            for m in range(n):
                t = dve(lambda e, m=m: e.tensor_scalar(tm[:, 128 * m:128 * m + 128], ident,
                                                       RS[:, col0 + m:col0 + m + 1], None, ALU.mult), t, t_const, rel)
            return i, tm, t

        def spread(o, tm, c, t, *after):
            return pe(lambda e: e.matmul(o, ones, tm[:, c:c + 256], start=True, stop=True), t, t_ones, after, sig=True)

        def hold():
            b = banks.take()
            banks.busy.add(b)
            return dict(R=PS[:, b, :], b=b, rel=[None, None], t=[])

        def let_go(r):
            banks.rel[r["b"]] = r["rel"]
            banks.busy.discard(r["b"])

        def rstd(n, cs, r=None, place=None):
            hf = HALF.index(cs)
            b = banks.take()
            t = sums(cs, SSQ, ssq_t, ssq_rel, b, 0)
            v = RS[:, 4 * hf:4 * hf + 2]
            t = banks.rel[b] = act(lambda e: e.activation(v, PS[:, b, 0:2], ACT.Sqrt, bias=EPSC, scale=1.0 / n), t, t_eps,
                                   rs_rel[hf])
            t = dve(lambda e: e.reciprocal(v, v), t)
            i, tm, t = diagonals(4 * hf, 2, t, place and place[hf])
            rs_rel[hf] = t

            def second():
                at = r or hold()
                at["t"].append(spread(at["R"][:, cs], tm, 0, t, banks.rel[at["b"]]))
                if not place:
                    tmps.rel[i] = at["t"][-1]
                return at

            return second

        def normed(cs, gain, shift, r, t_mod, chunks=range(8)):
            held = {}
            R, t_r, rel = r["R"], r["t"], r["rel"]
            after = [h_rel[i] for i in hs(cs)]
            for j in range(chunks.start, chunks.stop + 1):
                if j < chunks.stop:
                    i, tm, free = take_tmp()
                    t = dve(lambda e, j=j, tm=tm: e.scalar_tensor_tensor(tm[:, cs], X[:, j, cs], gain(j), R[:, cs],
                                                                         ALU.mult, ALU.mult), free, t_r, x_at(j, cs),
                            t_mod)
                    if shift is None:
                        th = act(lambda e, j=j, tm=tm: e.activation(HHI[:, j, cs], tm[:, cs], ACT.Copy), t, after)
                    else:
                        th = act(lambda e, j=j, tm=tm: e.activation(HHI[:, j, cs], tm[:, cs], ACT.Identity,
                                                                    bias=shift(j)), t, after, t_mod)
                    held[j] = (i, tm, t, th)
                    for i in hs(cs):
                        rel[i] = t
                if j > chunks.start:
                    p = j - 1
                    i, tm, t, th = held.pop(p)
                    if shift is None:
                        tl = (pool if p % 2 else dve)(lambda e, p=p, tm=tm: e.tensor_tensor(HLO[:, p, cs], tm[:, cs],
                                                                       HHI[:, p, cs].bitcast(F32), ALU.subtract),
                                 t, th, after)
                    else:
                        tl = dve(lambda e, p=p, tm=tm: e.scalar_tensor_tensor(HLO[:, p, cs], tm[:, cs], shift(p),
                                                                              HHI[:, p, cs].bitcast(F32), ALU.add,
                                                                              ALU.subtract), t, th, after)
                    tmps.rel[i] = [th, tl]
                    for i in hs(cs):
                        h_tok[p][i] = [th, tl]

        def modulation(l, v):
            while not ((l, v) in mod_tok and (l, v + 1) in mod_tok):
                if late:
                    late.pop(0)[1]()
                else:
                    split()
            return [mod_tok[(l, v)], mod_tok[(l, v + 1)]]

        def in_steps(scale, write):
            rs, ready = [], []

            def go(step):
                kind, hf = step[0], int(step[1])
                if kind == "a":
                    ready.append(scale(hf))
                    return
                if kind == "b":
                    rs.append(ready.pop()())
                write(HALF[hf], rs[-1], {"b0": range(4), "c0": range(4, 8), "b1": range(8)}[step])
                if step != "b0":
                    let_go(rs[-1])

            return go

        def plain_norm(name):
            return in_steps(lambda hf: rstd(D, HALF[hf]),
                            lambda cs, r, chunks: normed(cs, lambda j: col(name, j), None, r, None, chunks))

        def mod_norm(l, part):
            v = 3 * part
            t_mod = modulation(l, v)
            return in_steps(lambda hf: rstd(D, HALF[hf]),
                            lambda cs, r, chunks: normed(cs, lambda j: GS[:, 2 * l + part, j:j + 1],
                                                         lambda j: MOD[:, l, 8 * v + j:8 * v + j + 1], r, t_mod,
                                                         chunks))

        def hx(k, n, cs):
            return HHI[:, k, cs], HLO[:, k, cs], [h_tok[k][i] for i in hs(cs)]

        def hx_tok(k, n, cs):
            ts = slice(n * 128, n * 128 + 128)
            return HHI[:, k, ts], HLO[:, k, ts], h_tok[k][n // 2]

        def two_parts(hi, lo, src, t, *after):
            th = act(lambda e: e.activation(hi, src, ACT.Copy), t, after)
            tl = dve(lambda e: e.tensor_tensor(lo, src, hi.bitcast(F32), ALU.subtract), t, th, after)
            return [th, tl]

        def add_x(j, o, scale, t, t_scale, cs, stats=True):
            t = dve(lambda e: e.scalar_tensor_tensor(X[:, j, cs], o, scale, X[:, j, cs], ALU.mult, ALU.add),
                    t, x_at(j, cs), t_scale)
            for i in hs(cs):
                x_tok[j][i] = t
            add_up()
            if stats:
                sumsq(j, X[:, j, cs], t, cs)
            return t

        four = [(0, 128), (128, 128), (256, 128), (384, 128)]
        three = four[:3]

        def closing(norm):
            return dict(halves=True, mid={(1, 0, 0): lambda: norm("a0"), (1, 0, 2): lambda: norm("b0")})

        def opening(norm, at=2):
            def scales():
                norm("a1")
                ahead()

            return dict(halves=True, first=lambda: norm("c0"), mid={(0, 0, 0): scales, (0, 0, at): lambda: norm("b1")})

        def rotated(o, t, cosv, sinv, rotm, t_tab, then, cs=FULL):
            i, tm, rel = take_tmp()
            ta = act(lambda e: e.activation(tm[:, cs], o, ACT.Copy), t, rel)

            def turn():
                b2 = banks.take()
                banks.busy.add(b2)
                tp = pe(lambda e: e.matmul(PS[:, b2, cs], rotm, tm[:, cs], start=True, stop=True), ta, banks.rel[b2],
                        t_tab, sig=True)
                t1 = pool(lambda e: e.tensor_tensor(tm[:, cs], tm[:, cs], cosv, ALU.mult), ta, tp, t_tab)
                t2 = dve(lambda e: e.tensor_tensor(PS[:, b2, cs], PS[:, b2, cs], sinv, ALU.mult), tp, t_tab)

                def finish():
                    t3 = dve(lambda e: e.tensor_tensor(tm[:, cs], tm[:, cs], PS[:, b2, cs], ALU.add), t1, t2)
                    banks.busy.discard(b2)
                    banks.rel[b2] = t3
                    tmps.rel[i] = then(tm[:, cs], t3, cs)

                later.append(finish)

            later.append(turn)
            return ta

        def stacked(dst, src, e_half, t, *after):
            a, b = slice(64 * e_half, 64 * e_half + 64), slice(64 - 64 * e_half, 128 - 64 * e_half)
            th = act(lambda e: e.activation(dst[a, :], src[a, :], ACT.Copy), t, after)
            tl = dve(lambda e: e.tensor_tensor(dst[b, :], src[a, :], dst[a, :].bitcast(F32), ALU.subtract), t, th,
                     after)
            return [th, tl]

        def doubled(hi, lo, src, e_half, t, *after, both=True):
            a = slice(64 * e_half, 64 * e_half + 64)
            b = slice(64 - 64 * e_half, 128 - 64 * e_half)
            th = act(lambda e: e.activation(hi[a, :], src[a, :], ACT.Copy), t, after)
            out = [th, act(lambda e: e.activation(hi[b, :], src[a, :], ACT.Copy), t, after)]
            for rows in (a, b)[:1 + both]:
                out.append(dve(lambda e, rows=rows: e.tensor_tensor(lo[rows, :], src[a, :], hi[a, :].bitcast(F32),
                                                                    ALU.subtract), t, th, after))
            return out

        def masked_max(P, src, mask, st, t, *waits, first=-3.0e38):
            return dve(lambda e: e.tensor_tensor_reduce(out=P, in0=src, in1=mask, scale=1.0, scalar=first, op0=ALU.add,
                                                        op1=ALU.max, accum_out=st), t, waits)

        for j in range(8):
            b = banks.take()
            for t4 in range(4):
                t = pe(lambda e, j=j, b=b, t4=t4: e.transpose(PS[:, b, t4 * 128:(t4 + 1) * 128],
                                                              XIN[:, t4, j * 128:(j + 1) * 128], ident),
                       t_x, t_const, banks.rel[b] if t4 == 0 else None, sig=(t4 == 3))
            t = act(lambda e, j=j, b=b: e.activation(X[:, j, :], PS[:, b, :], ACT.Copy), t)
            banks.rel[b] = t
            x_tok[j] = [t, t]
            add_up()
            sumsq(j, X[:, j, :], t, on=pool)
            if j % 2:
                split()
        b = banks.take()
        pe(lambda e, b=b: e.transpose(PS[:, b, 0:115], V1[:, :], ident[0:115, 0:115]), t_vec, t_const, banks.rel[b])
        t = pe(lambda e, b=b: e.transpose(PS[:, b, 128:224], V2[:, :], ident[0:96, 0:96]), sig=True)
        t_cols.append(dve(lambda e, b=b: e.tensor_copy(VEC[:, 0:115], PS[:, b, 0:115]), t))
        t_cols.append(dve(lambda e, b=b: e.tensor_copy(MOD[:, :, :].rearrange("p l v -> p (l v)"), PS[:, b, 128:224]), t))
        banks.rel[b] = t_cols[1]
        late.pop(0)[1]()
        split()
        split()
        first_r = [rstd(D, cs) for cs in HALF]
        settle(True)

        TWO_PI = 6.283185307179586
        C1, C2 = 6.28125, 0.0019350051879882812
        C3 = TWO_PI - C1 - C2
        MAGIC = 12582912.0
        t_tab, t_arena = [], []

        def rope_angles():
            t = pool(lambda e: e.tensor_copy(PA[:, :], POS[:, :]), t_vec)
            t_ang = pool(lambda e: e.tensor_scalar(PB[:, :], PA[:, :], invf, None, ALU.mult), t)
            for dst, quarter in ((SIN, 0.0), (COS, 0.25)):
                t = pool(lambda e, quarter=quarter: e.tensor_scalar(PA[:, :], PB[:, :], 1.0 / TWO_PI, quarter, ALU.mult,
                                                                    ALU.add), t_ang)
                t = pool(lambda e: e.tensor_scalar(PC[:, :], PA[:, :], MAGIC, None, ALU.add), t)
                t = pool(lambda e: e.tensor_scalar(PA[:, :], PC[:, :], MAGIC, None, ALU.subtract), t)
                t_n, cur = t, PB
                for c, out in ((C1, PD), (C2, dst), (C3, PD)):
                    t = pool(lambda e, c=c: e.tensor_scalar(PC[:, :], PA[:, :], -c, None, ALU.mult), t)
                    t = pool(lambda e, out=out, cur=cur: e.tensor_tensor(out[:, :], PC[:, :], cur[:, :], ALU.add), t)
                    cur = out
                t = pool(lambda e, quarter=quarter: e.tensor_scalar(PC[:, :], PD[:, :], quarter * TWO_PI, 3.1415925,
                                                                    ALU.add, ALU.min), t)
                t = pool(lambda e, dst=dst: e.tensor_scalar(dst[:, :], PC[:, :], -3.1415925, None, ALU.max), t)
                t_tab.append(t)

        def rope_end():
            angles = list(t_tab)
            t_tab[:] = [act(lambda e, T=T: e.activation(T[:, :], T[:, :], ACT.Sin), angles) for T in (SIN, COS)]
            t_arena.extend(now("pe", "dve", "act", "pool"))

        rope_angles()
        split()
        split()
        t_mod = modulation(0, 0)
        for hf in range(2):
            ahead()
            r = first_r[hf]()
            normed(HALF[hf], lambda j: GS[:, 0, j:j + 1], lambda j: MOD[:, 0, j:j + 1], r, t_mod)
            let_go(r)
        VV = sb([128, 8, 4, 128], F32, AR)
        QNH = sb([128, 4, S], F32R, AR + 16 * KB)
        QNL = sb([128, 4, S], F32R, AR + 24 * KB)
        QRS = sb([128, 4, S], F32R, AR + 32 * KB)
        CQH = sb([128, 3, S], F32R, AR + 40 * KB)
        CQL = sb([128, 3, S], F32R, AR + 46 * KB)
        CKH = sb([128, 2, S], F32R, AR + 52 * KB)
        CKL = sb([128, 2, S], F32R, AR + 56 * KB)
        PBUF = [sb([128, 1280], F32, AR + c * KB) for c in (52, 57, 40, 45)]
        PSLOT = [0, 1, 0, 1, 2, 3, 0, 1]
        PT5 = [sb([128, 256], F32, AR + (50 + i) * KB) for i in range(2)]
        PT4 = [sb([128, S], F32, AR + (62 + 2 * i) * KB) for i in range(2)]
        KRH = sb([128, S], F32R, o_ssq)
        KRL = sb([128, S], F32R, o_r)

        def low_rank(n, gain, hi, lo, width, toks):
            held = []
            places = [(None, sb([128, 256], F32, AR + (4 * (n - 2) + i) * KB), None) for i in range(2)]

            def evac(m, o, t, cs):
                if cs != HALF[1]:
                    held.append([*take_tmp(), []])
                i, tm, rel, ts = held[m]
                t = act(lambda e: e.activation(tm[:, cs], o, ACT.Copy), t, rel)
                ts.append(t)
                add_up()
                sumsq(m, tm[:, cs], t, cs)
                return t

            r, ready = {}, []

            def scale_of(hf):
                ready.append(rstd(width, HALF[hf], r, places))

            def scale_end():
                if not r:
                    r.update(hold())
                ready.pop()()

            def norm():
                scale_end()
                scaled = []
                for j, (i, tm, _, ts) in enumerate(held):
                    scaled.append(dve(lambda e, j=j, tm=tm: e.scalar_tensor_tensor(
                        tm[:, :], tm[:, :], gain(j), r["R"], ALU.mult, ALU.mult), ts, r["t"], ssq_t))
                r["rel"][:] = scaled[-1:] * 2
                for j, (i, tm, _, _) in enumerate(held):
                    tt = two_parts(hi[:, j, :], lo[:, j, :], tm[:, :], scaled[j], t_arena)
                    tmps.rel[i] = tt
                    toks.append(tt)
                let_go(r)

            return evac, scale_of, scale_end, norm

        cq_tok, ck_tok, kr_tok = [], [], []
        cq_evac, cq_scale, cq_end, cq_norm = low_rank(3, lambda j: col("g_q", j), CQH, CQL, 384, cq_tok)
        ck_evac, ck_scale, ck_end, ck_norm = low_rank(2, lambda j: col("g_kv", j), CKH, CKL, 256, ck_tok)
        linear("dq", 2, list(three), hx, cq_evac, halves=True, 
               mid={(1, 0, 0): rope_end, (1, 0, 1): lambda: cq_scale(0), (1, 1, 0): cq_end})

        def kr_then(tm, t, cs):
            kr_tok.extend(two_parts(KRH[:, cs], KRL[:, cs], tm, t, ssq_rel, r_rel))
            return list(kr_tok)

        kr_later = []

        def dkv_evac(n, o, t, cs):
            if n < 2:
                return ck_evac(n, o, t, cs)
            add_up()
            ta = rotated(o, t, COS[:, cs], SIN[:, cs], rot, t_tab, kr_then, cs)
            kr_later.append(later.pop())
            return ta

        linear("dkv", 2, list(three), hx, dkv_evac, halves=True,
               mid={(0, 0, 0): lambda: cq_scale(1), (0, 0, 2): cq_norm, (1, 0, 1): lambda: ck_scale(0), (1, 1, 0): ck_end})

        qn_tok, qr_tok = {}, {}

        def uq(p):
            def then(tm, t, cs):
                out = []
                for e_half in range(2):
                    h = 2 * p + e_half
                    qr_tok[h] = stacked(QRS[:, h % 4, :], tm, e_half, t, t_arena)
                    out += qr_tok[h]
                return out

            def evac(n, o, t, cs):
                if n == 0:
                    return rotated(o, t, COS[:, :], SIN[:, :], rot, t_tab, then)
                h = 2 * p + n - 1
                qn_tok[h] = two_parts(QNH[:, h % 4, :], QNL[:, h % 4, :], o, t, t_arena)
                return qn_tok[h]

            linear("uq", 1, [(256, 128), (0, 128), (128, 128)],
                   lambda k, n, cs: (CQH[:, k, :], CQL[:, k, :], cq_tok[k]), evac)

        kr_turns, later[:] = list(kr_later), []
        later.append(lambda: ck_scale(1))
        uq(0)
        later.extend([ck_norm, *kr_turns])
        uq(1)
        kn_tok, vv_tok = {}, {}
        for hb in range(2):
            it = use("ukv")
            for hh in range(4):
                h = 4 * hb + hh
                b = banks.take()
                for k in range(2):
                    t = mm3(PS[:, b, :], it["hi"][:, k, 256 * hh:256 * hh + 128],
                            it["lo"][:, k, 256 * hh:256 * hh + 128], CKH[:, k, :], CKL[:, k, :], k == 0, k == 1,
                            [it["ready"], ck_tok[k], banks.rel[b] if k == 0 else None], k == 1)
                kn_tok[h] = banks.rel[b] = two_parts(HHI[:, h, :], HLO[:, h, :], PS[:, b, :], t)
                flush()
            vh = it["hi"].rearrange("p k (h c) -> p k h c", c=256)
            vl = it["lo"].rearrange("p k (h c) -> p k h c", c=256)
            for t4 in range(4):
                b = banks.take()
                ts = slice(t4 * 128, t4 * 128 + 128)
                o = PS[:, b, :].rearrange("p (h c) -> p h c", c=128)
                for k in range(2):
                    t = mm3(o, CKH[:, k, ts], CKL[:, k, ts], vh[:, k, :, 128:256], vl[:, k, :, 128:256],
                            k == 0, k == 1, [banks.rel[b] if k == 0 else None], k == 1)
                tv = act(lambda e, hb=hb, t4=t4, o=o: e.activation(VV[:, 4 * hb:4 * hb + 4, t4, :], o, ACT.Copy), t,
                         t_arena)
                banks.rel[b] = tv
                vv_tok[(hb, t4)] = tv
            done(it, t)

        MSCALE = 192.0 ** -0.5
        SPOS = {3: (0, 0, 512), 2: (1, 0, 384), 0: (2, 0, 256), 1: (2, 256, 256)}
        POFF = [0, 128, 384, 768]
        TPOS = {0: (3, 0), 1: (4, 0), 2: (5, 0), 3: (4, 384)}
        p_rel = [None] * 4
        pt4_rel, pt5_rel = [None] * 2, [None] * 2
        max_tok, exp_tok, soft, pt_of = {}, {}, {}, {}
        o_tok = [None] * 8
        state["reach"] = 0

        def m_scores(h):
            st = ST[:, 16 * (h % 4):16 * (h % 4) + 16]
            P = PBUF[PSLOT[h]]
            tx, s_tok = [], {}
            for i in (3, 2, 0, 1):
                bk, c, w = SPOS[i]
                o = PS[:, bk, c:c + w]
                qs = slice(i * 128, i * 128 + 128)
                assert bk not in banks.busy, banks.busy
                qh, ql, qr = QNH[:, h % 4, qs], QNL[:, h % 4, qs], QRS[:, h % 4, qs]
                kh, kl = HHI[:, h, 0:w], HLO[:, h, 0:w]
                prods = ((qh, kh), (ql, kh), (qh, kl), (qr, KRH[:, 0:w]), (qr, KRL[:, 0:w]))
                for m, (lhs, rhs) in enumerate(prods):
                    t = pe(lambda e, o=o, lhs=lhs, rhs=rhs, m=m: e.matmul(o, lhs, rhs, start=(m == 0), stop=(m == 4)),
                           banks.rel[bk] if m == 0 else None, qn_tok[h], kn_tok[h], qr_tok[h], kr_tok, sig=(m == 4))
                s_tok[i] = t
            s_tok[0] = s_tok[1]
            tm = {}
            for i in (3, 2, 0, 1):
                bk, c, _ = SPOS[i]
                d = 128 * i
                cur = masked_max(P[:, POFF[i] + d:POFF[i] + d + 128], PS[:, bk, c + d:c + d + 128], causal, st[:, i:i + 1],
                                 s_tok[i], p_rel[PSLOT[h]], t_const)
                if i:
                    cur = masked_max(P[:, POFF[i]:POFF[i] + d], PS[:, bk, c:c + d],
                                     ZERO.to_broadcast([128, d]), st[:, 4 + i:5 + i], cur, first=st[:, i:i + 1])
                tm[i] = cur
            banks.rel[0], banks.rel[1], banks.rel[2] = tm[3], tm[2], [tm[0], tm[1]]
            t0 = dve(lambda e: e.tensor_scalar(st[:, 0:1], st[:, 0:1], -MSCALE, None, ALU.mult), tm[0])
            tn = dve(lambda e: e.tensor_scalar(st[:, 1:4], st[:, 5:8], -MSCALE, None, ALU.mult), list(tm.values()))
            max_tok[h] = [tn, t0]

        def m_exps(h):
            st = ST[:, 16 * (h % 4):16 * (h % 4) + 16]
            P = PBUF[PSLOT[h]]
            te = []
            for i in (3, 2, 1, 0):
                Pi = P[:, POFF[i]:POFF[i] + 128 * (i + 1)]
                te.append(act(lambda e, i=i, Pi=Pi: e.activation(Pi, Pi, ACT.Exp, bias=st[:, i:i + 1], scale=MSCALE,
                                                                 accum_out=st[:, 8 + i:9 + i]), max_tok[h]))
            exp_tok[h] = te

        def m_soft(h):
            st = ST[:, 16 * (h % 4):16 * (h % 4) + 16]
            P = PBUF[PSLOT[h]]
            tr = dve(lambda e: e.reciprocal(st[:, 12:16], st[:, 8:12]), exp_tok[h])
            soft[h] = {}
            for i in (0, 1, 2, 3):
                Pi = P[:, POFF[i]:POFF[i] + 128 * (i + 1)]
                if i == 3:
                    soft[h][i] = act(lambda e, Pi=Pi, i=i: e.activation(Pi, Pi, ACT.Copy, scale=st[:, 12 + i:13 + i]),
                                     tr)
                else:
                    soft[h][i] = dve(lambda e, Pi=Pi, i=i: e.tensor_scalar(Pi, Pi, st[:, 12 + i:13 + i], None,
                                                                           ALU.mult), tr)

        def m_turn(h):
            P = PBUF[PSLOT[h]]
            tl = {}
            for j in (0, 1, 3, 2):
                bk, c = TPOS[j]
                assert bk not in banks.busy, banks.busy
                for i in range(j, 4):
                    t = pe(lambda e, bk=bk, c=c, i=i, j=j: e.transpose(
                        PS[:, bk, c + (i - j) * 128:c + (i - j) * 128 + 128],
                        P[:, POFF[i] + j * 128:POFF[i] + j * 128 + 128], ident), banks.rel[bk], soft[h][i],
                        sig=(i == 3))
                tl[j] = t
            p_rel[PSLOT[h]] = t
            pt_of[h] = {}
            for bk, n, tok in ((3, 512, tl[0]), (4, 512, tl[3]), (5, 256, tl[2])):
                if bk == 5 and h > 1:
                    i, tm, rel = pt5_rel, PT5[h % 2], pt5_rel[h % 2]
                elif bk == 4 and h > 2:
                    i, tm, rel = pt4_rel, PT4[h % 2], pt4_rel[h % 2]
                else:
                    i, tm, rel = take_tmp()
                t = act(lambda e, bk=bk, n=n, tm=tm: e.activation(tm[:, 0:n], PS[:, bk, 0:n], ACT.Copy), tok, rel)
                banks.rel[bk] = t
                pt_of[h][bk] = (i, tm, t)

        def m_values(h):
            ob = 6 + h % 2
            for j in range(4):
                bk, c = TPOS[j]
                w = 512 - 128 * j
                i, tm, t = pt_of[h][bk]
                tpv = pe(lambda e, j=j, c=c, w=w, tm=tm: e.matmul(PS[:, ob, 128 * j:512], VV[:, h, j, :], tm[:, c:c + w],
                                                                  start=(j == 0), stop=(j == 3),
                                                                  skip_group_check=True),
                         t, banks.rel[ob] if j == 0 else None, vv_tok[(h // 4, j)], sig=(j == 3))
            for i, tm, t in pt_of[h].values():
                if i is pt5_rel or i is pt4_rel:
                    i[h % 2] = tpv
                else:
                    tmps.rel[i] = tpv
            banks.rel[ob] = tpv

        def m_out(h):
            ob = 6 + h % 2
            o_tok[h] = banks.rel[ob] = two_parts(HHI[:, h, :], HLO[:, h, :], PS[:, ob, :], banks.rel[ob])

        ZERO = GS[:, 0, 0:1]
        t_zero = dve(lambda e: e.memset(ZERO, 0.0), now("dve"))
        for h in range(2):
            m_scores(h)
            m_exps(h)
        banks.only(3, 4, 5, 6, 0, 1, 2)
        m_soft(0)
        uq(2)
        for h in range(2):
            flush()
            m_turn(h)
            flush_all()
            m_soft(h + 1)
            if h:
                m_out(h - 1)
            m_scores(h + 2)
            m_exps(h + 2)
            m_values(h)
            ahead()
        uq(3)
        p_rel[2] = p_rel[3] = pt5_rel[0] = pt5_rel[1] = now("pe")
        m_out(1)
        banks.only(7)
        flush()
        banks.only(*range(7))
        m_scores(4)
        for h in range(2, 8):
            flush()
            if 3 <= h < 5:
                m_scores(h + 3)
            m_turn(h)
            flush_all()
            if h == 2:
                pt4_rel[:] = [now("dve", "pool")] * 2
                m_exps(4)
                m_scores(5)
                m_exps(5)
            elif h < 5:
                m_exps(h + 3)
            if h == 5:
                ssq_rel[:] = r_rel[:] = now("pe") * 2
            if h < 7:
                m_soft(h + 1)
            if h > 3:
                m_out(h - 2)
            if h > 2:
                m_values(h - 1)
            ahead()
        m_values(7)
        m_out(6)
        m_out(7)
        banks.only(*range(8))
        state["reach"] = 4

        def ox(k, n, cs):
            return HHI[:, k, cs], HLO[:, k, cs], o_tok[k]

        def mo_evac(n2):
            return lambda n, o, t, cs: add_x(4 * n2 + n, o, MOD[:, 0, 16 + 4 * n2 + n:17 + 4 * n2 + n], t,
                                             mod_tok[(0, 2)], cs)

        linear("mo", 2, list(four), ox, mo_evac(0))
        norm = mod_norm(0, 1)
        linear("mo", 2, list(four), ox, mo_evac(1), frees_h=True, **closing(norm))

        HID = [[sb([128, 8, S], F32R, AR + (2 * i + k) * 16 * KB) for k in range(2)] for i in range(2)]
        hid_tok = [[[None, None] for _ in range(8)] for _ in range(2)]
        hid_rel = [None, None]

        def hid(i):
            return lambda k, n, cs: (HID[i][0][:, k, cs], HID[i][1][:, k, cs], [hid_tok[i][k][f] for f in hs(cs)])

        def hidden(i, j, tm, t, cs):
            tt = two_parts(HID[i][0][:, j, cs], HID[i][1][:, j, cs], tm[:, cs], t, hid_rel[i])
            for f in hs(cs):
                hid_tok[i][j][f] = tt
            return tt

        def ff(l, norm, closing_norm, extra=None):
            hid_rel[:] = [now("pe", "dve", "act")] * 2

            def up(q):
                for n2 in range(2):
                    def evac(n, o, t, cs, n2=n2):
                        i, tm, rel = take_tmp()
                        ta = act(lambda e: e.activation(tm[:, cs], o, ACT.Relu), t, rel)
                        td = dve(lambda e: e.tensor_tensor(tm[:, cs], tm[:, cs], tm[:, cs], ALU.mult), ta)
                        tmps.rel[i] = hidden(q % 2, 4 * n2 + n, tm, td, cs)
                        return ta
                    linear(f"up{l}", 2, list(four), hx, evac, **(opening(norm) if q == 0 and n2 == 0 else {}))

            def down(q):
                for n2 in range(2):
                    def evac(n, o, t, cs, n2=n2):
                        j = 4 * n2 + n
                        t = add_x(j, o, MOD[:, l, 40 + j:41 + j], t, mod_tok[(l, 5)], cs, q == 3)
                        if extra and q == 3:
                            extra(j, cs, t)
                        return t
                    last = closing(closing_norm()) if q == 3 and n2 else {}
                    linear(f"down{l}", 2, list(four), hid(q % 2), evac, **last)
                hid_rel[q % 2] = now("pe")

            up(0)
            for q in range(4):
                if q < 3:
                    up(q + 1)
                if q == 2:
                    h_rel[:] = now("pe") * 2
                down(q)

        box = {}

        def then_norm(make):
            def go():
                box["norm"] = make()
                return box["norm"]
            return go

        ff(0, norm, then_norm(lambda: mod_norm(1, 0)))

        settle(True)
        t_arena = now("pe", "act", "dve")
        QS = sb([128, 16, S], F32R, AR)
        KH = sb([128, 4, S], F32R, AR + 32 * KB)
        KL = sb([128, 4, S], F32R, AR + 40 * KB)
        SV = sb([128, 4, 256], F32, AR + 48 * KB)
        SB2 = [sb([128, 896], F32, AR + 52 * KB + 3584 * i) for i in range(4)]
        BT = [sb([128, 512], F32, o_r), sb([128, 512], F32, o_ssq)]
        DIST = sb([128, 512], F32, o_acc)
        BV = sb([128, 256], F32, o_acc + 2 * KB)
        SINK = sb([128, 16], F32, o_acc + 3 * KB)
        NSINK = sb([128, 16], F32, o_acc + 3 * KB + 64)
        GB = sb([128, 8], F32, o_acc + 3 * KB + 128)
        t_swa = dma("swa", DIST[:, :], A["k_dist"], acc_rel, t_arena, eng="pool")
        t_swa = dma("swa", BV[:, :], A["swa_b_qkv"][:, 1280:1536].to_broadcast([128, 256]), eng="pool")
        t_swa = dma("swa", SINK[:, :], A["swa_sinks"].to_broadcast([128, 16]), eng="pool")

        sq_tok, sk_tok, sv_tok = {}, {}, {}

        def q_evac(half):
            def evac(n, o, t, cs):
                out = []
                for e_half in range(2):
                    h = 8 * half + 2 * n + e_half
                    a, b = slice(64 * e_half, 64 * e_half + 64), slice(64 - 64 * e_half, 128 - 64 * e_half)
                    src, bias, d = o[a, :], col("bq", h)[a, :], QS[:, h, cs]
                    th = act(lambda e, d=d, a=a, src=src, bias=bias: e.activation(d[a, :], src, ACT.Identity, bias=bias),
                             t, t_arena, t_cols)
                    tl = dve(lambda e, d=d, a=a, b=b, src=src, bias=bias: e.scalar_tensor_tensor(
                        d[b, :], src, bias, d[a, :].bitcast(F32), ALU.add, ALU.subtract), t, th, t_arena, t_cols)
                    sq_tok.setdefault(h, []).extend([th, tl])
                    out += [th, tl]
                return out
            return evac

        linear("qkv", 2, list(four), hx, q_evac(0), **opening(box["norm"]))
        t_nsink = dve(lambda e: e.tensor_scalar(NSINK[:, :], SINK[:, :], -1.0, None, ALU.mult), t_swa)
        t_gb = dve(lambda e: e.tensor_tensor(GB[:, :], MOD[:, 1, 16:24], col("b_o", 0, 8), ALU.mult), mod_tok[(1, 2)],
                   t_cols, t_swa)
        for j in range(8):
            x_tok[j][0] = x_tok[j][1] = pool(lambda e, j=j: e.tensor_scalar(
                X[:, j, :], X[:, j, :], GB[:, j:j + 1], None, ALU.add), x_tok[j], t_gb, h_tok[j])
        ia, ib = use("qkv"), use("qkv")
        for n in range(2):
            b = banks.take()
            for k in range(8):
                it = (ia, ib)[k // 4]
                cs = slice(128 * n, 128 * n + 128)
                t = mm3(PS[:, b, :], it["hi"][:, k % 4, cs], it["lo"][:, k % 4, cs], HHI[:, k, :], HLO[:, k, :],
                        k == 0, k == 7, [it["ready"], h_tok[k], banks.rel[b] if k == 0 else None], k == 7)
            i, tm, rel = take_tmp()
            t = act(lambda e, n=n, b=b, tm=tm: e.activation(tm[:, :], PS[:, b, :], ACT.Identity, bias=col("bk", n)),
                    t, rel)
            banks.rel[b] = t
            for e_half in range(2):
                g = 2 * n + e_half
                sk_tok[g] = doubled(KH[:, g, :], KL[:, g, :], tm, e_half, t, t_arena)
            tmps.rel[i] = [sk_tok[2 * n], sk_tok[2 * n + 1]]
        sb_rel, bt_rel = [None] * 4, [None, None]
        soft2, pt2_of, max_tok = {}, {}, {}

        SWIDE, SOFF = [128, 256, 256, 256], [0, 128, 384, 640]

        def s_block(h, n):
            return SB2[h % 4][:, SOFF[n]:SOFF[n] + SWIDE[n]]

        def s_scores(h):
            g, bk = h // 4, 4 * (h % 2)
            slope = 2.0 ** (-8.0 * (h + 1) / 16)
            T = BT[h % 2]
            st = ST[:, 16 * (h % 4):16 * (h % 4) + 16]
            t_bias = pool(lambda e: e.tensor_scalar(T[:, :], DIST[:, :], -8.0 * slope, None, ALU.mult), t_swa,
                          bt_rel[h % 2], t_arena, ssq_rel, r_rel)
            tx = []
            for n in range(4):
                ks = slice(128 * max(n - 1, 0), 128 * max(n - 1, 0) + 256)
                qs = slice(128 * n, 128 * n + 128)
                o = PS[:, bk + n // 2, 256 * (n % 2):256 * (n % 2) + 256]
                pe(lambda e, o=o, qs=qs, ks=ks: e.matmul(o, QS[:, h, qs], KH[:, g, ks], start=True, stop=False),
                   banks.rel[bk], banks.rel[bk + 1], sq_tok[h], sk_tok[g])
                t = pe(lambda e, o=o, qs=qs, ks=ks: e.matmul(o, QS[:, h, qs], KL[:, g, ks], start=False, stop=True),
                       sig=True)
                if n % 2 == 0:
                    continue
                for m in (n - 1, n):
                    w = SWIDE[m]
                    o = PS[:, bk + n // 2, 256 * (m % 2):256 * (m % 2) + w]
                    tx.append(masked_max(s_block(h, m), o, T[:, 256 * (m > 0):256 * (m > 0) + w], st[:, m:m + 1], t,
                                         t_bias, sb_rel[h % 4], t_arena))
            banks.rel[bk] = banks.rel[bk + 1] = bt_rel[h % 2] = tx[-1]
            t = dve(lambda e: e.tensor_scalar(st[:, 4:8], st[:, 0:4], -0.125, NSINK[:, h:h + 1], ALU.mult, ALU.min), tx,
                    t_nsink)
            max_tok[h] = t

        def s_exps(h):
            st = ST[:, 16 * (h % 4):16 * (h % 4) + 16]
            t, te = max_tok[h], []
            for n in range(4):
                te.append(act(lambda e, n=n: e.activation(s_block(h, n), s_block(h, n), ACT.Exp,
                                                          bias=st[:, 4 + n:5 + n], scale=0.125, accum_out=st[:, 8 + n:9 + n]), t))
            te.append(act(lambda e: e.activation(st[:, 12:16], st[:, 4:8], ACT.Exp, bias=SINK[:, h:h + 1]), t))
            exp_tok[h] = te

        def s_soft(h):
            st = ST[:, 16 * (h % 4):16 * (h % 4) + 16]
            t = dve(lambda e: e.tensor_tensor(st[:, 8:12], st[:, 8:12], st[:, 12:16], ALU.add), exp_tok[h])
            t = dve(lambda e: e.reciprocal(st[:, 0:4], st[:, 8:12]), t)
            soft2[h] = [dve(lambda e, n=n: e.tensor_scalar(s_block(h, n), s_block(h, n), st[:, n:n + 1], None,
                                                      ALU.mult), t) for n in range(4)]

        SPAIRS = [(0, 0, 0)] + [(n, w, n - 1 + w) for n in range(1, 4) for w in range(2)]

        def s_turn(h):
            pt2_of[h] = []
            for bk, lo, hi in ((2, 0, 4), (3, 4, 7)):
                for m in range(lo, hi):
                    n, w, _ = SPAIRS[m]
                    t = pe(lambda e, m=m, n=n, w=w, bk=bk, lo=lo: e.transpose(
                        PS[:, bk, 128 * (m - lo):128 * (m - lo) + 128], s_block(h, n)[:, 128 * w:128 * w + 128], ident),
                        banks.rel[bk], soft2[h][n], sig=(m == hi - 1))
                i, tm, rel = take_tmp()
                c = 128 * (hi - lo)
                if lo == 0 or h % 4:
                    t2 = act(lambda e, bk=bk, c=c, tm=tm: e.activation(tm[:, 0:c], PS[:, bk, 0:c], ACT.Copy), t, rel)
                else:
                    t2 = dve(lambda e, bk=bk, c=c, tm=tm: e.tensor_copy(tm[:, 0:c], PS[:, bk, 0:c]), t, rel)
                banks.rel[bk] = t2
                pt2_of[h].append((i, tm, t2))
            sb_rel[h % 4] = t

        def s_values(h):
            g = h // 4
            ob, off = 6 + (h // 2) % 2, 64 * (h % 2)
            for m, (n, w, kb) in enumerate(SPAIRS):
                i, tm, t = pt2_of[h][m // 4]
                tv = pe(lambda e, n=n, m=m, kb=kb, tm=tm, w=w: e.matmul(
                    PS[off:off + 64, ob, 128 * n:128 * n + 128], SV[:, kb, 64 * g:64 * g + 64],
                    tm[:, 128 * (m % 4):128 * (m % 4) + 128], start=(m == 0 or w == 0), stop=(m == 0 or w == 1)),
                    t, banks.rel[ob], sv_tok[kb], sig=(m == 6))
            for i, tm, t in pt2_of[h]:
                tmps.rel[i] = tv
            if h % 2:
                banks.rel[ob] = tv

        def s_out(j):
            ob = 6 + j % 2
            t = banks.rel[ob]
            th = act(lambda e: e.activation(HHI[:, j, :], PS[:, ob, :], ACT.Copy), t, t_h)

            def low():
                o_tok[j] = banks.rel[ob] = dve(lambda e: e.tensor_tensor(HLO[:, j, :], PS[:, ob, :], HHI[:, j, :].bitcast(F32),
                                                                         ALU.subtract), th)
            return low

        for t4 in range(4):
            b = banks.take()
            ts = slice(128 * t4, 128 * t4 + 128)
            for k in range(8):
                it = (ia, ib)[k // 4]
                t = mm3(PS[:, b, 0:256], HHI[:, k, ts], HLO[:, k, ts], it["hi"][:, k % 4, 256:512],
                        it["lo"][:, k % 4, 256:512], k == 0, k == 7, [banks.rel[b] if k == 0 else None], k == 7)
            sv_tok[t4] = dve(lambda e, t4=t4, b=b: e.tensor_tensor(SV[:, t4, :], PS[:, b, 0:256], BV[:, :], ALU.add), t,
                             t_swa, t_arena)
            banks.rel[b] = sv_tok[t4]
            if t4 % 2:
                s_scores(t4 // 2)
                s_exps(t4 // 2)
        done(ia, t)
        done(ib, t)
        s_scores(2)
        s_exps(2)
        banks.only(4, 5, 6, 7)
        s_soft(0)
        linear("qkv", 2, list(four), hx, q_evac(1))
        banks.only(*range(8))
        t_h = now("pe")
        for h in range(16):
            if h < 13:
                s_scores(h + 3)
            s_turn(h)
            low = s_out((h - 3) // 2) if h > 2 and h % 2 else None
            if h < 13:
                s_exps(h + 3)
            if h < 15:
                s_soft(h + 1)
            if low:
                low()
            if h == 13:
                ssq_rel[:] = r_rel[:] = now("dve") * 2
            if h:
                s_values(h - 1)
            ahead(True)
        s_values(15)
        s_out(7)()

        def so_evac(n2):
            return lambda n, o, t, cs: add_x(4 * n2 + n, o, MOD[:, 1, 16 + 4 * n2 + n:17 + 4 * n2 + n], t,
                                             mod_tok[(1, 2)], cs)

        linear("so", 2, list(four), ox, so_evac(0))
        norm = mod_norm(1, 1)
        linear("so", 2, list(four), ox, so_evac(1), frees_h=True, **closing(norm))

        def g_final(j):
            return col("g_final", j)

        def weighted(j, cs, t):
            sumsq(j, X[:, j, cs], t, cs, SSQ2, ssq2_t, ssq2_rel, g_final(j), pool)

        G2 = sb([128, 8], F32, o_st + 64 * 4)
        t_g2 = dve(lambda e: e.tensor_tensor(G2[:, :], col("g_final", 0, 8), col("ffn1_norm", 0, 8), ALU.mult), t_cols)

        t_rt = []

        def final_scale(hf):
            cs, b = HALF[hf], banks.take()
            sums(cs, SSQ, ssq_t, ssq_rel, b, 0)
            t = sums(cs, SSQ2, ssq2_t, ssq2_rel, b, 2)
            both, first = RS[:, 4 * hf:4 * hf + 2], RS[:, 4 * hf + 2:4 * hf + 4]
            t = dve(lambda e: e.tensor_scalar(first, PS[:, b, 0:2], 1.0 / D, EPS, ALU.mult, ALU.add), t, rs_rel[hf])
            t = banks.rel[b] = dve(lambda e: e.scalar_tensor_tensor(both, first, EPS * D, PS[:, b, 2:4], ALU.mult,
                                                                    ALU.add), t)
            act(lambda e: e.activation(both, both, ACT.Sqrt, scale=1.0 / D), t)
            t = act(lambda e: e.activation(first, first, ACT.Sqrt), t)
            t = dve(lambda e: e.reciprocal(RS[:, 4 * hf:4 * hf + 4], RS[:, 4 * hf:4 * hf + 4]), t)
            i, tm, t = diagonals(4 * hf, 4, t)
            rs_rel[hf] = t

            def second():
                r, b2 = hold(), banks.take()
                r["t"].append(spread(r["R"][:, cs], tm, 0, t, banks.rel[r["b"]]))
                tmps.rel[i] = spread(PS[:, b2, cs], tm, 256, t, banks.rel[b2])
                banks.rel[b2] = act(lambda e: e.activation(RT[:, cs], PS[:, b2, cs], ACT.Copy), tmps.rel[i], r_rel[hf])
                t_rt.append(banks.rel[b2])
                return r

            return second

        final_norm = in_steps(final_scale,
                              lambda cs, r, chunks: normed(cs, lambda j: G2[:, j:j + 1], None, r, t_g2, chunks))

        def first_norm_of_x():
            for j in range(8):
                t = dve(lambda e, j=j: e.scalar_tensor_tensor(X[:, j, :], X[:, j, :], g_final(j), RT[:, :], ALU.mult,
                                                              ALU.mult), x_tok[j], ssq_t, ssq2_t, t_rt)
                x_tok[j] = [t, t]
                r_rel[:] = [t, t]

        ff(1, norm, lambda: final_norm, weighted)

        def glu(norm, closing_norm, between=None):
            hid_rel[:] = [now("pe", "dve", "act")] * 2

            def evac(i_hid, j, b1, b3, t1, t3, cs):
                i, tm, rel = take_tmp()
                ta = act(lambda e: e.activation(tm[:, cs], PS[:, b1, cs], ACT.Silu), t1, rel)
                td = dve(lambda e: e.tensor_tensor(tm[:, cs], tm[:, cs], PS[:, b3, cs], ALU.mult), ta, t3)
                banks.rel[b1], banks.rel[b3] = ta, td
                banks.busy.difference_update((b1, b3))
                tmps.rel[i] = hidden(i_hid, j, tm, td, cs)

            def up(blk):
                for c in range((4, 4, 3)[blk]):
                    parts = HALF if blk == 0 and c == 0 else (FULL,)
                    its = []
                    for hf, cs in enumerate(parts):
                        bk = [banks.take() for _ in range(4)]
                        banks.busy.update(bk)
                        tk = []
                        for w, name in enumerate(("w1", "w3")):
                            if hf == 0:
                                if len(parts) == 2 and w == 0:
                                    norm("c0")
                                its.append(use(name))
                            it = its[w]
                            for n in range(2):
                                b = bk[2 * w + n]
                                for k in range(8):
                                    ws = slice(128 * n, 128 * n + 128)
                                    xh, xl, tx = hx(k, n, cs)
                                    t = mm3(PS[:, b, cs], it["hi"][:, k, ws], it["lo"][:, k, ws], xh, xl, k == 0,
                                            k == 7, [it["ready"], tx, banks.rel[b] if k == 0 else None], k == 7)
                                tk.append(t)
                                if w:
                                    evac(blk % 2, 2 * c + n, bk[n], bk[2 + n], tk[n], t, cs)
                                if len(parts) == 2 and (hf, w) == (0, 0):
                                    norm(("a1", "b1")[n])
                            if hf == len(parts) - 1:
                                done(it, t)

            def down(blk):
                for n2 in range(2):
                    last = closing(closing_norm) if blk == 2 and n2 else {}
                    linear("w2", 2, list(four), hid(blk % 2),
                           lambda n, o, t, cs: add_x(4 * n2 + n, o, 0.5, t, None, cs, blk == 2), **last)
                hid_rel[blk % 2] = now("pe")

            up(0)
            if between:
                between()
            for blk in range(3):
                if blk < 2:
                    up(blk + 1)
                if blk == 1:
                    h_rel[:] = now("pe") * 2
                down(blk)

        norm = plain_norm("mix_norm")
        glu(final_norm, norm, first_norm_of_x)

        t_arena = now("pe", "dve", "act")
        DQ = sb([128, 6, S], F32R, AR)
        DKH = sb([128, 6, S], F32R, AR + 12 * KB)
        DKL = sb([128, 6, S], F32R, AR + 24 * KB)
        DV = sb([128, 4, 768], F32, AR + 36 * KB)
        DM = sb([128, 10, 128], F32, AR + 48 * KB)
        SB3 = [sb([128, 128 * n], F32, AR + 53 * KB + 512 * c) for c, n in ((0, 3), (3, 6), (9, 8), (17, 10))]
        DCOS = sb([128, S], F32, o_acc)
        DSIN = sb([128, S], F32, o_acc + 2 * KB)
        OHI = [sb([128, S], F32R, o_ssq), sb([128, S], F32R, AR)]
        OLO = [sb([128, S], F32R, o_r), sb([128, S], F32R, AR + 2 * KB)]
        t_dm = dma("dil", DCOS[:, :], A["k_dcos"], t_arena, eng="pool")
        t_dm = dma("dil", DSIN[:, :], A["k_dsin"], eng="pool")
        t_dm = dma("dil", rot, A["k_drot"], eng="pool")
        t_dm = dma("dil", DM[:, :, :], A["k_dil"], eng="pool")
        dq_tok, dk_tok = {}, {}

        def qk(a, kind):
            def then_of(g):
                def then(tm, t, cs):
                    out = []
                    for e_half in range(2):
                        s = 2 * g + e_half
                        if kind == "q":
                            tt = stacked(DQ[:, s, cs], tm, e_half, t, t_arena)
                            dq_tok.setdefault((a, s), []).extend(tt)
                        else:
                            tt = doubled(DKH[:, s, cs], DKL[:, s, cs], tm, e_half, t, t_arena, both=False)
                            dk_tok.setdefault((a, s), []).extend(tt)
                        out += tt
                    return out
                return then

            return lambda n, o, t, cs: rotated(o, t, DCOS[:, cs], DSIN[:, cs], rot, t_dm, then_of(n), cs)

        dv_tok = {}

        def v_evac(c, w):
            def evac(n, o, t, cs):
                tv = act(lambda e: e.activation(DV[:, n, c:c + w], o, ACT.Copy), t, t_arena)
                dv_tok.setdefault(n, []).append(tv)
                return tv
            return evac

        sb3_rel = [None] * 4
        soft3, pt3_of = {}, {}
        SALL = PS[:, 0:3, :].rearrange("p n k -> p (n k)")
        TALL = PS[:, 3:6, :].rearrange("p n k -> p (n k)")

        def blocks(i):
            out = [(0, kb) for kb in ((i - 1, i) if i else (0,))]
            return out + [(1, kb) for kb in range(i + 1)] + [(2, kb) for kb in range(i + 1)]

        def d_scores(s):
            j, i = s // 4, s % 4
            a, e_half = j // 2, j % 2
            bl = blocks(i)
            own = slice(64 * e_half, 64 * e_half + 64)
            runs = []
            for c, (g, kb) in enumerate(bl):
                if runs and runs[-1][1] == g and c % 4:
                    runs[-1][3] += 1
                else:
                    runs.append([c, g, kb, 1])
            for m, (c, g, kb, n) in enumerate(runs):
                q, kh, kl = (T[:, 2 * g + e_half, :] for T in (DQ, DKH, DKL))
                qs, ks = slice(128 * i, 128 * i + 128), slice(128 * kb, 128 * (kb + n))
                o = SALL[:, 128 * c:128 * (c + n)]
                pe(lambda e, o=o, q=q, kh=kh, qs=qs, ks=ks: e.matmul(o, q[:, qs], kh[:, ks], start=True, stop=False),
                   [banks.rel[b] for b in range(3)], dq_tok[(a, 2 * g + e_half)], dk_tok[(a, 2 * g + e_half)])
                t = pe(lambda e, o=o, q=q, kl=kl, qs=qs, ks=ks: e.matmul(o, q[own, qs], kl[own, ks], start=False,
                                                                         stop=True), sig=(m == len(runs) - 1))
            assert not banks.busy & {0, 1, 2}, banks.busy
            B = SB3[s % 4]
            st = ST[:, 16 * (s % 4):16 * (s % 4) + 16]
            g0 = 2 if i else 1
            tm = []
            for m, (c, n, m0) in enumerate(((0, g0, 2 - g0), (g0, i + 1, 5 - i), (g0 + i + 1, i + 1, 9 - i))):
                tm = [masked_max(B[:, 128 * c:128 * (c + n)], SALL[:, 128 * c:128 * (c + n)],
                                 DM[:, m0:m0 + n, :].rearrange("p n k -> p (n k)"), st[:, m:m + 1], t, t_dm,
                                 sb3_rel[s % 4], t_arena, tm, first=st[:, m - 1:m] if m else -3.0e38)]
            for b in range(3):
                banks.rel[b] = tm[0]
            max_tok[s] = dve(lambda e: e.tensor_scalar(st[:, 4:5], st[:, 2:3], -0.125, None, ALU.mult), tm)

        def d_exp(s):
            B = SB3[s % 4]
            st = ST[:, 16 * (s % 4):16 * (s % 4) + 16]
            w = 128 * len(blocks(s % 4))
            exp_tok[s] = act(lambda e: e.activation(B[:, 0:w], B[:, 0:w], ACT.Exp, bias=st[:, 4:5], scale=0.125,
                                                    accum_out=st[:, 5:6]), max_tok[s])

        def d_soft(s):
            B = SB3[s % 4]
            st = ST[:, 16 * (s % 4):16 * (s % 4) + 16]
            w = 128 * len(blocks(s % 4))
            t = exp_tok[s]
            t = dve(lambda e: e.reciprocal(st[:, 6:7], st[:, 5:6]), t)
            soft3[s] = dve(lambda e: e.tensor_scalar(B[:, 0:w], B[:, 0:w], st[:, 6:7], None, ALU.mult), t)

        do_tok = [None, None]

        def d_turn(s):
            bl = blocks(s % 4)
            B = SB3[s % 4]
            n = len(bl)
            pt3_of[s] = []
            assert not banks.busy & {3, 4, 5}, banks.busy
            for q in range(-(-n // 4)):
                c0, c1 = 4 * q, min(4 * q + 4, n)
                for c in range(c0, c1):
                    t = pe(lambda e, c=c: e.transpose(TALL[:, 128 * c:128 * c + 128], B[:, 128 * c:128 * c + 128],
                                                      ident), banks.rel[3 + q], soft3[s], sig=(c == c1 - 1))
                i, tm, rel = take_tmp()
                w = 128 * (c1 - c0)
                src = TALL[:, 128 * c0:128 * c1]
                if q == 1:
                    t2 = dve(lambda e, tm=tm, w=w, src=src: e.tensor_copy(tm[:, 0:w], src), t, rel)
                else:
                    t2 = act(lambda e, tm=tm, w=w, src=src: e.activation(tm[:, 0:w], src, ACT.Copy), t, rel)
                banks.rel[3 + q] = t2
                pt3_of[s].append((i, tm, t2))
            sb3_rel[s % 4] = t

        def d_values(s):
            j, i = s // 4, s % 4
            a, off = j // 2, 64 * (j % 2)
            bl = blocks(i)
            ob = 6 + a
            o = PS[off:off + 64, ob, 128 * i:128 * i + 128]
            for c, (g, kb) in enumerate(bl):
                vc = 64 * (4 * g + j)
                _, tm, t = pt3_of[s][c // 4]
                tv = pe(lambda e, c=c, kb=kb, vc=vc, tm=tm: e.matmul(
                    o, DV[:, kb, vc:vc + 64], tm[:, 128 * (c % 4):128 * (c % 4) + 128], start=(c == 0),
                    stop=(c == len(bl) - 1)), t, banks.rel[ob], dv_tok[kb], sig=(c == len(bl) - 1))
            for idx, _, _ in pt3_of[s]:
                tmps.rel[idx] = tv
            if i == 3 and j % 2:
                do_tok[a] = banks.rel[ob] = two_parts(OHI[a][:, :], OLO[a][:, :], PS[:, ob, :], tv, ssq_rel, r_rel)

        linear("v", 2, [(0, 512)] * 4, hx_tok, v_evac(0, 512), swap=True, **opening(norm, 1))
        linear("qk", 2, list(three), hx, qk(0, "k"))
        linear("qk", 2, list(three), hx, qk(0, "q"))
        banks.only(3, 4, 5, 6, 7)

        def d_start(s):
            flush_all()
            d_scores(s)
            d_exp(s)

        linear("v2", 1, [(0, 256)] * 4, hx_tok, v_evac(512, 256), swap=True,
               mid={(0, 0, 2): lambda: d_start(0), (0, 0, 3): lambda: d_start(1)})
        d_start(2)
        d_soft(0)

        PZ = sb([128, 2, 16 + S], F32, AR + 4 * KB)
        DH = sb([128, 4, S], F32R, AR + 9 * KB)
        DL = sb([128, 4, S], F32R, AR + 17 * KB)
        CNT = sb([128, 4, S], F32, AR + 25 * KB)
        d_tok = {}
        pz_rel = [None]
        t_pz = []

        PZC = [sb([128, S], F32, c) for c in (o_acc, o_acc + 2 * KB, AR + 17 * KB, AR + 19 * KB)]
        pz_tok = {}

        def pz_evac(half):
            def evac(n, o, t, cs):
                n += 2 * half
                pz_tok[n] = act(lambda e: e.activation(PZC[n][:, :], o, ACT.Copy), t,
                                t_pz if half else now("dve", "pool"))
                return pz_tok[n]
            return evac

        def pz_pool(n):
            cur = act(lambda e: e.activation(PZ[:, 0, 16:16 + S], PZC[n][:, :], ACT.Copy), pz_tok[n], pz_rel, t_pz)
            for step in range(n + 1):
                w = 1 << step
                src, dst = step % 2, 1 - step % 2
                cur = dve(lambda e, w=w, src=src, dst=dst: e.tensor_tensor(
                    PZ[:, dst, 16:16 + S], PZ[:, src, 16:16 + S], PZ[:, src, 16 - w:16 - w + S], ALU.add), cur, t_pz,
                    pz_rel)
            fin = (n + 1) % 2
            i2, tm2, rel2 = take_tmp()
            t1 = pool(lambda e: e.tensor_tensor(tm2[:, :], PZ[:, fin, 16:16 + S], CNT[:, n, :], ALU.mult), cur, t_pz,
                      rel2)
            pz_rel[0] = t1
            t2 = pool(lambda e: e.tensor_tensor(tm2[:, :], tm2[:, :], PZC[n][:, :], ALU.subtract), t1, pz_tok[n])
            late_pz.append((n, i2, tm2, t2))

        late_pz = []

        def pz_parts():
            for n, i2, tm2, t2 in late_pz:
                d_tok[n] = two_parts(DH[:, n, :], DL[:, n, :], tm2[:, :], t2, t_pz)
                tmps.rel[i2] = d_tok[n]

        for s in range(16):
            if s == 5:
                banks.only(3, 4, 5, 0, 7, 1, 2)
                linear("qk", 2, list(three), hx, qk(1, "k"))
                linear("qk", 2, list(three), hx, qk(1, "q"))
                linear("pz", 1, [(0, 128), (128, 128)], hx, pz_evac(0))
                flush_all()
            if s == 13:
                t_pz.extend(now("pe", "act", "dve"))
                t_pz.append(dma("cnt", CNT[:, :, :], A["k_cnt"].to_broadcast([128, 4, S]), list(t_pz), eng="pool"))
                t_pz.append(dve(lambda e: e.memset(PZ[:, :, 0:16], 0.0), t_pz))
                banks.only(0, 1, 2, 6)
                linear("pz", 1, [(0, 128), (128, 128)], hx, pz_evac(1))
            if s < 13:
                d_scores(s + 3)
            d_turn(s)
            if s < 13:
                d_exp(s + 3)
            flush()
            if s < 15:
                d_soft(s + 1)
            if s:
                d_values(s - 1)
        d_values(15)
        for n in range(4):
            pz_pool(n)
        banks.only(*range(8))

        YH = sb([128, 4, S], F32R, AR + 33 * KB)
        YL = sb([128, 4, S], F32R, AR + 41 * KB)
        MH = [sb([128, S], F32R, AR + (49 + 2 * j) * KB) for j in range(8)]
        ML = [sb([128, S], F32R, AR + (9 + 2 * j) * KB) for j in range(8)]
        GA = [sb([128, S], F32, AR + (25 + 2 * n) * KB) for n in range(4)]
        t_att = now("pe", "dve", "act", "pool")
        ga_rel = [None] * 4
        y_tok, m_tok = {}, {}

        def pool_out():
            it = use("pw")
            for g in range(4):
                b = banks.take()
                t = mm3(PS[:, b, :], it["hi"][:, g, :], it["lo"][:, g, :], DH[:, g, :], DL[:, g, :], True, True,
                        [it["ready"], d_tok[g], banks.rel[b]], True)
                i, tm, rel = take_tmp()
                t1 = dve(lambda e, g=g, b=b, tm=tm: e.tensor_scalar(tm[:, :], PS[:, b, :], col("pool_scale", g), None,
                                                                    ALU.mult), t, rel)
                banks.rel[b] = t1
                y_tok[g] = two_parts(YH[:, g, :], YL[:, g, :], tm[:, :], t1, t_att)
                tmps.rel[i] = y_tok[g]
            done(it, t)
            return now("pe", "dve", "act")

        t_pool = []
        for n2 in range(2):
            g_tok, a_tok, gp = {}, {}, {}

            def ga_evac(n, o, t, cs):
                g_tok[n] = act(lambda e: e.activation(GA[n][:, :], o, ACT.Sigmoid), t, t_att, ga_rel[n])
                return g_tok[n]

            def ba_evac(n, o, t, cs):
                a_tok[n] = dve(lambda e: e.tensor_tensor(GA[n][:, :], GA[n][:, :], o, ALU.mult), t, g_tok[n])
                return a_tok[n]

            def gp_evac(n, o, t, cs):
                i, tm, rel = take_tmp()
                ta = act(lambda e: e.activation(tm[:, :], o, ACT.Sigmoid), t, rel)
                gp[n] = (i, tm, ta)
                return ta

            def bp_evac(n, o, t, cs, n2=n2):
                j = 4 * n2 + n
                i, tm, ta = gp[n]
                t1 = dve(lambda e: e.tensor_tensor(tm[:, :], tm[:, :], o, ALU.mult), t, ta)
                t2 = dve(lambda e: e.tensor_tensor(tm[:, :], tm[:, :], GA[n][:, :], ALU.add), t1, a_tok[n])
                ga_rel[n] = t2
                m_tok[j] = two_parts(MH[j][:, :], ML[j][:, :], tm[:, :], t2, t_pool)
                tmps.rel[i] = m_tok[j]
                return t1

            linear("ga", 2, list(four), hx, ga_evac)
            if n2 == 0:
                pz_parts()
                t_pool.extend(pool_out())
            linear("ba", 1, list(four), lambda k, n, cs: (OHI[k][:, :], OLO[k][:, :], do_tok[k]), ba_evac)
            linear("gp", 2, list(four), hx, gp_evac)
            linear("bp", 1, list(four), lambda k, n, cs: (YH[:, k, :], YL[:, k, :], y_tok[k]), bp_evac)
        ssq_rel[:] = r_rel[:] = h_rel[:] = now("pe") * 2

        def m_x(k, n, cs):
            return MH[k][:, cs], ML[k][:, cs], m_tok[k]

        norm = plain_norm("ffn2_norm")
        for n2 in range(2):
            linear("out", 2, list(four), m_x, lambda n, o, t, cs: add_x(4 * n2 + n, o, 1.0, t, None, cs),
                   **(closing(norm) if n2 else {}))

        OUT = sb([128, 4, D], F32, AR + 32 * KB)

        ready = []

        def last_norm(step):
            hf = int(step[1])
            cs = HALF[hf]
            if step[0] == "a":
                ready.append(rstd(D, cs))
                return
            r = ready.pop()()
            for j in range(8):
                x_tok[j][hf] = dve(lambda e, j=j: e.scalar_tensor_tensor(X[:, j, cs], X[:, j, cs],
                                                                         col("final_norm", j), r["R"][:, cs],
                                                                         ALU.mult, ALU.mult), r["t"], x_tok[j][hf],
                                       ssq_t[hf])
            r["rel"][hf] = x_tok[7][hf]
            let_go(r)

        glu(norm, last_norm)

        last_norm("a1")
        for hf in range(2):
            if hf:
                last_norm("b1")
            for t4 in (2 * hf, 2 * hf + 1):
                t_o = []
                for jb in range(2):
                    b = banks.take()
                    for jj in range(4):
                        t = pe(lambda e, b=b, t4=t4, jj=jj, j=4 * jb + jj: e.transpose(
                            PS[:, b, jj * 128:jj * 128 + 128], X[:, j, t4 * 128:t4 * 128 + 128], ident),
                            x_tok[4 * jb + jj][hf], banks.rel[b], sig=(jj == 3))
                    dst = OUT[:, t4, 512 * jb:512 * jb + 512]
                    if jb:
                        t = dve(lambda e, b=b, dst=dst: e.tensor_copy(dst, PS[:, b, :]), t, hid_rel[1])
                    else:
                        t = act(lambda e, b=b, dst=dst: e.activation(dst, PS[:, b, :], ACT.Copy), t, hid_rel[1])
                    banks.rel[b] = t
                    t_o.append(t)
                t_out = dma("out", out[0, 128 * t4:128 * t4 + 128, :], OUT[:, t4, :], t_o)
        assert state["split"] == len(plan) and not late and not later

        sems = {s: ctx.enter_context(nc.semaphore(f"s_{s}")) for s in Q.n}
        block = ctx.enter_context(nc.Block())

        @block.sync
        def _(e):
            Q.play("sp", e, sems)
            e.wait_ge(sems[t_out[0]], t_out[1])

        @block.scalar
        def _(e):
            Q.play("act", e, sems)

        @block.vector
        def _(e):
            Q.play("dve", e, sems)

        @block.tensor
        def _(e):
            Q.play("pe", e, sems)

        @block.gpsimd
        def _(e):
            Q.play("pool", e, sems)


_INS = ['x', 'c', 'positions', 'w_ada', 'b_ada', 'g_mix', 'g_mlp', 'mla_w_dq', 'mla_g_q', 'mla_w_uq', 'mla_w_dkv',
        'mla_g_kv', 'mla_w_ukv', 'mla_w_o', 'swa_w_qkv', 'swa_b_qkv', 'swa_sinks', 'swa_w_o', 'swa_b_o', 'w_ff1',
        'w_ff2', 'g_final', 'ffn1_norm_2', 'ffn1_w1_2', 'ffn1_w3_2', 'ffn1_w2_2', 'mix_norm_2', 'w_in_2',
        'w_branch_attn_2', 'w_branch_pool_2', 'pool_w_2', 'pool_scale_2', 'w_out_2', 'ffn2_norm_2', 'ffn2_w1_2',
        'ffn2_w3_2', 'ffn2_w2_2', 'final_norm_2']


def shape_constants():
    import numpy as np

    f = np.float32
    NEG = f(-2.0e38)
    p = np.arange(128)
    q, k = p[:, None], p[None, :]
    ident = np.eye(128, dtype=f)
    rot = np.zeros((128, 128), f)
    drot = np.zeros((128, 128), f)
    for m in range(128):
        d = m % 64
        rot[m + 32 if d < 32 else m - 32, m] = -1.0 if d < 32 else 1.0
        if d < 8:
            drot[m + 8, m] = -1.0
        elif d < 16:
            drot[m - 8, m] = 1.0
    causal = np.where(k <= q, f(0), NEG).astype(f)
    invf = (f(10000.0) ** (-np.arange(32, dtype=f) / f(32))).astype(f)[p % 32][:, None]
    BIG = f(1.0e37)
    own = np.where(k <= q, q - k, BIG).astype(f)
    prev = np.where(q + 128 - k < 128, q + 128 - k, BIG).astype(f)
    pair = np.concatenate([prev, own], 1)
    first = np.concatenate([own, np.full((128, 128), BIG, f)], 1)
    dist = np.concatenate([first, pair], 1)

    def mask(ok):
        return np.where(ok, f(0), NEG).astype(f)

    m4, m16 = (q - k) % 4 == 0, (q - k) % 16 == 0
    low = k <= q
    dil = np.stack([mask(k >= q), mask(low)] + [mask(m4)] * 3 + [mask(m4 & low)] + [mask(m16)] * 3
                   + [mask(m16 & low)], 1)
    inv = (f(500000.0) ** (-np.arange(0, 16, 2, dtype=f) / f(16))).astype(f)
    ang = (np.arange(512, dtype=f)[None, :] * inv[:, None]).astype(f)
    dcos, dsin = np.ones((128, 512), f), np.zeros((128, 512), f)
    for m in range(128):
        if m % 64 < 16:
            dcos[m] = np.cos(ang[m % 8])
            dsin[m] = np.sin(ang[m % 8])
    cnt = np.stack([f(1) / np.minimum(np.arange(1, 513), w).astype(f) for w in (2, 4, 8, 16)])[None]
    return {"k_const": np.stack([ident, causal, rot], 1), "k_invf": invf,
            "k_dist": dist, "k_dil": dil, "k_dcos": dcos, "k_dsin": dsin, "k_drot": drot, "k_cnt": cnt.astype(f)}


def kernel(**inputs):
    import numpy as _np
    import concourse.bacc as _bacc
    from concourse import mybir as _mybir
    from concourse.bass_utils import run_bass_kernel_spmd as _run

    nc = _bacc.Bacc("TRN2", target_bir_lowering=False, num_devices=1)
    arrays, aps = {}, {}
    given = {name: _np.ascontiguousarray(inputs[name]) for name in _INS}
    for name, a in {**given, **shape_constants()}.items():
        a = _np.ascontiguousarray(a)
        arrays[f"in_{name}_dram"] = a
        aps[name] = nc.dram_tensor(f"in_{name}_dram", a.shape, _mybir.dt.from_np(a.dtype), kind="ExternalInput").ap()
    out = nc.dram_tensor("out_0_dram", (1, 512, 1024), _mybir.dt.from_np(_np.dtype("float32")),
                         kind="ExternalOutput").ap()
    bass_two_blocks(nc, aps, out)
    r = _run(nc, [arrays], core_ids=[0])
    return r.results[0]["out_0_dram"]
```
